# Optimizing a Trainium2 kernel written in Bass

```python
import jax, jax.numpy as jnp
from jax import lax
import numpy as np

D_MODEL = 2048
BATCH = 1
SEQ = 256
DEPTH = 1

MIX_WIDTH = D_MODEL
POOL_WIDTH = MIX_WIDTH // 2
POOL_WINDOWS = (2, 4, 8, 16)
POOL_GROUP = POOL_WIDTH // len(POOL_WINDOWS)
ATTN_WIDTH = MIX_WIDTH - POOL_WIDTH
HEAD_DIM = 128
N_HEADS = ATTN_WIDTH // HEAD_DIM
DILATED_PATTERNS = ((128, 1), (512, 4), (2048, 16))
MAX_WINDOW = max(w for w, _ in DILATED_PATTERNS)
Q_BLOCK = 128
IN_WIDTH = POOL_WIDTH + 3 * ATTN_WIDTH
D_FF = 4 * D_MODEL
NORM_EPS = 1e-6


def rmsnorm(x, g):
    xf = x.astype(jnp.float32)
    y = xf * lax.rsqrt(jnp.mean(xf * xf, axis=-1, keepdims=True) + NORM_EPS)
    return (y * g.astype(jnp.float32)).astype(x.dtype)

def alibi_slopes():
    return 2.0 ** (-8.0 * jnp.arange(1, N_HEADS + 1, dtype=jnp.float32) / N_HEADS)

def pool_mixer(u, pool_w, pool_scale):
    B, S, _ = u.shape
    uf = u.astype(jnp.float32)
    cs = jnp.cumsum(uf, axis=1)
    pos = jnp.arange(1, S + 1, dtype=jnp.float32)[None, :, None]
    diffs = []
    for g, w in enumerate(POOL_WINDOWS):
        c = cs[..., g * POOL_GROUP:(g + 1) * POOL_GROUP]
        trailing = c - jnp.pad(c, ((0, 0), (w, 0), (0, 0)))[:, :S]
        mean = trailing / jnp.minimum(pos, float(w))
        diffs.append(mean - uf[..., g * POOL_GROUP:(g + 1) * POOL_GROUP])
    d = jnp.stack(diffs, axis=2).astype(u.dtype)
    y = jnp.einsum('bsgc,gcf->bsgf', d, pool_w).reshape(B, S, POOL_WIDTH)
    return y * pool_scale

def dilated_attention(q, k, v, slopes):
    B, S, H, Dh = q.shape
    scale = Dh ** -0.5
    kp = jnp.pad(k, ((0, 0), (MAX_WINDOW, 0), (0, 0), (0, 0)))
    vp = jnp.pad(v, ((0, 0), (MAX_WINDOW, 0), (0, 0), (0, 0)))
    qi = jnp.arange(Q_BLOCK)

    def block(b0):
        qb = lax.dynamic_slice_in_dim(q, b0, Q_BLOCK, axis=1).astype(jnp.float32) * scale
        kwin = lax.dynamic_slice_in_dim(kp, b0, Q_BLOCK + MAX_WINDOW, axis=1)
        vwin = lax.dynamic_slice_in_dim(vp, b0, Q_BLOCK + MAX_WINDOW, axis=1)
        ms, dens, nums = [], [], []
        for window, dil in DILATED_PATTERNS:
            dist = jnp.arange(window // dil + 1) * dil
            idx = qi[:, None] + MAX_WINDOW - dist[None, :]
            valid = (b0 + qi)[:, None] >= dist[None, :]
            kg = jnp.take(kwin, idx, axis=1).astype(jnp.float32)
            vg = jnp.take(vwin, idx, axis=1).astype(jnp.float32)
            s = jnp.einsum('bqhd,bqjhd->bqhj', qb, kg)
            s = s - slopes[:, None] * dist.astype(jnp.float32)[None, :]
            s = jnp.where(valid[None, :, None, :], s, -jnp.inf)
            m = jnp.max(s, axis=-1)
            p = jnp.exp(s - m[..., None])
            ms.append(m)
            dens.append(jnp.sum(p, axis=-1))
            nums.append(jnp.einsum('bqhj,bqjhd->bqhd', p, vg))
        m_all = jnp.stack(ms)
        w = jnp.exp(m_all - jnp.max(m_all, axis=0))
        den = jnp.sum(w * jnp.stack(dens), axis=0)
        num = jnp.sum(w[..., None] * jnp.stack(nums), axis=0)
        return num / den[..., None]

    starts = jnp.arange(S // Q_BLOCK) * Q_BLOCK
    out = lax.map(block, starts)
    return out.transpose(1, 0, 2, 3, 4).reshape(B, S, H * Dh).astype(q.dtype)

def first_inputs(seed: int = 0) -> dict:
    key = jax.random.key(seed)
    ks = jax.random.split(key, 12)
    f32 = jnp.float32
    x = jax.random.normal(ks[0], (BATCH, SEQ, D_MODEL), f32)
    norm_mix_g = 1.0 + 0.05 * jax.random.normal(ks[1], (DEPTH, D_MODEL), f32)
    w_in = jax.random.normal(ks[2], (DEPTH, D_MODEL, IN_WIDTH), f32) * D_MODEL ** -0.5
    pool_w = jax.random.normal(ks[3], (DEPTH, len(POOL_WINDOWS), POOL_GROUP, POOL_GROUP), f32) * POOL_GROUP ** -0.5
    pool_scale = 1.0 + 0.1 * jax.random.normal(ks[4], (DEPTH, POOL_WIDTH), f32)
    pool_out_norm_g = 1.0 + 0.05 * jax.random.normal(ks[5], (DEPTH, POOL_WIDTH), f32)
    attn_out_norm_g = 1.0 + 0.05 * jax.random.normal(ks[6], (DEPTH, ATTN_WIDTH), f32)
    w_out = jax.random.normal(ks[7], (DEPTH, MIX_WIDTH, D_MODEL), f32) * MIX_WIDTH ** -0.5
    norm_mlp_g = 1.0 + 0.05 * jax.random.normal(ks[8], (DEPTH, D_MODEL), f32)
    w_up = jax.random.normal(ks[9], (DEPTH, D_MODEL, D_FF), f32) * D_MODEL ** -0.5
    w_down = jax.random.normal(ks[10], (DEPTH, D_FF, D_MODEL), f32) * D_FF ** -0.5
    norm_final_g = 1.0 + 0.05 * jax.random.normal(ks[11], (D_MODEL,), f32)
    return {"x": x, "norm_mix_g": norm_mix_g, "w_in": w_in, "pool_w": pool_w,
            "pool_scale": pool_scale, "pool_out_norm_g": pool_out_norm_g,
            "attn_out_norm_g": attn_out_norm_g, "w_out": w_out, "norm_mlp_g": norm_mlp_g,
            "w_up": w_up, "w_down": w_down, "norm_final_g": norm_final_g}

def first_block(x, norm_mix_g, w_in, pool_w, pool_scale, pool_out_norm_g, attn_out_norm_g,
              w_out, norm_mlp_g, w_up, w_down, norm_final_g):
    B, S, _ = x.shape
    slopes = alibi_slopes()
    for l in range(DEPTH):
        h = rmsnorm(x, norm_mix_g[l])
        proj = h @ w_in[l]
        u = proj[..., :POOL_WIDTH]
        qkv = proj[..., POOL_WIDTH:].reshape(B, S, 3, N_HEADS, HEAD_DIM)
        y_pool = rmsnorm(pool_mixer(u, pool_w[l], pool_scale[l]), pool_out_norm_g[l])
        y_attn = rmsnorm(dilated_attention(qkv[:, :, 0], qkv[:, :, 1], qkv[:, :, 2], slopes),
                         attn_out_norm_g[l])
        x = x + jnp.concatenate([y_pool, y_attn], axis=-1) @ w_out[l]
        h = rmsnorm(x, norm_mlp_g[l])
        x = x + jnp.square(jax.nn.relu(h @ w_up[l])) @ w_down[l]
    return rmsnorm(x, norm_final_g)


N_MEM = 256
D_MIX = D_MODEL
D_DELTA = D_MIX // 2
D_CONV = D_MIX - D_DELTA
DN_HEADS = 8
DN_HEAD_DIM = D_DELTA // DN_HEADS
DN_CONV_W = 4
DN_CHUNK = 64
CF_CONV_W = 31
XA_HEADS = 4
XA_HEAD_DIM = D_MODEL // XA_HEADS
D_FF_2 = 4 * D_MODEL
EPS = 1e-6
D_IN = 4 * D_DELTA + 2 * DN_HEADS + 2 * D_CONV


def rms_norm(x, g):
    xf = x.astype(jnp.float32)
    y = xf * lax.rsqrt(jnp.mean(xf * xf, axis=-1, keepdims=True) + EPS)
    return (y * g.astype(jnp.float32)).astype(x.dtype)

def layer_norm(x, g, b):
    xf = x.astype(jnp.float32)
    mu = jnp.mean(xf, axis=-1, keepdims=True)
    xc = xf - mu
    var = jnp.mean(xc * xc, axis=-1, keepdims=True)
    y = xc * lax.rsqrt(var + EPS) * g.astype(jnp.float32) + b.astype(jnp.float32)
    return y.astype(x.dtype)

def l2_normalize(x):
    xf = x.astype(jnp.float32)
    return xf * lax.rsqrt(jnp.sum(xf * xf, axis=-1, keepdims=True) + EPS)

def causal_depthwise_conv(x, w):
    width, ch = w.shape
    return lax.conv_general_dilated(
        x, w[:, None, :].astype(x.dtype), window_strides=(1,), padding=[(width - 1, 0)],
        dimension_numbers=("NWC", "WIO", "NWC"), feature_group_count=ch)

def chunk_gated_delta_rule(q, k, v, g, beta):
    B, T, H, Dk = q.shape
    Dv = v.shape[-1]
    C = DN_CHUNK
    N = T // C

    def to_chunks(t):
        t = t.reshape((B, N, C, H) + t.shape[3:])
        return jnp.moveaxis(t, 3, 1)

    q, k, v, g, beta = (to_chunks(t) for t in (q, k, v, g, beta))
    q = q * (Dk ** -0.5)
    g = jnp.cumsum(g, axis=-1)
    causal = jnp.tril(jnp.ones((C, C), dtype=bool))
    strict = jnp.tril(jnp.ones((C, C), dtype=bool), -1)
    decay = jnp.exp(jnp.where(causal, g[..., :, None] - g[..., None, :], -jnp.inf))

    k_beta = k * beta[..., None]
    v_beta = v * beta[..., None]
    a = jnp.einsum("bhncd,bhnsd->bhncs", k_beta, k) * decay
    t_mat = jnp.eye(C, dtype=jnp.float32) + jnp.where(strict, a, 0.0)
    rhs = jnp.concatenate([v_beta, k_beta * jnp.exp(g)[..., None]], axis=-1)
    sol = lax.linalg.triangular_solve(t_mat, rhs, left_side=True, lower=True, unit_diagonal=True)
    u, w = sol[..., :Dv], sol[..., Dv:]

    attn = jnp.einsum("bhncd,bhnsd->bhncs", q, k) * decay
    q_dec = q * jnp.exp(g)[..., None]
    g_last = g[..., -1]
    k_dec = k * jnp.exp(g_last[..., None] - g)[..., None]

    def step(S, xs):
        q_c, k_c, u_c, w_c, attn_c, gl = xs
        v_new = u_c - jnp.einsum("bhcd,bhde->bhce", w_c, S)
        o = jnp.einsum("bhcd,bhde->bhce", q_c, S) + jnp.einsum("bhcs,bhse->bhce", attn_c, v_new)
        S = S * jnp.exp(gl)[..., None, None] + jnp.einsum("bhcd,bhce->bhde", k_c, v_new)
        return S, o

    xs = tuple(jnp.moveaxis(t, 2, 0) for t in (q_dec, k_dec, u, w, attn, g_last))
    S0 = jnp.zeros((B, H, Dk, Dv), dtype=jnp.float32)
    _, o = lax.scan(step, S0, xs)
    return jnp.transpose(o, (1, 0, 3, 2, 4)).reshape(B, T, H, Dv)

def hybrid_mixer(xn, w_in, dn_conv_w, dn_a_log, dn_dt_bias, dn_norm_g,
                 cf_dw_w, cf_dw_b, cf_ln_g, cf_ln_b, w_out):
    B, T, _ = xn.shape
    proj = xn @ w_in
    qkv, z, b_raw, a_raw, glu = jnp.split(
        proj, [3 * D_DELTA, 4 * D_DELTA, 4 * D_DELTA + DN_HEADS, 4 * D_DELTA + 2 * DN_HEADS], axis=-1)

    qkv = jax.nn.silu(causal_depthwise_conv(qkv, dn_conv_w))
    q, k, v = jnp.split(qkv, 3, axis=-1)
    hd = (B, T, DN_HEADS, DN_HEAD_DIM)
    q = l2_normalize(q.reshape(hd))
    k = l2_normalize(k.reshape(hd))
    v = v.reshape(hd).astype(jnp.float32)
    beta = jax.nn.sigmoid(b_raw.astype(jnp.float32))
    g = -jnp.exp(dn_a_log.astype(jnp.float32)) * jax.nn.softplus(
        a_raw.astype(jnp.float32) + dn_dt_bias.astype(jnp.float32))
    o = chunk_gated_delta_rule(q, k, v, g, beta)
    o = rms_norm(o, dn_norm_g) * jax.nn.silu(z.reshape(hd).astype(jnp.float32))
    o = o.reshape(B, T, D_DELTA).astype(xn.dtype)

    c = glu[..., :D_CONV] * jax.nn.sigmoid(glu[..., D_CONV:])
    c = causal_depthwise_conv(c, cf_dw_w) + cf_dw_b
    c = jax.nn.silu(layer_norm(c, cf_ln_g, cf_ln_b))

    return jnp.concatenate([o, c], axis=-1) @ w_out

def memory_cross_attention(hn, mem_n, w_q, w_k, w_v, w_o):
    B, T, _ = hn.shape
    M = mem_n.shape[1]
    q = (hn @ w_q).reshape(B, T, XA_HEADS, XA_HEAD_DIM)
    k = (mem_n @ w_k).reshape(B, M, XA_HEADS, XA_HEAD_DIM)
    v = (mem_n @ w_v).reshape(B, M, XA_HEADS, XA_HEAD_DIM)
    s = jnp.einsum("bthd,bmhd->bhtm", q, k).astype(jnp.float32) * (XA_HEAD_DIM ** -0.5)
    p = jax.nn.softmax(s, axis=-1).astype(v.dtype)
    o = jnp.einsum("bhtm,bmhd->bthd", p, v).reshape(B, T, D_MODEL)
    return o @ w_o

def squared_relu_mlp(hn, w1, w2):
    return jnp.square(jax.nn.relu(hn @ w1)) @ w2

def second_inputs(seed: int = 0) -> dict:
    key = jax.random.key(seed)
    ks = jax.random.split(key, 24)
    f32 = jnp.float32
    L = DEPTH

    def dense(k, fan_in, fan_out):
        return jax.random.normal(k, (L, fan_in, fan_out), f32) * fan_in ** -0.5

    def gain(k, n):
        return 1.0 + 0.02 * jax.random.normal(k, (L, n), f32)

    dt = jnp.exp(jax.random.uniform(ks[6], (L, DN_HEADS), f32, np.log(1e-3), np.log(1e-1)))
    return {
        "x": jax.random.normal(ks[0], (BATCH, SEQ, D_MODEL), f32),
        "mem": jax.random.normal(ks[1], (BATCH, N_MEM, D_MODEL), f32),
        "norm_mix_g": gain(ks[2], D_MODEL),
        "w_in": dense(ks[3], D_MODEL, D_IN),
        "dn_conv_w": jax.random.normal(ks[4], (L, DN_CONV_W, 3 * D_DELTA), f32) * DN_CONV_W ** -0.5,
        "dn_a_log": jnp.log(jax.random.uniform(ks[5], (L, DN_HEADS), f32, 1.0, 16.0)),
        "dn_dt_bias": dt + jnp.log(-jnp.expm1(-dt)),
        "dn_norm_g": gain(ks[7], DN_HEAD_DIM),
        "cf_dw_w": jax.random.normal(ks[8], (L, CF_CONV_W, D_CONV), f32) * CF_CONV_W ** -0.5,
        "cf_dw_b": 0.02 * jax.random.normal(ks[9], (L, D_CONV), f32),
        "cf_ln_g": gain(ks[10], D_CONV),
        "cf_ln_b": 0.02 * jax.random.normal(ks[11], (L, D_CONV), f32),
        "w_out": dense(ks[12], D_MIX, D_MODEL),
        "norm_xa_g": gain(ks[13], D_MODEL),
        "norm_mem_g": gain(ks[14], D_MODEL),
        "xa_wq": dense(ks[15], D_MODEL, D_MODEL),
        "xa_wk": dense(ks[16], D_MODEL, D_MODEL),
        "xa_wv": dense(ks[17], D_MODEL, D_MODEL),
        "xa_wo": dense(ks[18], D_MODEL, D_MODEL),
        "norm_mlp_g": gain(ks[19], D_MODEL),
        "mlp_w1": dense(ks[20], D_MODEL, D_FF_2),
        "mlp_w2": dense(ks[21], D_FF_2, D_MODEL),
        "norm_final_g": 1.0 + 0.02 * jax.random.normal(ks[22], (D_MODEL,), f32),
    }

def second_block(x, mem, norm_mix_g, w_in, dn_conv_w, dn_a_log, dn_dt_bias, dn_norm_g,
              cf_dw_w, cf_dw_b, cf_ln_g, cf_ln_b, w_out, norm_xa_g, norm_mem_g,
              xa_wq, xa_wk, xa_wv, xa_wo, norm_mlp_g, mlp_w1, mlp_w2, norm_final_g):
    h = x
    for i in range(DEPTH):
        h = h + hybrid_mixer(rms_norm(h, norm_mix_g[i]), w_in[i], dn_conv_w[i], dn_a_log[i],
                             dn_dt_bias[i], dn_norm_g[i], cf_dw_w[i], cf_dw_b[i],
                             cf_ln_g[i], cf_ln_b[i], w_out[i])
        h = h + memory_cross_attention(rms_norm(h, norm_xa_g[i]), rms_norm(mem, norm_mem_g[i]),
                                       xa_wq[i], xa_wk[i], xa_wv[i], xa_wo[i])
        h = h + squared_relu_mlp(rms_norm(h, norm_mlp_g[i]), mlp_w1[i], mlp_w2[i])
    return rms_norm(h, norm_final_g)


def setup_inputs(seed=0):
    out = dict(first_inputs(seed))
    for name, value in second_inputs(seed + 1).items():
        if name != "x":
            out[name + "_2"] = value
    return out


def reference(
    x, norm_mix_g, w_in, pool_w, pool_scale, pool_out_norm_g, attn_out_norm_g, w_out,
    norm_mlp_g, w_up, w_down, norm_final_g, mem_2, norm_mix_g_2, w_in_2, dn_conv_w_2,
    dn_a_log_2, dn_dt_bias_2, dn_norm_g_2, cf_dw_w_2, cf_dw_b_2, cf_ln_g_2, cf_ln_b_2, w_out_2,
    norm_xa_g_2, norm_mem_g_2, xa_wq_2, xa_wk_2, xa_wv_2, xa_wo_2, norm_mlp_g_2, mlp_w1_2,
    mlp_w2_2, norm_final_g_2,
):
    x = first_block(
        x, norm_mix_g, w_in, pool_w, pool_scale, pool_out_norm_g, attn_out_norm_g, w_out,
        norm_mlp_g, w_up, w_down, norm_final_g,
    )
    return second_block(
        x, mem_2, norm_mix_g_2, w_in_2, dn_conv_w_2, dn_a_log_2, dn_dt_bias_2, dn_norm_g_2,
        cf_dw_w_2, cf_dw_b_2, cf_ln_g_2, cf_ln_b_2, w_out_2, norm_xa_g_2, norm_mem_g_2, xa_wq_2,
        xa_wk_2, xa_wv_2, xa_wo_2, norm_mlp_g_2, mlp_w1_2, mlp_w2_2, norm_final_g_2,
    )


_drawn_inputs = setup_inputs


def setup_inputs(seed=0):
    import zlib

    import numpy as np

    out = dict(_drawn_inputs(seed))
    spreads = {}
    factors = {'norm_mix_g_2': 3.596,
     'dn_norm_g_2': 8.0,
     'cf_dw_b_2': 3.221,
     'cf_ln_g_2': 20.3,
     'cf_ln_b_2': 23.556,
     'norm_xa_g_2': 8.0,
     'norm_mem_g_2': 8.0,
     'norm_mlp_g_2': 12.62,
     'norm_final_g_2': 22.649}
    for name, (base, spread) in spreads.items():
        noise = np.random.default_rng([zlib.crc32(name.encode()), seed]).standard_normal(out[name].shape)
        drawn = base * np.exp(spread * noise) if base else spread * noise
        out[name] = __import__('jax').numpy.asarray(drawn.astype(out[name].dtype))
    for name, factor in factors.items():
        out[name] = (out[name] * factor).astype(out[name].dtype)
    return out
```

```python
from contextlib import ExitStack

import numpy as np

import concourse.bass as bass
from concourse import mybir

F32 = mybir.dt.float32
F32R = mybir.dt.float32r
ACT = mybir.ActivationFunctionType
ALU = mybir.AluOpType
AX_X = mybir.AxisListType.X

P = 128
T = 256
TT = T // P
D = 2048
KT = D // P
FF = 4 * D
HALF = FF // 2
HK = HALF // P
EPS = 1e-6

COLS = 1024
BANK = 512
STEP = 2
NRAW = 4
NSPLIT = 2

HEADS = 8
HD = 128
CHUNK = 64
WINDOWS = (2, 4, 8, 16)
GROUP = 256
PATTERNS = ((128, 1), (512, 4), (2048, 16))
CONV = 4
DW = 31
XHEADS = 4
XHD = D // XHEADS
XDT = XHD // P
QK_TILES = 3 * HEADS
LOG_TERMS = 8
NEG = -1e30


def shape_constants():
    i = np.arange(P)
    same = (i[:, None] // CHUNK) == (i[None, :] // CHUNK)
    ident = np.eye(P)
    tri = same & (i[:, None] <= i[None, :])
    negmask = np.where(tri, 0.0, NEG)
    mats = [ident, tri, same, negmask, np.ones((P, P))]
    b = 1
    while b < CHUNK:
        lower = (i[:, None] // (2 * b) == i[None, :] // (2 * b)) & (i[:, None] // b < i[None, :] // b)
        mats.append(lower)
        b *= 2
    squares = np.stack([np.asarray(m, np.float32) for m in mats], 1)

    t = np.arange(T)
    dist = t[:, None] - t[None, :]
    times = sum(((dist >= 0) & (dist <= w) & (dist % r == 0)).astype(np.float64) for w, r in PATTERNS)
    logs = np.where(times > 0, np.log(np.maximum(times, 1.0)), NEG)
    far = np.maximum(dist, 0)
    cut = lambda m: np.concatenate([m[:P, :P], m[P:, :]], 1)
    alibi = np.stack([cut(far), cut(logs)], 1).astype(np.float32)

    pool = np.zeros((len(WINDOWS), T, T))
    for g, w in enumerate(WINDOWS):
        pool[g] = np.where((dist >= 0) & (dist < w), 1.0 / np.minimum(t + 1, w)[:, None], 0.0) - np.eye(T)
    pool_t = pool.transpose(2, 0, 1).reshape(TT, P, len(WINDOWS), T).transpose(1, 2, 0, 3)
    return squares, alibi, np.ascontiguousarray(pool_t, np.float32)


class Own:

    def __init__(self, eng, sem):
        self.eng, self.sem, self.n = eng, sem, 0

    def mark(self, ins):
        self.n += 1
        ins.then_inc(self.sem, 1)

    def wait(self):
        self.eng.wait_ge(self.sem, self.n)


def build(nc, x, mem, vectors, squares, alibi, pool_avg, w_in, pool_w, pool_scale, w_out, w_up, w_down,
          final_g, w_in2, a_log, dt_bias, w_out2, wq, wk, wv, wo, w1, w2, final_g2, out):
    ctx = ExitStack()
    with ctx:
        def sem(name):
            return ctx.enter_context(nc.semaphore(name))

        KB = 1024
        base = (nc.sbuf_base + 63) // 64 * 64
        ctx.enter_context(nc.sbuf_tensor("slab", [P, (207 * KB + 512) // 4], F32))

        def at(name, shape, where, dtype=F32):
            return nc.alloc_sbuf_tensor_at(name, shape, dtype, offset=base + int(where * KB))

        X = at("residual", [P, TT, D], 0)
        HHI = at("stationary_hi", [P, KT, T], 16, F32R)
        HLO = at("stationary_lo", [P, KT, T], 32, F32R)
        RAW = at("weights_raw", [P, NRAW, STEP, COLS], 48)
        WHI = at("weights_hi", [P, NSPLIT, STEP, COLS], 80, F32R)
        WLO = at("weights_lo", [P, NSPLIT, STEP, COLS], 96, F32R)
        SQ = at("squares", [P, 11, P], 112)
        VEC = at("vectors", [P, 4, P], 117.5)
        VEC_RAW = at("vectors_raw", [P, 4, P], 121.5 + 84)
        free_small = [119.5]

        def small(name, shape, dtype=F32):
            t = at(name, shape, free_small[0], dtype)
            free_small[0] += (int(np.prod(shape[1:])) * 4 + 31) // 32 * 32 / KB
            assert free_small[0] <= 121.5
            return t

        A0 = 121.5
        IDENT, TRI, SAME, NEGMASK, ONES = (SQ[:, n, :] for n in range(5))
        LEVELS = 6

        ss = small("ss", [P, 4])
        ms = small("ms", [P, 4])
        rstd = small("rstd", [P, 4])
        halves = small("halves", [P, 32])

        xn = at("normed", [P, TT, D], A0 + 64)
        AHI = at("hidden_hi", [P, HK, T], A0 + 0, F32R)
        ALO = at("hidden_lo", [P, HK, T], A0 + 32, F32R)
        R = at("hidden", [P, TT, COLS], A0 + 64)
        GB = at("final_gain", [P, D], A0 + 72)
        ROWS = at("final_rows", [P, TT, D], A0 + 0)

        PROJ = at("proj", [P, TT, 4 * COLS], A0 + 0)
        QT = at("q_t", [P, HEADS, T], A0 + 32)
        KTT = at("k_t", [P, HEADS, T], A0 + 40)
        POOLW = at("pool_w", [P, len(WINDOWS), 2, GROUP], A0 + 48)
        POOLA = at("pool_avg", [P, len(WINDOWS), TT, T], A0 + 56)
        DT = at("pooled_t", [P, HEADS, T], A0 + 64)
        NS = P + T
        S1 = at("scores", [P, 2, NS], A0 + 72)
        PT1 = at("probs_t", [P, 2, NS], A0 + 76)
        ALIBI = at("alibi", [P, 2, NS], A0 + 80)
        BIAS = at("bias", [P, NS], A0 + 83)
        PSB = at("pool_scale", [P, COLS], 16)
        nmax = small("nmax", [P, 2, 2])
        den = small("den", [P, 2, 2])
        rden = small("rden", [P, 2, 2])

        PROJ2 = at("proj2", [P, 6, TT, COLS], A0 + 0)
        QTOK, KTOK, VTOK, ZTOK, GA, GBT = (PROJ2[:, n] for n in range(6))
        CIN = at("conv_in", [P, HEADS, CONV - 1 + T], A0 + 48)
        COUT = at("conv_out", [P, HEADS, T], A0 + 57)
        CIN31 = at("conv31_in", [P, HEADS, DW - 1 + T], A0 + 65)
        COUT31 = at("conv31_out", [P, HEADS, T], A0 + 74)
        NBA = 16
        BARAW = at("w_ba", [P, KT, NBA], A0 + 82)
        BAHI = at("w_ba_hi", [P, KT, NBA], A0 + 83, F32R)
        BALO = at("w_ba_lo", [P, KT, NBA], A0 + 84, F32R)
        KB_ = at("k_beta", [P, TT, HEADS, HD], A0 + 40)
        KBG = at("k_beta_decayed", [P, TT, HEADS, HD], A0 + 48)
        KDEC = at("k_to_end", [P, TT, HEADS, HD], A0 + 56)
        SQQ = at("q_squared", [P, TT, HEADS, HD], A0 + 48)
        SQK = at("k_squared", [P, TT, HEADS, HD], A0 + 56)
        QT2 = at("q2_t", [P, HEADS, T], A0 + 64)
        KT2 = at("k2_t", [P, HEADS, T], A0 + 72)
        U16 = TT * HEADS
        DEC = at("decay", [P, U16, P], 16)
        ATT = at("attn_t", [P, U16, P], 24)
        KBT = at("k_beta_t", [P, HEADS, T], 32)
        DIAG = at("gate_diag", [P, U16, P], 40)
        LT = at("lower_t", [P, U16, P], 40)
        XI = at("inverse", [P, U16, P], A0 + 40)
        XT = at("inverse_t", [P, U16, P], A0 + 72)
        WL = at("level_product", [P, U16, P], A0 + 0)
        LB = at("level_t", [P, U16, P], A0 + 8)
        U = at("u", [P, TT, HEADS, HD], 40)
        WT = at("w_t", [P, HEADS, T], 16)
        ST = at("state", [P, HEADS, HD], 32)
        SD = at("state_decayed", [P, HEADS, HD], 36)
        VN = at("v_new", [P, HEADS, HD], A0 + 80)
        O = at("delta_out", [P, TT, HEADS, HD], A0 + 40)
        OSQ = at("delta_out_squared", [P, TT, HEADS, HD], A0 + 48)
        CS = at("conv_silu", [P, HEADS, T], A0 + 0)
        ba = small("beta_alpha", [P, TT, NBA])
        beta = small("beta", [P, TT, HEADS])
        adt = small("a_plus_dt", [P, TT, HEADS])
        sp_e = small("softplus_e", [P, TT, HEADS])
        sp_z = small("softplus_z", [P, TT, HEADS])
        sp_q = small("softplus_q", [P, TT, HEADS])
        sp_p = small("softplus_p", [P, TT, HEADS])
        gate = small("gate", [P, TT, HEADS])
        gcs = small("gate_cumsum", [P, TT, HEADS])
        eg = small("exp_gate", [P, TT, HEADS])
        kd = small("exp_to_end", [P, TT, HEADS])
        egl = small("exp_chunk", [P, T // CHUNK, HEADS])
        alog = small("a_log", [P, HEADS])
        dtb = small("dt_bias", [P, HEADS])
        l2 = small("l2", [P, 2, U16])
        l2r = small("l2r", [P, 2, U16])
        osum = small("osum", [P, U16])
        orst = small("orst", [P, U16])
        cmean = small("cmean", [P, TT])

        KV = at("kv", [P, TT, 2 * D], A0 + 0)
        KXT = at("kx_t", [P, KT, T], A0 + 32)
        QX = at("qx", [P, TT, D], A0 + 48)
        QXT = at("qx_t", [P, KT, T], A0 + 64)
        PX = at("probs", [P, 2, TT, T], A0 + 80)
        PXT = at("xprobs_t", [P, 2, TT, T], A0 + 0)
        MEM = at("memory", [P, TT, D], A0 + 64)

        ps = ctx.enter_context(nc.psum_tensor("ps", [P, 8, BANK], F32))

        x_landed = sem("x_landed")
        vec_landed = sem("vec_landed")
        sq_landed = sem("sq_landed")
        alibi_landed = sem("alibi_landed")
        poolw_landed = sem("poolw_landed")
        poola_landed = sem("poola_landed")
        pools_landed = sem("pools_landed")
        ba_landed = sem("ba_landed")
        gates_landed = sem("gates_landed")
        final_landed = sem("final_landed")
        mem_landed = sem("mem_landed")
        raw_landed = [sem(f"raw_landed{n}") for n in range(NRAW)]
        out_landed = sem("out_landed")
        hi_ready = sem("hi_ready")
        lo_ready = sem("lo_ready")
        w_used = sem("w_used")
        out0 = sem("out0")
        out1 = sem("out1")
        vec_turned = sem("vec_turned")
        vec_ready = sem("vec_ready")
        halves_ready = sem("halves_ready")
        sq_done = sem("sq_done")
        rstd_ready = sem("rstd_ready")
        xn_ready = sem("xn_ready")
        turned = sem("turned")
        ht_hi = sem("ht_hi")
        ht_lo = sem("ht_lo")
        relu_done = sem("relu_done")
        r_turned = sem("r_turned")
        at_hi = sem("at_hi")
        at_lo = sem("at_lo")
        x_final = sem("x_final")
        act_own = sem("act_own")
        dve_own = sem("dve_own")
        pool_own = sem("pool_own")
        qk_turned = sem("qk_turned")
        qt_ready = sem("qt_ready")
        kt_ready = sem("kt_ready")
        pooled = sem("pooled")
        pooled_ready = sem("pooled_ready")
        pool_out = sem("pool_out")
        y_pool = sem("y_pool")
        scored = sem("scored")
        max_ready = sem("max_ready")
        probs_ready = sem("probs_ready")
        probs_turned = sem("probs_turned")
        pt_ready = sem("pt_ready")
        attended = sem("attended")
        y_attn = sem("y_attn")
        y_ready = sem("y_ready")
        ba_split = sem("ba_split")
        ba_done = sem("ba_done")
        ba_out = sem("ba_out")
        pads_ready = sem("pads_ready")
        glu_sig = sem("glu_sig")
        glu_ready = sem("glu_ready")
        conv_turned = sem("conv_turned")
        cin_ready = sem("cin_ready")
        conv_done = sem("conv_done")
        silu_ready = sem("silu_ready")
        conv_back = sem("conv_back")
        sec0 = sem("sec0")
        sec1 = sem("sec1")
        beta_ready = sem("beta_ready")
        adt_ready = sem("adt_ready")
        ea_ready = sem("ea_ready")
        spe_ready = sem("spe_ready")
        gate_ready = sem("gate_ready")
        gate_summed = sem("gate_summed")
        gcs_ready = sem("gcs_ready")
        kd_sub = sem("kd_sub")
        exps_ready = sem("exps_ready")
        l2_sq = sem("l2_sq")
        l2_sum = sem("l2_sum")
        l2_ready = sem("l2_ready")
        qn_ready = sem("qn_ready")
        kn_ready = sem("kn_ready")
        kb_ready = sem("kb_ready")
        tok_ready = sem("tok_ready")
        diag_ready = sem("diag_ready")
        qk2_turned = sem("qk2_turned")
        qk2_ready = sem("qk2_ready")
        rows_ready = sem("rows_ready")
        decsub_ready = sem("decsub_ready")
        decay_ready = sem("decay_ready")
        gram_done = sem("gram_done")
        gram_ready = sem("gram_ready")
        level_ready = sem("level_ready")
        level_first = sem("level_first")
        wl_done = sem("wl_done")
        wl_ready = sem("wl_ready")
        xw_done = sem("xw_done")
        x_up = sem("x_up")
        xt_done = sem("xt_done")
        xt_up = sem("xt_up")
        uw_done = sem("uw_done")
        u_ready = sem("u_ready")
        wt_ready = sem("wt_ready")
        state_ready = sem("state_ready")
        sd_ready = sem("sd_ready")
        ws_done = sem("ws_done")
        vn_ready = sem("vn_ready")
        qs_ready = sem("qs_ready")
        vn_used = sem("vn_used")
        o_ready = sem("o_ready")
        osq_ready = sem("osq_ready")
        osum_ready = sem("osum_ready")
        orst_ready = sem("orst_ready")
        z_ready = sem("z_ready")
        o_final = sem("o_final")
        csum = sem("csum")
        csq = sem("csq")
        crst = sem("crst")
        c_final = sem("c_final")
        cs_ready = sem("cs_ready")
        kx_turned = sem("kx_turned")
        kx_ready = sem("kx_ready")
        xscored = sem("xscored")
        xmax = sem("xmax")
        xprobs = sem("xprobs")
        xturned = sem("xturned")
        xpt = sem("xpt")
        xatt = sem("xatt")
        xout = sem("xout")

        PS = D // (STEP * P)
        S_IN, P_IN = 0, 0
        S_OUT, P_OUT = S_IN + 4 * PS, P_IN + 4
        S_MLP, P_MLP = S_OUT + 2 * PS, P_OUT + 2
        HALF_STEPS = 4 * PS + 2 * (HK // STEP)
        HALF_PASSES = 6
        S_IN2, P_IN2 = S_MLP + 2 * HALF_STEPS, P_MLP + 2 * HALF_PASSES
        S_OUT2, P_OUT2 = S_IN2 + 6 * PS, P_IN2 + 6
        S_KV, P_KV = S_OUT2 + 2 * PS, P_OUT2 + 2
        S_Q, P_Q = S_KV + 4 * PS, P_KV + 4
        S_O, P_O = S_Q + 2 * PS, P_Q + 2
        S_MLP2, P_MLP2 = S_O + 2 * PS, P_O + 2
        S_END = S_MLP2 + 2 * HALF_STEPS
        GLU0 = 4 * COLS + NBA
        IN2_COLS = [0, COLS, 2 * COLS, 3 * COLS, GLU0, GLU0 + COLS]
        (H_IN, H_OUT, H_MLP, H_IN2, H_OUT2, H_MEM, H_XQ, H_XO, H_MLP2) = range(9)
        (N_IN, N_MIX, N_MLP, N_F1, N_IN2, N_LN, N_MEM, N_XQ, N_MLP2, N_F2) = range(10)
        G_IN, G_OUT, G_MLP, G_IN2, G_XQ, G_MEM, G_MLP2, G_DN = 0, 16, 32, 48, 64, 80, 96, 112

        def gain(k):
            return VEC[:, 0, k:k + 1]

        def tap(j, c):
            return VEC[:, 1, j * QK_TILES + c:j * QK_TILES + c + 1]

        def dw_vec(n, c):
            k = CONV * QK_TILES + n * HEADS + c
            return VEC[:, 1, k:k + 1]

        def dw_tap(j, c):
            k = j * HEADS + c
            return VEC[:, 2 + k // 124, k % 124:k % 124 + 1]

        def blocks(w):
            return w.rearrange("(s j p) n -> s p j n", j=STEP, p=P)

        block = ctx.enter_context(nc.Block())

        @block.sync
        def _(sp):
            sp.dma_start(X[:], x.rearrange("(t p) d -> p t d", p=P)).then_inc(x_landed, 16)
            sp.dma_start(VEC_RAW[:], vectors.rearrange("n r c -> r n c")).then_inc(vec_landed, 16)
            sp.dma_start(SQ[:], squares).then_inc(sq_landed, 16)

            def load(s, src, off=0):
                if s >= NRAW:
                    sp.wait_ge(hi_ready, s + off - NRAW + 1)
                    sp.wait_ge(lo_ready, s + off - NRAW + 1)
                sp.dma_start(RAW[:, s % NRAW], src).then_inc(raw_landed[s % NRAW], 16)

            def load_pass(s0, w, c0):
                for k in range(PS):
                    load(s0 + k, blocks(w)[k, :, :, c0:c0 + COLS])

            def load_mlp(s0, up, down):
                with sp.Fori(0, 2) as half:
                    off = half * HALF_STEPS
                    for p in range(4):
                        for k in range(PS):
                            load(s0 + p * PS + k, blocks(up)[k, :, :, bass.ds(half * HALF + p * COLS, COLS)], off)
                    rows = down.rearrange("(h s j p) n -> h s p j n", h=2, j=STEP, p=P)
                    for d in range(2):
                        for k in range(HK // STEP):
                            load(s0 + 4 * PS + d * (HK // STEP) + k,
                                 rows[bass.ds(half, 1), k, :, :, d * COLS:(d + 1) * COLS].rearrange("h p j n -> (h p) j n"), off)

            for n in range(4):
                load_pass(S_IN + n * PS, w_in, n * COLS)
            for n in range(2):
                load_pass(S_OUT + n * PS, w_out, n * COLS)
            load_mlp(S_MLP, w_up, w_down)
            for n in range(6):
                load_pass(S_IN2 + n * PS, w_in2, IN2_COLS[n])
            for n in range(2):
                load_pass(S_OUT2 + n * PS, w_out2, n * COLS)
            for n in range(4):
                load_pass(S_KV + n * PS, wk if n < 2 else wv, (n % 2) * COLS)
            for n in range(2):
                load_pass(S_Q + n * PS, wq, n * COLS)
            for n in range(2):
                load_pass(S_O + n * PS, wo, n * COLS)
            load_mlp(S_MLP2, w1, w2)
            for t in range(TT):
                sp.wait_ge(x_final, t + 1 + TT)
                sp.dma_start(out[t * P:(t + 1) * P, :], ROWS[:, t, :]).then_inc(out_landed, 16)
            sp.wait_ge(out_landed, 16 * TT)

        @block.gpsimd
        def _(pool):
            own = Own(pool, pool_own)
            pool.memset(halves[:], -0.5).then_inc(halves_ready, 1)
            pool.dma_start(ALIBI[:], alibi).then_inc(alibi_landed, 16)
            pool.dma_start(POOLW[:], pool_w.rearrange("g (c p) f -> p g c f", p=P)).then_inc(poolw_landed, 16)
            pool.dma_start(POOLA[:], pool_avg).then_inc(poola_landed, 16)
            pool.dma_start(alog[:], a_log.partition_broadcast(P)).then_inc(gates_landed, 16)
            pool.dma_start(dtb[:], dt_bias.partition_broadcast(P)).then_inc(gates_landed, 16)

            def root(n_sq, n_norm, cols, width):
                pool.wait_ge(sq_done, n_sq)
                own.mark(pool.tensor_scalar(ms[:, 0:cols], ss[:, 0:cols], 1.0 / width, EPS, ALU.mult, ALU.add))
                own.wait()
                pool.wait_ge(halves_ready, 1)
                pool.tensor_tensor(rstd[:, 0:cols], ms[:, 0:cols], halves[:, 0:cols], ALU.pow).then_inc(rstd_ready, 1)

            root(2, N_IN, 2, D)
            pool.wait_ge(w_used, S_OUT)
            pool.dma_start(PSB[:], pool_scale.partition_broadcast(P)).then_inc(pools_landed, 16)
            root(6, N_MIX, 4, COLS)
            root(8, N_MLP, 2, D)
            pool.wait_ge(turned, KT // 2 * (H_MLP + 1))
            pool.dma_start(GB[:], final_g.partition_broadcast(P)).then_inc(final_landed, 16)
            root(10, N_F1, 2, D)
            root(12, N_IN2, 2, D)
            pool.wait_ge(turned, KT // 2 * (H_IN2 + 1))
            pool.dma_start(BARAW[:], w_in2[:, 4 * COLS:4 * COLS + NBA].rearrange("(k p) n -> p k n", p=P)).then_inc(ba_landed, 16)
            pool.memset(CIN[:, :, 0:CONV - 1], 0.0).then_inc(pads_ready, 1)
            pool.memset(CIN31[:, :, 0:DW - 1], 0.0).then_inc(pads_ready, 1)
            root(14, N_LN, 2, COLS)
            pool.wait_ge(l2_sum, 2)
            own.mark(pool.tensor_scalar(l2[:], l2[:], EPS, None, ALU.add))
            own.wait()
            for n in range(2):
                own.mark(pool.tensor_tensor(l2r[:, n, :], l2[:, n, :], halves[:, 0:U16], ALU.pow))
            own.wait()
            pool.tensor_scalar(l2r[:, 0, :], l2r[:, 0, :], float(HD) ** -0.5, None, ALU.mult).then_inc(l2_ready, 1)
            pool.wait_ge(gram_ready, 2)
            pool.memset(ST[:], 0.0).then_inc(state_ready, 1)
            for n in range(T // CHUNK):
                pool.wait_ge(state_ready, n + 1)
                if n >= 1:
                    pool.wait_ge(exps_ready, 1)
                else:
                    pool.wait_ge(exps_ready, 1)
                pool.tensor_tensor(SD[:], ST[:], egl[:, n, :].unsqueeze(2).broadcast_to([P, HEADS, HD]), ALU.mult).then_inc(sd_ready, 1)
            pool.wait_ge(osum_ready, 1)
            own.mark(pool.tensor_scalar(osum[:], osum[:], 1.0 / HD, EPS, ALU.mult, ALU.add))
            own.wait()
            pool.tensor_tensor(orst[:], osum[:], halves[:, 0:U16], ALU.pow).then_inc(orst_ready, 1)
            pool.wait_ge(vn_used, T // CHUNK)
            pool.wait_ge(o_ready, T // CHUNK)
            pool.dma_start(MEM[:], mem.rearrange("(t p) d -> p t d", p=P)).then_inc(mem_landed, 16)
            root(16, N_MEM, 2, D)
            root(18, N_XQ, 2, D)
            root(20, N_MLP2, 2, D)
            pool.wait_ge(turned, KT // 2 * (H_MLP2 + 1))
            pool.dma_start(GB[:], final_g2.partition_broadcast(P)).then_inc(final_landed, 16)
            root(22, N_F2, 2, D)

        @block.tensor
        def _(pe):
            def vec_turn():
                pe.wait_ge(vec_landed, 16)
                pe.wait_ge(sq_landed, 16)
                for n in range(4):
                    last = pe.transpose(ps[:, 0, n * P:(n + 1) * P], VEC_RAW[:, n, :], IDENT)
                last.then_inc(vec_turned, 1)

            def turn(src):
                for k in range(KT):
                    for t in range(TT):
                        last = pe.transpose(ps[:, k // 2, (k % 2) * T + t * P:(k % 2) * T + (t + 1) * P], src(k, t), IDENT)
                    if k % 2:
                        last.then_inc(turned, 1)

            def stationary(h):
                pe.wait_ge(ht_hi, KT * (h + 1))
                pe.wait_ge(ht_lo, KT * (h + 1))

            def step(s, hi, lo, k, group, first, last, off=0):
                pe.wait_ge(hi_ready, s + off + 1)
                pe.wait_ge(lo_ready, s + off + 1)
                slot = s % NSPLIT
                for j in range(STEP):
                    for t in range(TT):
                        xh = hi[:, k + j, t * P:(t + 1) * P]
                        xl = lo[:, k + j, t * P:(t + 1) * P]
                        for c in range(2):
                            o = ps[:, 4 * group + 2 * t + c, :]
                            pe.matmul(o, xh, WHI[:, slot, j, c * BANK:(c + 1) * BANK], start=first and j == 0, stop=False)
                            pe.matmul(o, xh, WLO[:, slot, j, c * BANK:(c + 1) * BANK], start=False, stop=False)
                        for c in range(2):
                            o = ps[:, 4 * group + 2 * t + c, :]
                            mm = pe.matmul(o, xl, WHI[:, slot, j, c * BANK:(c + 1) * BANK], start=False, stop=last and j == STEP - 1)
                mm.then_inc(w_used, 1)

            def bank_free(p, off=0):
                if p >= 2:
                    pe.wait_ge(out0, p + off - 1)
                    pe.wait_ge(out1, p + off - 1)

            def gemm_pass(s0, p):
                bank_free(p)
                for k in range(PS):
                    step(s0 + k, HHI, HLO, STEP * k, p % 2, k == 0, k == PS - 1)

            def mlp(m, s0, p0, h):
                stationary(h)
                with pe.Fori(0, 2) as half:
                    off, poff, aoff = half * HALF_STEPS, half * HALF_PASSES, half * 16

                    def turn_hidden(p):
                        pe.wait_ge(out0, p0 + p + 1 + poff)
                        pe.wait_ge(out1, p0 + p + 1 + poff)
                        g = 4 * (p % 2)
                        for b in range(4):
                            for k in range(2 * b, 2 * b + 2):
                                for t in range(TT):
                                    last = pe.transpose(ps[:, g + b, (k % 2) * T + t * P:(k % 2) * T + (t + 1) * P],
                                                        R[:, t, k * P:(k + 1) * P], IDENT)
                            last.then_inc(r_turned, 1)

                    for p in range(4):
                        bank_free(p0 + p, poff)
                        if p >= 2:
                            pe.wait_ge(at_hi, 32 * m + 4 * (p - 1) + aoff)
                            pe.wait_ge(at_lo, 32 * m + 4 * (p - 1) + aoff)
                        for k in range(PS):
                            if p >= 1 and k == 2:
                                turn_hidden(p - 1)
                            step(s0 + p * PS + k, HHI, HLO, STEP * k, p % 2, k == 0, k == PS - 1, off)
                    for d in range(2):
                        n = HK // STEP
                        bank_free(p0 + 4 + d, poff)
                        pe.wait_ge(at_hi, 32 * m + 12 + 4 * d + aoff)
                        pe.wait_ge(at_lo, 32 * m + 12 + 4 * d + aoff)
                        for k in range(n):
                            if d == 0 and k == 2:
                                turn_hidden(3)
                            if d == 0 and k == 12:
                                pe.wait_ge(at_hi, 32 * m + 16 + aoff)
                                pe.wait_ge(at_lo, 32 * m + 16 + aoff)
                            step(s0 + 4 * PS + d * n + k, AHI, ALO, STEP * k, d, k == 0, k == n - 1, off)

            vec_turn()
            pe.wait_ge(vec_ready, 1)
            pe.wait_ge(xn_ready, 2)
            turn(lambda k, t: xn[:, t, k * P:(k + 1) * P])
            stationary(H_IN)
            for n in range(4):
                gemm_pass(S_IN + n * PS, P_IN + n)
            pe.wait_ge(out0, P_IN + 4)
            pe.wait_ge(out1, P_IN + 4)
            for n in range(2):
                for h in range(HEADS):
                    for t in range(TT):
                        c = (1 + n) * COLS + h * HD
                        last = pe.transpose(ps[:, 4 * n + h // 2, (h % 2) * T + t * P:(h % 2) * T + (t + 1) * P],
                                            PROJ[:, t, c:c + HD], IDENT)
                last.then_inc(qk_turned, 1)
            pe.wait_ge(poola_landed, 16)
            pe.wait_ge(qt_ready, 1)
            for n in range(2 * len(WINDOWS)):
                for t in range(TT):
                    last = pe.matmul(ps[:, n // 2, (n % 2) * T:(n % 2 + 1) * T], PROJ[:, t, n * P:(n + 1) * P],
                                     POOLA[:, n // 2, t, :], start=t == 0, stop=t == TT - 1)
            last.then_inc(pooled, 1)
            pe.wait_ge(pooled_ready, 1)
            pe.wait_ge(poolw_landed, 16)
            pe.wait_ge(kt_ready, 1)
            for t in range(TT):
                for g in range(len(WINDOWS)):
                    for c in range(2):
                        last = pe.matmul(ps[:, 4 + 2 * t + g // 2, (g % 2) * GROUP:(g % 2 + 1) * GROUP],
                                         DT[:, 2 * g + c, t * P:(t + 1) * P], POOLW[:, g, c, :], start=c == 0, stop=c == 1)
            last.then_inc(pool_out, 1)

            def scores(h):
                if h >= 2:
                    pe.wait_ge(max_ready, h - 1)
                pe.matmul(ps[:, h % 2, 0:P], QT[:, h, 0:P], KTT[:, h, 0:P], start=True, stop=True)
                pe.matmul(ps[:, h % 2, P:P + T], QT[:, h, P:T], KTT[:, h, :], start=True, stop=True).then_inc(scored, 1)

            def attend(h):
                s = h % 2
                pe.wait_ge(probs_ready, h + 1)
                if h >= 2:
                    pe.wait_ge(pt_ready, h - 1)
                pe.transpose(ps[:, 2 + s, 0:P], S1[:, s, 0:P], IDENT)
                pe.transpose(ps[:, 2 + s, P:T], S1[:, s, P:T], IDENT)
                pe.transpose(ps[:, 2 + s, T:NS], S1[:, s, T:NS], IDENT).then_inc(probs_turned, 1)
                pe.wait_ge(pt_ready, h + 1)
                if h >= 2:
                    pe.wait_ge(y_attn, h - 1)
                v = [PROJ[:, t, 3 * COLS + h * HD:3 * COLS + (h + 1) * HD] for t in range(TT)]
                pe.matmul(ps[:, 4 + s, 0:P], PT1[:, s, 0:P], v[0], start=True, stop=True)
                pe.matmul(ps[:, 4 + s, P:T], PT1[:, s, P:T], v[0], start=True, stop=False)
                pe.matmul(ps[:, 4 + s, P:T], PT1[:, s, T:NS], v[1], start=False, stop=True).then_inc(attended, 1)

            pe.wait_ge(y_pool, 1)
            scores(0)
            for h in range(HEADS):
                if h + 1 < HEADS:
                    scores(h + 1)
                attend(h)
            pe.wait_ge(y_ready, 1)
            turn(lambda k, t: PROJ[:, t, k * P:(k + 1) * P])
            stationary(H_OUT)
            for n in range(2):
                gemm_pass(S_OUT + n * PS, P_OUT + n)
            pe.wait_ge(xn_ready, 4)
            turn(lambda k, t: xn[:, t, k * P:(k + 1) * P])
            mlp(0, S_MLP, P_MLP, H_MLP)

            pe.wait_ge(xn_ready, 6)
            turn(lambda k, t: xn[:, t, k * P:(k + 1) * P])
            stationary(H_IN2)
            for n in range(6):
                gemm_pass(S_IN2 + n * PS, P_IN2 + n)
            bank_free(P_IN2 + 6)
            pe.wait_ge(ba_split, 2)
            for t in range(TT):
                for k in range(KT):
                    xh, xl = HHI[:, k, t * P:(t + 1) * P], HLO[:, k, t * P:(t + 1) * P]
                    o = ps[:, 2 * t, 0:NBA]
                    pe.matmul(o, xh, BAHI[:, k, :], start=k == 0, stop=False)
                    pe.matmul(o, xh, BALO[:, k, :], start=False, stop=False)
                    last = pe.matmul(o, xl, BAHI[:, k, :], start=False, stop=k == KT - 1)
            last.then_inc(ba_done, 1)
            pe.wait_ge(ba_out, 1)

            SECTIONS = [(GA, COUT31), (QTOK, COUT), (KTOK, COUT), (VTOK, COUT)]

            def conv_in(n):
                if n == 0:
                    pe.wait_ge(glu_ready, 1)
                else:
                    pe.wait_ge(cin_ready, n)
                for c in range(HEADS):
                    for t in range(TT):
                        last = pe.transpose(ps[:, c // 2, (c % 2) * T + t * P:(c % 2) * T + (t + 1) * P],
                                            SECTIONS[n][0][:, t, c * P:(c + 1) * P], IDENT)
                last.then_inc(conv_turned, 1)

            def conv_out(n):
                pe.wait_ge(silu_ready, n + 1)
                if n >= 1:
                    pe.wait_ge(sec0, n)
                    pe.wait_ge(sec1, n)
                for t in range(TT):
                    for c in range(HEADS):
                        last = pe.transpose(ps[:, 4 + 2 * t + c // 4, (c % 4) * P:(c % 4 + 1) * P],
                                            SECTIONS[n][1][:, c, t * P:(t + 1) * P], IDENT)
                last.then_inc(conv_back, 1)

            pe.wait_ge(out0, P_IN2 + 6)
            pe.wait_ge(out1, P_IN2 + 6)
            conv_in(0)
            conv_in(1)
            conv_out(0)
            conv_in(2)
            conv_out(1)
            conv_in(3)
            conv_out(2)
            conv_out(3)

            pe.wait_ge(gate_ready, 1)
            G16 = gate[:].rearrange("p t h -> p (t h)")
            pe.matmul(ps[:, 0, 0:U16], TRI, G16, start=True, stop=True)
            pe.matmul(ps[:, 0, 16:16 + U16], SAME, G16, start=True, stop=True)
            for n in range(T // CHUNK):
                r = CHUNK * (n % 2)
                last = pe.matmul(ps[:, n % 2, 32 + n // 2 * HEADS:32 + (n // 2 + 1) * HEADS], ONES[r:r + CHUNK, :],
                                 gate[r:r + CHUNK, n // 2, :], start=True, stop=True)
            last.then_inc(gate_summed, 1)
            for n, (src, ready) in enumerate(((QTOK, qn_ready), (KTOK, kn_ready), (KB_, kb_ready))):
                pe.wait_ge(ready, 1)
                g = 4 * ((n + 1) % 2)
                if n == 1:
                    pe.wait_ge(kd_sub, 1)
                    pe.wait_ge(exps_ready, 1)
                if n == 2:
                    pe.wait_ge(qk2_ready, 1)
                for h in range(HEADS):
                    for t in range(TT):
                        v = src[:, t, h * HD:(h + 1) * HD] if n < 2 else KB_[:, t, h, :]
                        last = pe.transpose(ps[:, g + h // 2, (h % 2) * T + t * P:(h % 2) * T + (t + 1) * P], v, IDENT)
                last.then_inc(qk2_turned, 1)
            pe.wait_ge(qk2_ready, 2)
            pe.wait_ge(diag_ready, 1)
            for b in range(4):
                last = pe.matmul(ps[:, b, :], ONES, DIAG[:, 4 * b:4 * b + 4, :].rearrange("p u c -> p (u c)"), start=True, stop=True)
            last.then_inc(rows_ready, 1)
            pe.wait_ge(qk2_ready, 3)
            for n, other in enumerate((KBT, QT2)):
                if n == 1:
                    pe.wait_ge(decsub_ready, 1)
                for u in range(U16):
                    t, h = u // HEADS, u % HEADS
                    last = pe.matmul(ps[:, 4 * (1 - n) + u // 4, (u % 4) * P:(u % 4 + 1) * P],
                                     KT2[:, h, t * P:(t + 1) * P], other[:, h, t * P:(t + 1) * P], start=True, stop=True)
                last.then_inc(gram_done, 1)
            pe.wait_ge(gram_ready, 2)

            def units(group, lhs, rhs):
                for u in range(U16):
                    last = pe.matmul(ps[:, 4 * group + u // 4, (u % 4) * P:(u % 4 + 1) * P], lhs[:, u, :], rhs[:, u, :], start=True, stop=True)
                return last

            pe.wait_ge(level_ready, 1)
            for u in range(U16):
                last = pe.transpose(ps[:, u // 4, (u % 4) * P:(u % 4 + 1) * P], LB[:, u, :], IDENT)
            last.then_inc(wl_done, 1)
            for lv in range(1, LEVELS):
                pe.wait_ge(level_ready, lv + 1)
                pe.wait_ge(x_up, lv)
                pe.wait_ge(xt_up, lv)
                units(0, LB, XI).then_inc(wl_done, 1)
                pe.wait_ge(wl_ready, lv)
                if lv < LEVELS - 1:
                    units(1, XT, WL).then_inc(xw_done, 1)
                units(0, WL, XT).then_inc(xt_done, 1)
            pe.wait_ge(xt_up, LEVELS)
            pe.wait_ge(tok_ready, 1)
            for u in range(U16):
                t, h = u // HEADS, u % HEADS
                pe.matmul(ps[:, u // 4, (u % 4) * P:(u % 4 + 1) * P], XT[:, u, :], VTOK[:, t, h * HD:(h + 1) * HD], start=True, stop=True)
            for h in range(HEADS):
                for t in range(TT):
                    last = pe.matmul(ps[:, 4 + h // 2, (h % 2) * T + t * P:(h % 2) * T + (t + 1) * P],
                                     KBG[:, t, h, :], XT[:, t * HEADS + h, :], start=True, stop=True)
            last.then_inc(uw_done, 1)
            pe.wait_ge(u_ready, 1)
            pe.wait_ge(wt_ready, 1)
            for n in range(T // CHUNK):
                t, r = n // 2, CHUNK * (n % 2)
                rows = slice(r, r + CHUNK)
                pe.wait_ge(state_ready, n + 1)
                if n >= 1:
                    pe.wait_ge(qs_ready, n)
                for h in range(HEADS):
                    pe.matmul(ps[rows, h // 4, (h % 4) * P:(h % 4 + 1) * P], WT[:, h, t * P + r:t * P + r + CHUNK], ST[:, h, :], start=True, stop=True)
                for h in range(HEADS):
                    last = pe.matmul(ps[rows, 2 + h // 4, (h % 4) * P:(h % 4 + 1) * P], QT2[:, h, t * P + r:t * P + r + CHUNK], ST[:, h, :], start=True, stop=True)
                last.then_inc(ws_done, 1)
                pe.wait_ge(vn_ready, n + 1)
                for h in range(HEADS):
                    pe.matmul(ps[:, 6 + h // 4, (h % 4) * P:(h % 4 + 1) * P], KDEC[rows, t, h, :], VN[rows, h, :], start=True, stop=True)
                if n >= 1:
                    pe.wait_ge(o_ready, n)
                for h in range(HEADS):
                    last = pe.matmul(ps[rows, 4 + h // 4, (h % 4) * P:(h % 4 + 1) * P], ATT[rows, t * HEADS + h, r:r + CHUNK], VN[rows, h, :], start=True, stop=True)
                last.then_inc(vn_used, 1)
            pe.wait_ge(o_final, 1)
            pe.wait_ge(c_final, 1)
            turn(lambda k, t: O[:, t, k, :] if k < HEADS else GA[:, t, (k - HEADS) * P:(k - HEADS + 1) * P])
            stationary(H_OUT2)
            for n in range(2):
                gemm_pass(S_OUT2 + n * PS, P_OUT2 + n)

            pe.wait_ge(xn_ready, 8)
            pe.wait_ge(out0, P_OUT2 + 2)
            pe.wait_ge(out1, P_OUT2 + 2)
            turn(lambda k, t: MEM[:, t, k * P:(k + 1) * P])
            stationary(H_MEM)
            for n in range(4):
                gemm_pass(S_KV + n * PS, P_KV + n)
            pe.wait_ge(out0, P_KV + 4)
            pe.wait_ge(out1, P_KV + 4)

            def turn_rows(src):
                for k in range(KT):
                    for t in range(TT):
                        last = pe.transpose(ps[:, k // 2, (k % 2) * T + t * P:(k % 2) * T + (t + 1) * P], src(k, t), IDENT)
                last.then_inc(kx_turned, 1)

            turn_rows(lambda k, t: KV[:, t, k * P:(k + 1) * P])
            pe.wait_ge(kx_ready, 2)
            pe.wait_ge(xn_ready, 10)
            turn(lambda k, t: xn[:, t, k * P:(k + 1) * P])
            stationary(H_XQ)
            for n in range(2):
                gemm_pass(S_Q + n * PS, P_Q + n)
            pe.wait_ge(out0, P_Q + 2)
            pe.wait_ge(out1, P_Q + 2)
            turn_rows(lambda k, t: QX[:, t, k * P:(k + 1) * P])
            pe.wait_ge(kx_ready, 4)

            def xscores(h):
                if h >= 2:
                    pe.wait_ge(xprobs, h - 1)
                for q in range(TT):
                    for d in range(XDT):
                        last = pe.matmul(ps[:, h % 2, q * T:(q + 1) * T], QXT[:, XDT * h + d, q * P:(q + 1) * P],
                                         KXT[:, XDT * h + d, :], start=d == 0, stop=d == XDT - 1)
                last.then_inc(xscored, 1)

            def xattend(h):
                s = h % 2
                pe.wait_ge(xprobs, h + 1)
                if h >= 2:
                    pe.wait_ge(xpt, h - 1)
                for k in range(TT):
                    for q in range(TT):
                        last = pe.transpose(ps[:, 2 + s, k * T + q * P:k * T + (q + 1) * P], PX[:, s, q, k * P:(k + 1) * P], IDENT)
                last.then_inc(xturned, 1)
                pe.wait_ge(xpt, h + 1)
                if h >= 2:
                    pe.wait_ge(xout, h - 1)
                for q in range(TT):
                    for k in range(TT):
                        last = pe.matmul(ps[:, 4 + 2 * s + q, :], PXT[:, s, k, q * P:(q + 1) * P],
                                         KV[:, k, D + h * XHD:D + (h + 1) * XHD], start=k == 0, stop=k == TT - 1)
                last.then_inc(xatt, 1)

            xscores(0)
            for h in range(XHEADS):
                if h + 1 < XHEADS:
                    xscores(h + 1)
                xattend(h)
            pe.wait_ge(xout, XHEADS)
            turn(lambda k, t: QX[:, t, k * P:(k + 1) * P])
            stationary(H_XO)
            for n in range(2):
                gemm_pass(S_O + n * PS, P_O + n)
            pe.wait_ge(xn_ready, 12)
            turn(lambda k, t: xn[:, t, k * P:(k + 1) * P])
            mlp(1, S_MLP2, P_MLP2, H_MLP2)

        @block.scalar
        def _(act):
            own = Own(act, act_own)

            def split(s, off=0):
                act.wait_ge(raw_landed[s % NRAW], 16 * (s // NRAW + 1) + off * (16 // NRAW))
                if s >= NSPLIT:
                    act.wait_ge(w_used, s + off - NSPLIT + 1)
                act.activation(WHI[:, s % NSPLIT], RAW[:, s % NRAW], ACT.Copy).then_inc(hi_ready, 1)

            def squares_of(src, dst, junk=xn):
                for t in range(TT):
                    act.activation(junk[:, t, :], src[:, t, :], ACT.Square, accum_out=dst[:, t:t + 1]).then_inc(sq_done, 1)

            def split_turned(h, g):
                for k in range(KT):
                    act.wait_ge(turned, KT // 2 * h + k // 2 + 1)
                    v = ps[:, k // 2, (k % 2) * T:(k % 2 + 1) * T]
                    if g is None:
                        act.activation(HHI[:, k, :], v, ACT.Copy).then_inc(ht_hi, 1)
                    else:
                        act.activation(HHI[:, k, :], v, ACT.Copy, scale=gain(g(k))).then_inc(ht_hi, 1)

            def leave(s_end, p, dst):
                act.wait_ge(w_used, s_end)
                g = 4 * (p % 2)
                act.activation(dst, ps[:, g:g + 2, :].rearrange("p b n -> p (b n)"), ACT.Copy).then_inc(out0, 1)

            def passes(s0, p0, dsts):
                for n, dst in enumerate(dsts):
                    for k in range(PS):
                        split(s0 + n * PS + k)
                        if k == 0 and n > 0 and dsts[n - 1] is not None:
                            leave(s0 + n * PS, p0 + n - 1, dsts[n - 1])
                if dsts[-1] is not None:
                    leave(s0 + len(dsts) * PS, p0 + len(dsts) - 1, dsts[-1])

            def mlp(m, s0, p0):
                with act.Fori(0, 2) as half:
                    off, roff = half * HALF_STEPS, half * 16

                    def relu(p):
                        act.wait_ge(w_used, s0 + (p + 1) * PS + off)
                        if p >= 1:
                            act.wait_ge(r_turned, 32 * m + 4 * p + roff)
                        g = 4 * (p % 2)
                        for t in range(TT):
                            act.activation(R[:, t, :], ps[:, g + 2 * t:g + 2 * t + 2, :].rearrange("p b n -> p (b n)"), ACT.Relu).then_inc(relu_done, 1)

                    def hidden_hi(p):
                        g = 4 * (p % 2)
                        for b in range(4):
                            act.wait_ge(r_turned, 32 * m + 4 * p + b + 1 + roff)
                            act.activation(AHI[:, 8 * p + 2 * b:8 * p + 2 * b + 2, :].rearrange("p k t -> p (k t)"), ps[:, g + b, :], ACT.Copy).then_inc(at_hi, 1)

                    for p in range(4):
                        for k in range(PS):
                            split(s0 + p * PS + k, off)
                            if p >= 1 and k == 0:
                                relu(p - 1)
                            if p >= 1 and k == 2:
                                hidden_hi(p - 1)
                    n = HK // STEP
                    for k in range(2 * n):
                        split(s0 + 4 * PS + k, off)
                        if k == 0:
                            relu(3)
                        if k == 2:
                            hidden_hi(3)

            act.wait_ge(x_landed, 16)
            squares_of(X, ss)
            act.wait_ge(vec_ready, 1)
            split_turned(H_IN, lambda k: G_IN + k)
            passes(S_IN, P_IN, [PROJ[:, 0, n * COLS:(n + 1) * COLS] for n in range(4)])
            act.wait_ge(qk_turned, 1)
            act.activation(QT[:].rearrange("p h t -> p (h t)"), ps[:, 0:4, :].rearrange("p b n -> p (b n)"), ACT.Copy).then_inc(qt_ready, 1)
            act.wait_ge(pooled, 1)
            act.activation(DT[:].rearrange("p h t -> p (h t)"), ps[:, 0:4, :].rearrange("p b n -> p (b n)"), ACT.Copy).then_inc(pooled_ready, 1)
            for h in range(HEADS):
                s = h % 2
                act.wait_ge(max_ready, h + 1)
                act.activation(S1[:, s, 0:P], S1[:, s, 0:P], ACT.Exp, bias=nmax[:, s, 0:1], accum_out=den[:, s, 0:1])
                act.activation(S1[:, s, P:NS], S1[:, s, P:NS], ACT.Exp, bias=nmax[:, s, 1:2], accum_out=den[:, s, 1:2]).then_inc(probs_ready, 1)
                act.wait_ge(probs_turned, h + 1)
                if h >= 2:
                    act.wait_ge(attended, h - 1)
                act.activation(PT1[:, s, :], ps[:, 2 + s, 0:NS], ACT.Copy).then_inc(pt_ready, 1)
            act.wait_ge(y_attn, HEADS)
            for n in range(2):
                for t in range(TT):
                    act.activation((DT, QT)[n][:, 4 * t:4 * t + 4, :].rearrange("p h t -> p (h t)"), PROJ[:, t, n * COLS:(n + 1) * COLS], ACT.Square,
                                   accum_out=ss[:, 2 * n + t:2 * n + t + 1]).then_inc(sq_done, 1)
            split_turned(H_OUT, lambda k: G_OUT + k)
            passes(S_OUT, P_OUT, [None, None])
            act.wait_ge(out1, P_OUT + 2)
            squares_of(X, ss)
            split_turned(H_MLP, lambda k: G_MLP + k)
            mlp(0, S_MLP, P_MLP)
            act.wait_ge(out1, P_MLP + 2 * HALF_PASSES)
            squares_of(X, ss, ROWS)
            act.wait_ge(x_final, 2)
            squares_of(X, ss)
            split_turned(H_IN2, lambda k: G_IN2 + k)
            act.wait_ge(ba_landed, 16)
            act.activation(BAHI[:], BARAW[:], ACT.Copy).then_inc(ba_split, 1)
            passes(S_IN2, P_IN2, [PROJ2[:, n, 0, :] for n in range(6)])
            act.wait_ge(out0, P_IN2 + 6)
            act.wait_ge(out1, P_IN2 + 6)
            act.activation(GBT, GBT, ACT.Sigmoid).then_inc(glu_sig, 1)
            act.wait_ge(ba_out, 1)
            act.activation(beta[:], ba[:, :, 0:HEADS], ACT.Sigmoid).then_inc(beta_ready, 1)
            SEC = [GA, QTOK, KTOK, VTOK]

            def conv_load(n):
                act.wait_ge(conv_turned, n + 1)
                act.wait_ge(pads_ready, 2)
                if n >= 2:
                    act.wait_ge(conv_done, n)
                dst = CIN31[:, :, DW - 1:] if n == 0 else CIN[:, :, CONV - 1:]
                act.activation(dst, ps[:, 0:4, :].rearrange("p b (c t) -> p (b c) t", t=T), ACT.Copy).then_inc(cin_ready, 1)

            def conv_silu(n):
                act.wait_ge(conv_done, n + 1)
                if n == 0:
                    act.activation(COUT31[:], COUT31[:], ACT.Copy).then_inc(silu_ready, 1)
                else:
                    act.activation(COUT[:], COUT[:], ACT.Silu).then_inc(silu_ready, 1)

            def conv_store(n):
                act.wait_ge(conv_back, n + 1)
                act.activation(SEC[n][:, 0, :], ps[:, 4:6, :].rearrange("p b n -> p (b n)"), ACT.Copy).then_inc(sec0, 1)

            conv_load(0)
            conv_load(1)
            conv_silu(0)
            conv_store(0)
            conv_silu(1)
            conv_load(2)
            conv_store(1)
            conv_silu(2)
            conv_load(3)
            conv_store(2)
            conv_silu(3)
            conv_store(3)
            act.activation(ZTOK, ZTOK, ACT.Silu).then_inc(z_ready, 1)
            act.wait_ge(csum, 1)
            for t in range(TT):
                act.activation(GBT[:, t, :], GA[:, t, :], ACT.Square, accum_out=ss[:, t:t + 1]).then_inc(sq_done, 1)
            for n, (src, dst) in enumerate(((QTOK, SQQ), (KTOK, SQK))):
                act.wait_ge(sec0, 4)
                act.wait_ge(sec1, 4)
                act.activation(dst[:].rearrange("p t h d -> p (t h d)"), src.rearrange("p t d -> p (t d)"), ACT.Square).then_inc(l2_sq, 1)
            act.wait_ge(gates_landed, 32)
            act.activation(alog[:], alog[:], ACT.Exp).then_inc(ea_ready, 1)
            act.wait_ge(adt_ready, 1)
            act.activation(sp_e[:], sp_e[:], ACT.Exp, scale=-1.0).then_inc(spe_ready, 1)
            act.wait_ge(gate_summed, 1)
            act.activation(egl[:].rearrange("p (t b) h -> p b t h", b=2), ps[:, 0:2, 32:48].rearrange("p b (t h) -> p b t h", h=HEADS), ACT.Exp)
            act.activation(gcs[:].rearrange("p t h -> p (t h)"), ps[:, 0, 0:U16], ACT.Copy).then_inc(gcs_ready, 1)
            act.wait_ge(gcs_ready, 1)
            act.activation(eg[:], gcs[:], ACT.Exp)
            act.wait_ge(kd_sub, 1)
            act.activation(kd[:], kd[:], ACT.Exp).then_inc(exps_ready, 1)
            for n, dst in enumerate((QT2, KT2, KBT)):
                act.wait_ge(qk2_turned, n + 1)
                g = 4 * ((n + 1) % 2)
                act.activation(dst[:].rearrange("p h t -> p (h t)"), ps[:, g:g + 4, :].rearrange("p b n -> p (b n)"), ACT.Copy).then_inc(qk2_ready, 1)
            act.wait_ge(decsub_ready, 1)
            act.activation(DEC[:], DEC[:], ACT.Exp).then_inc(decay_ready, 1)
            for lv in range(1, LEVELS):
                act.wait_ge(wl_done, lv + 1)
                if lv >= 2:
                    act.wait_ge(xt_done, lv - 1)
                act.activation(WL[:].rearrange("p u c -> p (u c)"), ps[:, 0:4, :].rearrange("p b n -> p (b n)"), ACT.Copy).then_inc(wl_ready, 1)
            act.wait_ge(uw_done, 1)
            act.activation(WT[:].rearrange("p h t -> p (h t)"), ps[:, 4:8, :].rearrange("p b n -> p (b n)"), ACT.Copy).then_inc(wt_ready, 1)
            act.wait_ge(o_ready, T // CHUNK)
            act.activation(OSQ[:], O[:], ACT.Square).then_inc(osq_ready, 1)
            for k in range(KT):
                act.wait_ge(turned, KT // 2 * H_OUT2 + k // 2 + 1)
                v = ps[:, k // 2, (k % 2) * T:(k % 2 + 1) * T]
                if k < HEADS:
                    act.activation(HHI[:, k, :], v, ACT.Copy, scale=gain(G_DN)).then_inc(ht_hi, 1)
                else:
                    c = k - HEADS
                    act.activation(CS[:, c, :], v, ACT.Silu, scale=dw_vec(1, c), bias=dw_vec(2, c)).then_inc(cs_ready, 1)
                    act.wait_ge(cs_ready, c + 1)
                    act.activation(HHI[:, k, :], CS[:, c, :], ACT.Copy).then_inc(ht_hi, 1)
            passes(S_OUT2, P_OUT2, [None, None])
            act.wait_ge(mem_landed, 16)
            for t in range(TT):
                act.activation(QX[:, t, :], MEM[:, t, :], ACT.Square, accum_out=ss[:, t:t + 1]).then_inc(sq_done, 1)
            split_turned(H_MEM, lambda k: G_MEM + k)
            passes(S_KV, P_KV, [KV[:, 0, n * COLS:(n + 1) * COLS] for n in range(4)])
            act.wait_ge(kx_turned, 1)
            act.activation(KXT[:, 0:8, :].rearrange("p k t -> p (k t)"), ps[:, 0:4, :].rearrange("p b n -> p (b n)"), ACT.Copy).then_inc(kx_ready, 1)
            squares_of(X, ss)
            split_turned(H_XQ, lambda k: G_XQ + k)
            passes(S_Q, P_Q, [QX[:, 0, n * COLS:(n + 1) * COLS] for n in range(2)])
            act.wait_ge(kx_turned, 2)
            act.activation(QXT[:, 0:8, :].rearrange("p k t -> p (k t)"), ps[:, 0:4, :].rearrange("p b n -> p (b n)"), ACT.Copy).then_inc(kx_ready, 1)
            for h in range(XHEADS):
                s = h % 2
                act.wait_ge(xmax, h + 1)
                if h >= 2:
                    act.wait_ge(xturned, h - 1)
                for q in range(TT):
                    last = act.activation(PX[:, s, q, :], ps[:, s, q * T:(q + 1) * T], ACT.Exp, bias=nmax[:, s, q:q + 1],
                                          scale=float(XHD) ** -0.5, accum_out=den[:, s, q:q + 1])
                last.then_inc(xprobs, 1)
                act.wait_ge(xturned, h + 1)
                if h >= 2:
                    act.wait_ge(xatt, h - 1)
                act.activation(PXT[:, s].rearrange("p k t -> p (k t)"), ps[:, 2 + s, :], ACT.Copy).then_inc(xpt, 1)
            split_turned(H_XO, None)
            passes(S_O, P_O, [None, None])
            act.wait_ge(out1, P_O + 2)
            squares_of(X, ss)
            split_turned(H_MLP2, lambda k: G_MLP2 + k)
            mlp(1, S_MLP2, P_MLP2)
            act.wait_ge(out1, P_MLP2 + 2 * HALF_PASSES)
            squares_of(X, ss, ROWS)

        @block.vector
        def _(dve):
            own = Own(dve, dve_own)

            def split(s, off=0):
                dve.wait_ge(hi_ready, s + off + 1)
                if s >= NSPLIT:
                    dve.wait_ge(w_used, s + off - NSPLIT + 1)
                dve.tensor_tensor(WLO[:, s % NSPLIT], RAW[:, s % NRAW], WHI[:, s % NSPLIT].bitcast(F32), ALU.subtract).then_inc(lo_ready, 1)

            def normalise(n, dst, src):
                dve.wait_ge(rstd_ready, n + 1)
                for t in range(TT):
                    dve.tensor_scalar(dst[:, t, :], src[:, t, :], rstd[:, t:t + 1], None, ALU.mult).then_inc(xn_ready, 1)

            def split_turned(h, g):
                for k in range(KT):
                    dve.wait_ge(ht_hi, KT * h + k // 2 * 2 + 2)
                    v = ps[:, k // 2, (k % 2) * T:(k % 2 + 1) * T]
                    if g is None:
                        dve.tensor_tensor(HLO[:, k, :], v, HHI[:, k, :].bitcast(F32), ALU.subtract).then_inc(ht_lo, 1)
                    else:
                        dve.scalar_tensor_tensor(HLO[:, k, :], v, gain(g(k)), HHI[:, k, :].bitcast(F32), ALU.mult, ALU.subtract).then_inc(ht_lo, 1)

            def leave(s_end, p, dst):
                dve.wait_ge(w_used, s_end)
                g = 4 * (p % 2) + 2
                dve.tensor_copy(dst, ps[:, g:g + 2, :].rearrange("p b n -> p (b n)")).then_inc(out1, 1)

            def add_residual(s_end, p, c0, off=0):
                dve.wait_ge(w_used, s_end + off)
                for t, o in enumerate((out0, out1)):
                    g = 4 * (p % 2) + 2 * t
                    v = X[:, t, c0:c0 + COLS]
                    dve.tensor_tensor(v, ps[:, g:g + 2, :].rearrange("p b n -> p (b n)"), v, ALU.add).then_inc(o, 1)

            def passes(s0, p0, dsts):
                for n in range(len(dsts) + 1):
                    for k in range(PS if n < len(dsts) else 0):
                        split(s0 + n * PS + k)
                        if k == 0 and n > 0:
                            done(s0, p0, n - 1, dsts)
                done(s0, p0, len(dsts) - 1, dsts)

            def done(s0, p0, n, dsts):
                if dsts[n] is None:
                    add_residual(s0 + (n + 1) * PS, p0 + n, n * COLS)
                else:
                    leave(s0 + (n + 1) * PS, p0 + n, dsts[n])

            def mlp(m, s0, p0):
                with dve.Fori(0, 2) as half:
                    off, roff, hoff = half * HALF_STEPS, half * 16, half * 8

                    def square(p):
                        g = 4 * (p % 2)
                        for t, o in enumerate((out0, out1)):
                            dve.wait_ge(relu_done, 16 * m + 2 * p + t + 1 + hoff)
                            dve.scalar_tensor_tensor(R[:, t, :], ps[:, g + 2 * t:g + 2 * t + 2, :].rearrange("p b n -> p (b n)"), 0.0, R[:, t, :],
                                                     ALU.max, ALU.mult).then_inc(o, 1)

                    def hidden_lo(p):
                        g = 4 * (p % 2)
                        for b in range(4):
                            dve.wait_ge(at_hi, 32 * m + 4 * p + b + 1 + roff)
                            k = 8 * p + 2 * b
                            dve.tensor_tensor(ALO[:, k:k + 2, :].rearrange("p k t -> p (k t)"), ps[:, g + b, :],
                                              AHI[:, k:k + 2, :].bitcast(F32).rearrange("p k t -> p (k t)"), ALU.subtract).then_inc(at_lo, 1)

                    for p in range(4):
                        for k in range(PS):
                            split(s0 + p * PS + k, off)
                            if p >= 1 and k == 0:
                                square(p - 1)
                            if p >= 1 and k == 2:
                                hidden_lo(p - 1)
                    n = HK // STEP
                    for k in range(2 * n):
                        split(s0 + 4 * PS + k, off)
                        if k == 0:
                            square(3)
                        if k == 2:
                            hidden_lo(3)
                        if k == n:
                            add_residual(s0 + 4 * PS + n, 0, 0, off)
                    add_residual(s0 + 4 * PS + 2 * n, 1, COLS, off)

            dve.wait_ge(vec_turned, 1)
            dve.tensor_copy(VEC[:].rearrange("p n c -> p (n c)"), ps[:, 0, :]).then_inc(vec_ready, 1)
            normalise(N_IN, xn, X)
            dve.wait_ge(vec_ready, 1)
            split_turned(H_IN, lambda k: G_IN + k)
            passes(S_IN, P_IN, [PROJ[:, 1, n * COLS:(n + 1) * COLS] for n in range(4)])
            dve.wait_ge(qk_turned, 2)
            dve.tensor_copy(KTT[:].rearrange("p h t -> p (h t)"), ps[:, 4:8, :].rearrange("p b n -> p (b n)")).then_inc(kt_ready, 1)
            dve.wait_ge(pool_out, 1)
            dve.wait_ge(pools_landed, 16)
            for t in range(TT):
                last = dve.tensor_tensor(PROJ[:, t, 0:COLS], ps[:, 4 + 2 * t:6 + 2 * t, :].rearrange("p b n -> p (b n)"), PSB[:], ALU.mult)
            last.then_inc(y_pool, 1)
            dve.wait_ge(alibi_landed, 16)

            def biased(h):
                s = h % 2
                slope = 2.0 ** (-8.0 * (h + 1) / HEADS)
                own.wait()
                own.mark(dve.scalar_tensor_tensor(BIAS[:], ALIBI[:, 0, :], -slope, ALIBI[:, 1, :], ALU.mult, ALU.add))
                own.wait()
                dve.wait_ge(scored, h + 1)
                if h >= 2:
                    dve.wait_ge(probs_turned, h - 1)
                own.mark(dve.scalar_tensor_tensor(S1[:, s, :], ps[:, s, 0:NS], float(HD) ** -0.5, BIAS[:], ALU.mult, ALU.add))
                own.wait()
                own.mark(dve.tensor_reduce(nmax[:, s, 0:1], S1[:, s, 0:P], AX_X, ALU.max))
                own.mark(dve.tensor_reduce(nmax[:, s, 1:2], S1[:, s, P:NS], AX_X, ALU.max))
                own.wait()
                dve.tensor_scalar(nmax[:, s, :], nmax[:, s, :], -1.0, None, ALU.mult).then_inc(max_ready, 1)

            def weighted(h):
                s = h % 2
                dve.wait_ge(attended, h + 1)
                own.mark(dve.reciprocal(rden[:, s, :], den[:, s, :]))
                own.wait()
                for t in range(TT):
                    last = dve.tensor_scalar(PROJ[:, t, COLS + h * HD:COLS + (h + 1) * HD], ps[:, 4 + s, t * P:(t + 1) * P], rden[:, s, t:t + 1], None, ALU.mult)
                last.then_inc(y_attn, 1)

            biased(0)
            for h in range(HEADS):
                if h + 1 < HEADS:
                    biased(h + 1)
                weighted(h)
            dve.wait_ge(rstd_ready, N_MIX + 1)
            for n in range(2):
                for t in range(TT):
                    v = PROJ[:, t, n * COLS:(n + 1) * COLS]
                    last = dve.tensor_scalar(v, v, rstd[:, 2 * n + t:2 * n + t + 1], None, ALU.mult)
            last.then_inc(y_ready, 1)
            split_turned(H_OUT, lambda k: G_OUT + k)
            passes(S_OUT, P_OUT, [None, None])
            normalise(N_MLP, xn, X)
            split_turned(H_MLP, lambda k: G_MLP + k)
            mlp(0, S_MLP, P_MLP)

            def final(n, dst):
                dve.wait_ge(rstd_ready, n + 1)
                dve.wait_ge(final_landed, 16 if n == N_F1 else 32)
                for t in range(TT):
                    dve.scalar_tensor_tensor(dst[:, t, :], X[:, t, :], rstd[:, t:t + 1], GB[:], ALU.mult, ALU.mult).then_inc(x_final, 1)

            final(N_F1, X)
            dve.wait_ge(x_final, 2)
            normalise(N_IN2, xn, X)
            split_turned(H_IN2, lambda k: G_IN2 + k)
            dve.wait_ge(ba_split, 1)
            dve.tensor_tensor(BALO[:], BARAW[:], BAHI[:].bitcast(F32), ALU.subtract).then_inc(ba_split, 1)
            passes(S_IN2, P_IN2, [PROJ2[:, n, 1, :] for n in range(6)])
            dve.wait_ge(ba_done, 1)
            dve.tensor_copy(ba[:], ps[:, 0:4:2, 0:NBA]).then_inc(ba_out, 1)
            dve.wait_ge(glu_sig, 1)
            dve.tensor_tensor(GA, GA, GBT, ALU.mult).then_inc(glu_ready, 1)

            def conv4(n):
                dve.wait_ge(cin_ready, n + 1)
                if n >= 2:
                    dve.wait_ge(conv_back, n)
                c0 = (n - 1) * HEADS
                for j in range(CONV):
                    for c in range(HEADS):
                        src = CIN[:, c, j:j + T]
                        if j == 0:
                            last = dve.tensor_scalar(COUT[:, c, :], src, tap(j, c0 + c), None, ALU.mult)
                        else:
                            if c == 0:
                                own.wait()
                            last = dve.scalar_tensor_tensor(COUT[:, c, :], src, tap(j, c0 + c), COUT[:, c, :], ALU.mult, ALU.add)
                        if j < CONV - 1:
                            own.mark(last)
                last.then_inc(conv_done, 1)

            def conv31():
                dve.wait_ge(cin_ready, 1)
                for j in range(DW):
                    for c in range(HEADS):
                        src = CIN31[:, c, j:j + T]
                        if j == 0:
                            last = dve.tensor_scalar(COUT31[:, c, :], src, dw_tap(j, c), dw_vec(0, c), ALU.mult, ALU.add)
                        else:
                            if c == 0:
                                own.wait()
                            last = dve.scalar_tensor_tensor(COUT31[:, c, :], src, dw_tap(j, c), COUT31[:, c, :], ALU.mult, ALU.add)
                        if j < DW - 1:
                            own.mark(last)
                last.then_inc(conv_done, 1)

            SEC = [GA, QTOK, KTOK, VTOK]

            def conv_store(n):
                dve.wait_ge(conv_back, n + 1)
                dve.tensor_copy(SEC[n][:, 1, :], ps[:, 6:8, :].rearrange("p b n -> p (b n)")).then_inc(sec1, 1)

            conv31()
            conv4(1)
            conv_store(0)
            conv4(2)
            conv_store(1)
            conv4(3)
            conv_store(2)
            conv_store(3)
            dve.wait_ge(sec0, 4)
            dve.wait_ge(sec1, 4)
            own.mark(dve.tensor_reduce(cmean[:], GA, AX_X, ALU.add))
            own.wait()
            own.mark(dve.tensor_scalar(cmean[:], cmean[:], -1.0 / COLS, None, ALU.mult))
            own.wait()
            for t in range(TT):
                last = dve.tensor_scalar(GA[:, t, :], GA[:, t, :], cmean[:, t:t + 1], None, ALU.add)
            last.then_inc(csum, 1)
            dve.wait_ge(gates_landed, 32)
            own.mark(dve.tensor_tensor(adt[:], ba[:, :, HEADS:NBA], dtb[:].unsqueeze(1).broadcast_to([P, TT, HEADS]), ALU.add))
            own.wait()
            dve.scalar_tensor_tensor(sp_e[:], adt[:], -1.0, adt[:], ALU.mult, ALU.max).then_inc(adt_ready, 1)
            dve.wait_ge(spe_ready, 1)
            own.mark(dve.tensor_scalar(sp_z[:], sp_e[:], 2.0, None, ALU.add))
            own.wait()
            own.mark(dve.reciprocal(sp_z[:], sp_z[:]))
            own.wait()
            own.mark(dve.tensor_tensor(sp_z[:], sp_z[:], sp_e[:], ALU.mult))
            own.wait()
            own.mark(dve.tensor_tensor(sp_q[:], sp_z[:], sp_z[:], ALU.mult))
            own.wait()
            own.mark(dve.tensor_scalar(sp_p[:], sp_q[:], 1.0 / (2 * LOG_TERMS - 1), None, ALU.mult))
            for n in range(LOG_TERMS - 2, 0, -1):
                own.wait()
                own.mark(dve.scalar_tensor_tensor(sp_p[:], sp_p[:], 1.0 / (2 * n + 1), sp_q[:], ALU.add, ALU.mult))
            own.wait()
            own.mark(dve.scalar_tensor_tensor(sp_p[:], sp_p[:], 1.0, sp_z[:], ALU.add, ALU.mult))
            own.mark(dve.tensor_scalar(adt[:], adt[:], 0.0, None, ALU.max))
            own.wait()
            own.mark(dve.scalar_tensor_tensor(sp_p[:], sp_p[:], 2.0, adt[:], ALU.mult, ALU.add))
            own.wait()
            dve.wait_ge(ea_ready, 1)
            dve.scalar_tensor_tensor(gate[:], sp_p[:], -1.0, alog[:].unsqueeze(1).broadcast_to([P, TT, HEADS]), ALU.mult, ALU.mult).then_inc(gate_ready, 1)
            dve.wait_ge(l2_sq, 2)
            for n, v in enumerate((SQQ, SQK)):
                dve.tensor_reduce(l2[:, n, :], v[:].rearrange("p t h d -> p (t h) d"), AX_X, ALU.add).then_inc(l2_sum, 1)
            dve.wait_ge(gcs_ready, 1)
            dve.tensor_tensor(kd[:].rearrange("p t h -> p (t h)"), ps[:, 0, 16:16 + U16], gcs[:].rearrange("p t h -> p (t h)"), ALU.subtract).then_inc(kd_sub, 1)
            dve.wait_ge(rstd_ready, N_LN + 1)
            for t in range(TT):
                last = dve.tensor_scalar(GA[:, t, :], GA[:, t, :], rstd[:, t:t + 1], None, ALU.mult)
            last.then_inc(c_final, 1)

            def heads(v):
                return v.rearrange("p t (h d) -> p t h d", d=HD)

            def per_head(v):
                return v.unsqueeze(3).broadcast_to([P, TT, HEADS, HD])

            def l2_of(n):
                return per_head(l2r[:, n, :].rearrange("p (t h) -> p t h", t=TT))

            dve.wait_ge(l2_ready, 1)
            dve.tensor_tensor(heads(QTOK), heads(QTOK), l2_of(0), ALU.mult).then_inc(qn_ready, 1)
            dve.tensor_tensor(heads(KTOK), heads(KTOK), l2_of(1), ALU.mult).then_inc(kn_ready, 1)
            dve.wait_ge(kn_ready, 1)
            dve.wait_ge(beta_ready, 1)
            dve.tensor_tensor(KB_[:], heads(KTOK), per_head(beta[:]), ALU.mult).then_inc(kb_ready, 1)
            for u in range(U16):
                last = dve.tensor_scalar(DIAG[:, u, :], IDENT, gcs[:, u // HEADS, u % HEADS:u % HEADS + 1], None, ALU.mult)
            last.then_inc(diag_ready, 1)
            dve.wait_ge(exps_ready, 1)
            dve.wait_ge(kb_ready, 1)
            dve.tensor_tensor(KBG[:], KB_[:], per_head(eg[:]), ALU.mult)
            dve.tensor_tensor(KDEC[:], heads(KTOK), per_head(kd[:]), ALU.mult)
            dve.tensor_tensor(heads(VTOK), heads(VTOK), per_head(beta[:]), ALU.mult).then_inc(tok_ready, 1)
            dve.wait_ge(rows_ready, 1)
            own.mark(dve.tensor_tensor(DEC[:], ps[:, 0:4, :].rearrange("p b (u c) -> p (b u) c", c=P),
                                       gcs[:].rearrange("p t h -> p (t h)").unsqueeze(2).broadcast_to([P, U16, P]), ALU.subtract))
            own.wait()
            dve.tensor_tensor(DEC[:], DEC[:], NEGMASK.unsqueeze(1).broadcast_to([P, U16, P]), ALU.add).then_inc(decsub_ready, 1)
            dve.wait_ge(decay_ready, 1)
            for n, dst in enumerate((LT, ATT)):
                dve.wait_ge(gram_done, n + 1)
                g = 4 * (1 - n)
                dve.tensor_tensor(dst[:].rearrange("p u c -> p (u c)"), ps[:, g:g + 4, :].rearrange("p b n -> p (b n)"),
                                  DEC[:].rearrange("p u c -> p (u c)"), ALU.mult).then_inc(gram_ready, 1)
            eye = IDENT.unsqueeze(1).broadcast_to([P, U16, P])

            def level(lv):
                if lv >= 1:
                    dve.wait_ge(wl_done, lv)
                dve.tensor_tensor(LB[:], LT[:], SQ[:, 5 + lv, :].unsqueeze(1).broadcast_to([P, U16, P]), ALU.mult).then_inc(level_ready, 1)

            flat_x = XI[:].rearrange("p u c -> p (u c)")
            flat_xt = XT[:].rearrange("p u c -> p (u c)")
            low = ps[:, 0:4, :].rearrange("p b n -> p (b n)")
            high = ps[:, 4:8, :].rearrange("p b n -> p (b n)")
            dve.wait_ge(gram_ready, 2)
            level(0)
            dve.wait_ge(level_ready, 1)
            dve.tensor_tensor(XT[:], eye, LB[:], ALU.subtract).then_inc(xt_up, 1)
            dve.wait_ge(wl_done, 1)
            dve.tensor_tensor(XI[:], eye, ps[:, 0:4, :].rearrange("p b (u c) -> p (b u) c", c=P), ALU.subtract).then_inc(x_up, 1)
            dve.wait_ge(xt_up, 1)
            for lv in range(1, LEVELS):
                level(lv)
                if lv < LEVELS - 1:
                    dve.wait_ge(xw_done, lv)
                    dve.wait_ge(x_up, lv)
                    dve.tensor_tensor(flat_x, flat_x, high, ALU.subtract).then_inc(x_up, 1)
                dve.wait_ge(xt_done, lv)
                dve.wait_ge(xt_up, lv)
                dve.tensor_tensor(flat_xt, flat_xt, low, ALU.subtract).then_inc(xt_up, 1)
            dve.wait_ge(uw_done, 1)
            dve.tensor_copy(U[:].rearrange("p t h d -> p (t h d)"), low).then_inc(u_ready, 1)
            dve.wait_ge(u_ready, 1)
            def two(b):
                return ps[:, b:b + 2, :].rearrange("p b (h d) -> p (b h) d", d=HD)

            for n in range(T // CHUNK):
                t, r = n // 2, CHUNK * (n % 2)
                rows = slice(r, r + CHUNK)
                dve.wait_ge(ws_done, n + 1)
                dve.tensor_tensor(VN[rows], U[rows, t], two(0)[rows], ALU.subtract).then_inc(vn_ready, 1)
                dve.tensor_tensor(O[rows, t], two(2)[rows], eg[rows, t, :].unsqueeze(2).broadcast_to([CHUNK, HEADS, HD]), ALU.mult).then_inc(qs_ready, 1)
                dve.wait_ge(vn_used, n + 1)
                dve.wait_ge(sd_ready, n + 1)
                if n + 1 < T // CHUNK:
                    dve.tensor_tensor(ST[:], SD[:], two(6), ALU.add).then_inc(state_ready, 1)
                dve.wait_ge(qs_ready, n + 1)
                dve.tensor_tensor(O[rows, t], O[rows, t], two(4)[rows], ALU.add).then_inc(o_ready, 1)
            dve.wait_ge(osq_ready, 1)
            dve.tensor_reduce(osum[:], OSQ[:].rearrange("p t h d -> p (t h) d"), AX_X, ALU.add).then_inc(osum_ready, 1)
            dve.wait_ge(z_ready, 1)
            own.mark(dve.tensor_tensor(O[:].rearrange("p t h d -> p (t h d)"), O[:].rearrange("p t h d -> p (t h d)"), ZTOK.rearrange("p t d -> p (t d)"), ALU.mult))
            own.wait()
            dve.wait_ge(orst_ready, 1)
            dve.tensor_tensor(O[:], O[:], per_head(orst[:].rearrange("p (t h) -> p t h", t=TT)), ALU.mult).then_inc(o_final, 1)
            for k in range(KT):
                dve.wait_ge(ht_hi, KT * H_OUT2 + k // 2 * 2 + 2)
                if k < HEADS:
                    dve.scalar_tensor_tensor(HLO[:, k, :], ps[:, k // 2, (k % 2) * T:(k % 2 + 1) * T], gain(G_DN), HHI[:, k, :].bitcast(F32), ALU.mult, ALU.subtract).then_inc(ht_lo, 1)
                else:
                    dve.tensor_tensor(HLO[:, k, :], CS[:, k - HEADS, :], HHI[:, k, :].bitcast(F32), ALU.subtract).then_inc(ht_lo, 1)
            passes(S_OUT2, P_OUT2, [None, None])
            dve.wait_ge(rstd_ready, N_MEM + 1)
            for t in range(TT):
                dve.tensor_scalar(MEM[:, t, :], MEM[:, t, :], rstd[:, t:t + 1], None, ALU.mult).then_inc(xn_ready, 1)
            split_turned(H_MEM, lambda k: G_MEM + k)
            passes(S_KV, P_KV, [KV[:, 1, n * COLS:(n + 1) * COLS] for n in range(4)])
            dve.wait_ge(kx_turned, 1)
            dve.tensor_copy(KXT[:, 8:16, :].rearrange("p k t -> p (k t)"), high).then_inc(kx_ready, 1)
            normalise(N_XQ, xn, X)
            split_turned(H_XQ, lambda k: G_XQ + k)
            passes(S_Q, P_Q, [QX[:, 1, n * COLS:(n + 1) * COLS] for n in range(2)])
            dve.wait_ge(kx_turned, 2)
            dve.tensor_copy(QXT[:, 8:16, :].rearrange("p k t -> p (k t)"), high).then_inc(kx_ready, 1)

            def xmaxima(h):
                s = h % 2
                dve.wait_ge(xscored, h + 1)
                if h >= 2:
                    dve.wait_ge(xprobs, h - 1)
                own.mark(dve.tensor_reduce(nmax[:, s, :], ps[:, s, :].rearrange("p (q k) -> p q k", q=TT), AX_X, ALU.max))
                own.wait()
                dve.tensor_scalar(nmax[:, s, :], nmax[:, s, :], -float(XHD) ** -0.5, None, ALU.mult).then_inc(xmax, 1)

            xmaxima(0)
            for h in range(XHEADS):
                s = h % 2
                if h + 1 < XHEADS:
                    xmaxima(h + 1)
                dve.wait_ge(xatt, h + 1)
                own.mark(dve.reciprocal(rden[:, s, :], den[:, s, :]))
                own.wait()
                for q in range(TT):
                    last = dve.tensor_scalar(QX[:, q, h * XHD:(h + 1) * XHD], ps[:, 4 + 2 * s + q, :], rden[:, s, q:q + 1], None, ALU.mult)
                last.then_inc(xout, 1)
            split_turned(H_XO, None)
            passes(S_O, P_O, [None, None])
            normalise(N_MLP2, xn, X)
            split_turned(H_MLP2, lambda k: G_MLP2 + k)
            mlp(1, S_MLP2, P_MLP2)
            final(N_F2, ROWS)


def kernel(**inputs):
    import numpy as _np
    import concourse.bacc as _bacc
    from concourse import mybir as _mybir
    from concourse.bass_utils import run_bass_kernel_spmd as _run

    a = {k: _np.asarray(v) for k, v in inputs.items()}

    def rows(*names):
        got = _np.concatenate([a[n].reshape(-1, 128) for n in names], 0)
        return _np.concatenate([got, _np.zeros((128 - len(got), 128), got.dtype)], 0)

    taps = a["cf_dw_w_2"].reshape(-1, 128)
    pad = _np.zeros((4, 128), taps.dtype)
    vectors = _np.stack([
        rows("norm_mix_g", "pool_out_norm_g", "attn_out_norm_g", "norm_mlp_g", "norm_mix_g_2", "norm_xa_g_2", "norm_mem_g_2",
             "norm_mlp_g_2", "dn_norm_g_2"),
        rows("dn_conv_w_2", "cf_dw_b_2", "cf_ln_g_2", "cf_ln_b_2"),
        _np.concatenate([taps[:124], pad], 0), _np.concatenate([taps[124:], pad], 0)])
    squares, alibi, pool_avg = shape_constants()
    feeds = {
        "x": a["x"][0], "mem": a["mem_2"][0], "vectors": vectors, "squares": squares, "alibi": alibi, "pool_avg": pool_avg,
        "w_in": a["w_in"][0], "pool_w": a["pool_w"][0], "pool_scale": a["pool_scale"][0], "w_out": a["w_out"][0],
        "w_up": a["w_up"][0], "w_down": a["w_down"][0], "final_g": a["norm_final_g"], "w_in2": a["w_in_2"][0],
        "a_log": a["dn_a_log_2"][0], "dt_bias": a["dn_dt_bias_2"][0], "w_out2": a["w_out_2"][0],
        "wq": a["xa_wq_2"][0], "wk": a["xa_wk_2"][0], "wv": a["xa_wv_2"][0], "wo": a["xa_wo_2"][0],
        "w1": a["mlp_w1_2"][0], "w2": a["mlp_w2_2"][0], "final_g2": a["norm_final_g_2"],
    }
    nc = _bacc.Bacc("TRN2", target_bir_lowering=False, num_devices=1)
    arrays, args = {}, {}
    for name, v in feeds.items():
        v = _np.ascontiguousarray(v)
        arrays[f"in_{name}"] = v
        args[name] = nc.dram_tensor(f"in_{name}", v.shape, _mybir.dt.from_np(v.dtype), kind="ExternalInput").ap()
    args["out"] = nc.dram_tensor("out_y", (T, D), F32, kind="ExternalOutput").ap()
    build(nc, **args)
    r = _run(nc, [arrays], core_ids=[0])
    return r.results[0]["out_y"].reshape(1, T, D)
```

```python
from contextlib import ExitStack

import numpy as np

import concourse.bass as bass
from concourse import mybir

F32 = mybir.dt.float32
F32R = mybir.dt.float32r
ACT = mybir.ActivationFunctionType
ALU = mybir.AluOpType
AX_X = mybir.AxisListType.X

P = 128
T = 256
TT = T // P
D = 2048
KT = D // P
FF = 4 * D
HALF = FF // 2
HK = HALF // P
EPS = 1e-6

COLS = 1024
BANK = 512
STEP = 2
NRAW = 4
NSPLIT = 2

HEADS = 8
HD = 128
CHUNK = 64
WINDOWS = (2, 4, 8, 16)
GROUP = 256
PATTERNS = ((128, 1), (512, 4), (2048, 16))
CONV = 4
DW = 31
XHEADS = 4
XHD = D // XHEADS
XDT = XHD // P
QK_TILES = 3 * HEADS
LOG_TERMS = 8
NEG = -1e30


def shape_constants():
    i = np.arange(P)
    same = (i[:, None] // CHUNK) == (i[None, :] // CHUNK)
    ident = np.eye(P)
    tri = same & (i[:, None] <= i[None, :])
    negmask = np.where(tri, 0.0, NEG)
    mats = [ident, tri, same, negmask, np.ones((P, P))]
    b = 1
    while b < CHUNK:
        lower = (i[:, None] // (2 * b) == i[None, :] // (2 * b)) & (i[:, None] // b < i[None, :] // b)
        mats.append(lower if b == 1 else lower.T)
        b *= 2
    squares = np.stack([np.asarray(m, np.float32) for m in mats], 1)

    t = np.arange(T)
    dist = t[:, None] - t[None, :]
    times = sum(((dist >= 0) & (dist <= w) & (dist % r == 0)).astype(np.float64) for w, r in PATTERNS)
    logs = np.where(times > 0, np.log(np.maximum(times, 1.0)), NEG)
    far = np.maximum(dist, 0)
    cut = lambda m: np.concatenate([m[:P, :P], m[P:, :]], 1)
    alibi = np.stack([cut(far), cut(logs)], 1).astype(np.float32)

    pool = np.zeros((len(WINDOWS), T, T))
    for g, w in enumerate(WINDOWS):
        pool[g] = np.where((dist >= 0) & (dist < w), 1.0 / np.minimum(t + 1, w)[:, None], 0.0) - np.eye(T)
    pool_t = pool.transpose(2, 0, 1).reshape(TT, P, len(WINDOWS), T).transpose(1, 2, 0, 3)
    return squares, alibi, np.ascontiguousarray(pool_t, np.float32)


class Own:

    def __init__(self, eng, sem):
        self.eng, self.sem, self.n = eng, sem, 0

    def mark(self, ins):
        self.n += 1
        ins.then_inc(self.sem, 1)

    def wait(self):
        self.eng.wait_ge(self.sem, self.n)


def build(nc, x, mem, vectors, squares, alibi, pool_avg, w_in, pool_w, pool_scale, w_out, w_up, w_down,
          final_g, w_in2, a_log, dt_bias, w_out2, wq, wk, wv, wo, w1, w2, final_g2, out):
    ctx = ExitStack()
    with ctx:
        def sem(name):
            return ctx.enter_context(nc.semaphore(name))

        KB = 1024
        base = (nc.sbuf_base + 63) // 64 * 64
        ctx.enter_context(nc.sbuf_tensor("slab", [P, (207 * KB + 512) // 4], F32))

        def at(name, shape, where, dtype=F32):
            return nc.alloc_sbuf_tensor_at(name, shape, dtype, offset=base + int(where * KB))

        X = at("residual", [P, TT, D], 0)
        HHI = at("stationary_hi", [P, KT, T], 16, F32R)
        HLO = at("stationary_lo", [P, KT, T], 32, F32R)
        RAW = at("weights_raw", [P, NRAW, STEP, COLS], 48)
        WHI = at("weights_hi", [P, NSPLIT, STEP, COLS], 80, F32R)
        WLO = at("weights_lo", [P, NSPLIT, STEP, COLS], 96, F32R)
        SQ = at("squares", [P, 11, P], 112)
        VEC = at("vectors", [P, 4, P], 117.5)
        VEC_RAW = at("vectors_raw", [P, 4, P], 121.5 + 84)
        free_small = [119.5]

        def small(name, shape, dtype=F32):
            t = at(name, shape, free_small[0], dtype)
            free_small[0] += (int(np.prod(shape[1:])) * 4 + 31) // 32 * 32 / KB
            assert free_small[0] <= 121.5
            return t

        A0 = 121.5
        IDENT, TRI, SAME, NEGMASK, ONES = (SQ[:, n, :] for n in range(5))
        LEVELS = 6

        ss = small("ss", [P, 4])
        ms = small("ms", [P, 4])
        rstd = small("rstd", [P, 4])
        halves = small("halves", [P, 32])

        xn = at("normed", [P, TT, D], A0 + 64)
        AHI = at("hidden_hi", [P, HK, T], A0 + 0, F32R)
        ALO = at("hidden_lo", [P, HK, T], A0 + 32, F32R)
        R = at("hidden", [P, TT, COLS], A0 + 64)
        GB = at("final_gain", [P, D], A0 + 72)
        ROWS = at("final_rows", [P, TT, D], A0 + 0)

        PROJ = at("proj", [P, TT, 4 * COLS], A0 + 0)
        QT = at("q_t", [P, HEADS, T], A0 + 32)
        KTT = at("k_t", [P, HEADS, T], A0 + 40)
        POOLW = at("pool_w", [P, len(WINDOWS), 2, GROUP], A0 + 48)
        POOLA = at("pool_avg", [P, len(WINDOWS), TT, T], A0 + 56)
        DT = at("pooled_t", [P, HEADS, T], A0 + 64)
        NS = P + T
        S1 = at("scores", [P, 2, NS], A0 + 72)
        PT1 = at("probs_t", [P, 2, NS], A0 + 76)
        ALIBI = at("alibi", [P, 2, NS], A0 + 80)
        BIAS = at("bias", [P, NS], A0 + 83)
        PSB = at("pool_scale", [P, COLS], 16)
        nmax = small("nmax", [P, 2, 2])
        den = small("den", [P, 2, 2])
        rden = small("rden", [P, 2, 2])

        def slot(n):
            return A0 + 8 * n

        def rows_at(name, n):
            return at(name, [P, TT, COLS], slot(n))[:]

        def units_at(name, n):
            return at(name, [P, U16, P], slot(n))

        U16 = TT * HEADS
        QTOK, KTOK, VTOK, ZTOK = rows_at("q_tok", 0), rows_at("k_tok", 1), rows_at("v_tok", 2), rows_at("z_tok", 9)
        GA, GBT = rows_at("glu_a", 8), rows_at("glu_gate", 5)
        CIN = at("conv_in", [P, HEADS, CONV - 1 + T], slot(3))
        COUT = at("conv_out", [P, HEADS, T], slot(4) + 1)
        SQT = at("squared", [P, TT, HEADS, HD], slot(6))
        MEM_JUNK = at("memory_squares", [P, D], slot(7))
        KB_ = at("k_beta", [P, TT, HEADS, HD], slot(7))
        QT2 = at("q2_t", [P, HEADS, T], slot(6))
        KT2 = at("k2_t", [P, HEADS, T], slot(3))
        KBT = at("k_beta_t", [P, HEADS, T], slot(4))
        DIAG = units_at("gate_diag", 5)
        DEC = units_at("decay", 0)
        LT = units_at("lower_t", 5)
        ATT = units_at("attn_t", 4)
        XI = units_at("inverse", 0)
        XT = units_at("inverse_t", 3)
        WL = units_at("level_product", 7)
        KBG = at("k_beta_decayed", [P, TT, HEADS, HD], slot(0))
        U = at("u", [P, TT, HEADS, HD], slot(5))
        WT = at("w_t", [P, HEADS, T], slot(7))
        ST = at("state", [P, HEADS, HD], slot(10))
        SD = at("state_decayed", [P, HEADS, HD], slot(3))
        O = at("delta_out", [P, TT, HEADS, HD], slot(0))
        OSQ = at("delta_out_squared", [P, TT, HEADS, HD], slot(5))
        MEM = at("memory", [P, TT, D], 0)
        CIN31 = at("conv31_in", [P, HEADS, DW - 1 + T], 0)
        COUT31 = at("conv31_out", [P, HEADS, T], slot(8))
        C = rows_at("conv_rows", 6)
        CS = at("conv_silu", [P, HEADS, T], slot(7))
        CSQ = rows_at("conv_squares", 5)
        NBA = 16
        BARAW = at("w_ba", [P, KT, NBA], slot(10) + 2)
        BAHI = at("w_ba_hi", [P, KT, NBA], slot(10) + 3, F32R)
        BALO = at("w_ba_lo", [P, KT, NBA], slot(10) + 4, F32R)
        ba = small("beta_alpha", [P, TT, NBA])
        beta = small("beta", [P, TT, HEADS])
        adt = small("a_plus_dt", [P, TT, HEADS])
        sp_e = small("softplus_e", [P, TT, HEADS])
        sp_z = small("softplus_z", [P, TT, HEADS])
        sp_q = small("softplus_q", [P, TT, HEADS])
        sp_p = small("softplus_p", [P, TT, HEADS])
        gate = small("gate", [P, TT, HEADS])
        gcs = small("gate_cumsum", [P, TT, HEADS])
        eg = small("exp_gate", [P, TT, HEADS])
        kd = small("exp_to_end", [P, TT, HEADS])
        bke = small("beta_exp_gate", [P, TT, HEADS])
        egl = small("exp_chunk", [P, T // CHUNK, HEADS])
        alog = small("a_log", [P, HEADS])
        dtb = small("dt_bias", [P, HEADS])
        l2 = small("l2", [P, 2, U16])
        l2r = small("l2r", [P, 2, U16])
        osum = small("osum", [P, U16])
        orst = small("orst", [P, U16])
        cmean = small("cmean", [P, TT])

        KV = at("kv", [P, 4, TT, COLS], slot(1))
        V_0, K_0, K_1, V_1 = (KV[:, n] for n in range(4))
        KXT = at("kx_t", [P, KT, T], slot(8))
        XQN = at("normed_x", [P, TT, D], slot(5))
        QX = at("qx", [P, TT, D], slot(5))
        QXT = at("qx_t", [P, KT, T], slot(2))
        PX = at("probs", [P, 2, TT, T], slot(7))
        PXT = at("xprobs_t", [P, 2, TT, T], slot(7) + 4)

        ps = ctx.enter_context(nc.psum_tensor("ps", [P, 8, BANK], F32))

        x_landed = sem("x_landed")
        vec_landed = sem("vec_landed")
        sq_landed = sem("sq_landed")
        alibi_landed = sem("alibi_landed")
        poolw_landed = sem("poolw_landed")
        poola_landed = sem("poola_landed")
        pools_landed = sem("pools_landed")
        ba_landed = sem("ba_landed")
        gates_landed = sem("gates_landed")
        final_landed = sem("final_landed")
        mem_landed = sem("mem_landed")
        raw_landed = [sem(f"raw_landed{n}") for n in range(NRAW)]
        out_landed = sem("out_landed")
        hi_ready = sem("hi_ready")
        lo_ready = sem("lo_ready")
        w_used = sem("w_used")
        out0 = sem("out0")
        out1 = sem("out1")
        vec_turned = sem("vec_turned")
        vec_ready = sem("vec_ready")
        halves_ready = sem("halves_ready")
        sq_done = sem("sq_done")
        rstd_ready = sem("rstd_ready")
        xn_ready = sem("xn_ready")
        turned = sem("turned")
        ht_hi = sem("ht_hi")
        ht_lo = sem("ht_lo")
        relu_done = sem("relu_done")
        r_turned = sem("r_turned")
        at_hi = sem("at_hi")
        at_lo = sem("at_lo")
        x_final = sem("x_final")
        act_own = sem("act_own")
        dve_own = sem("dve_own")
        c31_own = sem("c31_own")
        pool_own = sem("pool_own")
        qk_turned = sem("qk_turned")
        qt_ready = sem("qt_ready")
        kt_ready = sem("kt_ready")
        pooled = sem("pooled")
        pooled_ready = sem("pooled_ready")
        pool_out = sem("pool_out")
        y_pool = sem("y_pool")
        scored = sem("scored")
        max_ready = sem("max_ready")
        probs_ready = sem("probs_ready")
        probs_turned = sem("probs_turned")
        pt_ready = sem("pt_ready")
        attended = sem("attended")
        y_attn = sem("y_attn")
        y_ready = sem("y_ready")
        parked = sem("parked")
        x_back = sem("x_back")
        mem_ready = sem("mem_ready")
        ba_split = sem("ba_split")
        ba_done = sem("ba_done")
        ba_out = sem("ba_out")
        pads_ready = sem("pads_ready")
        conv_turned = sem("conv_turned")
        cin_ready = sem("cin_ready")
        conv_done = sem("conv_done")
        silu_ready = sem("silu_ready")
        conv_back = sem("conv_back")
        sec0 = sem("sec0")
        sec1 = sem("sec1")
        beta_ready = sem("beta_ready")
        adt_ready = sem("adt_ready")
        ea_ready = sem("ea_ready")
        spe_ready = sem("spe_ready")
        gate_ready = sem("gate_ready")
        gate_summed = sem("gate_summed")
        gcs_ready = sem("gcs_ready")
        kd_sub = sem("kd_sub")
        exps_ready = sem("exps_ready")
        l2_sq = sem("l2_sq")
        l2_sum = sem("l2_sum")
        l2_ready = sem("l2_ready")
        qn_ready = sem("qn_ready")
        kn_ready = sem("kn_ready")
        kb_ready = sem("kb_ready")
        v_ready = sem("v_ready")
        kbg_ready = sem("kbg_ready")
        kdec_ready = sem("kdec_ready")
        diag_ready = sem("diag_ready")
        qk2_turned = sem("qk2_turned")
        qk2_ready = sem("qk2_ready")
        rows_ready = sem("rows_ready")
        decsub_ready = sem("decsub_ready")
        decay_ready = sem("decay_ready")
        gram_done = sem("gram_done")
        gram_ready = sem("gram_ready")
        level0_ready = sem("level0_ready")
        level0_turned = sem("level0_turned")
        wl_done = sem("wl_done")
        wl_ready = sem("wl_ready")
        xw_done = sem("xw_done")
        x_up = sem("x_up")
        xt_done = sem("xt_done")
        xt_up = sem("xt_up")
        glu_sig = sem("glu_sig")
        glu_ready = sem("glu_ready")
        pad31_ready = sem("pad31_ready")
        c31_turned = sem("c31_turned")
        c31_in = sem("c31_in")
        c31_done = sem("c31_done")
        c31_back = sem("c31_back")
        c_rows0 = sem("c_rows0")
        c_rows1 = sem("c_rows1")
        u_done = sem("u_done")
        u_ready = sem("u_ready")
        wt_done = sem("wt_done")
        wt_ready = sem("wt_ready")
        state_ready = sem("state_ready")
        sd_ready = sem("sd_ready")
        ws_done = sem("ws_done")
        vn_ready = sem("vn_ready")
        qs_ready = sem("qs_ready")
        vn_used = sem("vn_used")
        o_ready = sem("o_ready")
        osq_ready = sem("osq_ready")
        osum_ready = sem("osum_ready")
        orst_ready = sem("orst_ready")
        o_final = sem("o_final")
        csum = sem("csum")
        c_final = sem("c_final")
        cs_ready = sem("cs_ready")
        kx_turned = sem("kx_turned")
        kx_ready = sem("kx_ready")
        xscored = sem("xscored")
        xmax = sem("xmax")
        xprobs = sem("xprobs")
        xturned = sem("xturned")
        xpt = sem("xpt")
        xatt = sem("xatt")
        xout = sem("xout")

        PS = D // (STEP * P)
        S_IN, P_IN = 0, 0
        S_OUT, P_OUT = S_IN + 4 * PS, P_IN + 4
        S_MLP, P_MLP = S_OUT + 2 * PS, P_OUT + 2
        HALF_STEPS = 4 * PS + 2 * (HK // STEP)
        HALF_PASSES = 6
        S_IN2, P_IN2 = S_MLP + 2 * HALF_STEPS, P_MLP + 2 * HALF_PASSES
        S_KV, P_KV = S_IN2 + 6 * PS, P_IN2 + 6
        S_OUT2, P_OUT2 = S_KV + 4 * PS, P_KV + 4
        S_Q, P_Q = S_OUT2 + 2 * PS, P_OUT2 + 2
        S_O, P_O = S_Q + 2 * PS, P_Q + 2
        S_MLP2, P_MLP2 = S_O + 2 * PS, P_O + 2
        GROUPS = [0, 1] * ((P_IN2 + 4) // 2) + [0, 0] + [0, 0, 1, 0] + [1, 0] + [0, 1] * 2 + [0, 1] * HALF_PASSES
        C31_WK0 = 3
        C31_WK1 = C31_WK0 + 3 * (T // CHUNK)

        def level_part(k, j):
            n = 2 * (k - 1) + j
            return (1 + n // 3, n % 3) if n < 3 * (LEVELS - 2) else (LEVELS - 1, (0, 2)[n - 3 * (LEVELS - 2)])

        GLU0 = 4 * COLS + NBA
        IN2_COLS = [0, COLS, 2 * COLS, 3 * COLS, GLU0, GLU0 + COLS]
        (H_IN, H_OUT, H_MLP, H_IN2, H_MEM, H_OUT2, H_XQ, H_XO, H_MLP2) = range(9)
        (N_IN, N_MIX, N_MLP, N_F1, N_IN2, N_MEM, N_LN, N_XQ, N_MLP2, N_F2) = range(10)
        G_IN, G_OUT, G_MLP, G_IN2, G_XQ, G_MEM, G_MLP2, G_DN = 0, 16, 32, 48, 64, 80, 96, 112

        def gain(k):
            return VEC[:, 0, k:k + 1]

        def tap(j, c):
            return VEC[:, 1, j * QK_TILES + c:j * QK_TILES + c + 1]

        def dw_vec(n, c):
            k = CONV * QK_TILES + n * HEADS + c
            return VEC[:, 1, k:k + 1]

        def dw_tap(j, c):
            k = j * HEADS + c
            return VEC[:, 2 + k // 124, k % 124:k % 124 + 1]

        def blocks(w):
            return w.rearrange("(s j p) n -> s p j n", j=STEP, p=P)

        block = ctx.enter_context(nc.Block())

        @block.sync
        def _(sp):
            sp.dma_start(X[:], x.rearrange("(t p) d -> p t d", p=P)).then_inc(x_landed, 16)
            sp.dma_start(VEC_RAW[:], vectors.rearrange("n r c -> r n c")).then_inc(vec_landed, 16)
            sp.dma_start(SQ[:], squares).then_inc(sq_landed, 16)

            def load(s, src, off=0):
                if s >= NRAW:
                    sp.wait_ge(hi_ready, s + off - NRAW + 1)
                    sp.wait_ge(lo_ready, s + off - NRAW + 1)
                sp.dma_start(RAW[:, s % NRAW], src).then_inc(raw_landed[s % NRAW], 16)

            def load_pass(s0, w, c0):
                for k in range(PS):
                    load(s0 + k, blocks(w)[k, :, :, c0:c0 + COLS])

            def load_mlp(s0, up, down):
                with sp.Fori(0, 2) as half:
                    off = half * HALF_STEPS
                    for p in range(4):
                        for k in range(PS):
                            load(s0 + p * PS + k, blocks(up)[k, :, :, bass.ds(half * HALF + p * COLS, COLS)], off)
                    rows = down.rearrange("(h s j p) n -> h s p j n", h=2, j=STEP, p=P)
                    for d in range(2):
                        for k in range(HK // STEP):
                            load(s0 + 4 * PS + d * (HK // STEP) + k,
                                 rows[bass.ds(half, 1), k, :, :, d * COLS:(d + 1) * COLS].rearrange("h p j n -> (h p) j n"), off)

            for n in range(4):
                load_pass(S_IN + n * PS, w_in, n * COLS)
            for n in range(2):
                load_pass(S_OUT + n * PS, w_out, n * COLS)
            load_mlp(S_MLP, w_up, w_down)
            for n in range(6):
                load_pass(S_IN2 + n * PS, w_in2, IN2_COLS[n])
            for n in range(4):
                load_pass(S_KV + n * PS, wk if n < 2 else wv, (n % 2) * COLS)
            for n in range(2):
                load_pass(S_OUT2 + n * PS, w_out2, n * COLS)
            for n in range(2):
                load_pass(S_Q + n * PS, wq, n * COLS)
            for n in range(2):
                load_pass(S_O + n * PS, wo, n * COLS)
            load_mlp(S_MLP2, w1, w2)
            for t in range(TT):
                sp.wait_ge(x_final, t + 1 + TT)
                sp.dma_start(out[t * P:(t + 1) * P, :], ROWS[:, t, :]).then_inc(out_landed, 16)
            sp.wait_ge(out_landed, 16 * TT)

        @block.gpsimd
        def _(pool):
            own = Own(pool, pool_own)
            pool.memset(halves[:], -0.5).then_inc(halves_ready, 1)
            pool.dma_start(ALIBI[:], alibi).then_inc(alibi_landed, 16)
            pool.dma_start(POOLW[:], pool_w.rearrange("g (c p) f -> p g c f", p=P)).then_inc(poolw_landed, 16)
            pool.dma_start(POOLA[:], pool_avg).then_inc(poola_landed, 16)
            pool.dma_start(alog[:], a_log.partition_broadcast(P)).then_inc(gates_landed, 16)
            pool.dma_start(dtb[:], dt_bias.partition_broadcast(P)).then_inc(gates_landed, 16)

            def root(n_sq, n_norm, cols, width):
                pool.wait_ge(sq_done, n_sq)
                own.mark(pool.tensor_scalar(ms[:, 0:cols], ss[:, 0:cols], 1.0 / width, EPS, ALU.mult, ALU.add))
                own.wait()
                pool.wait_ge(halves_ready, 1)
                pool.tensor_tensor(rstd[:, 0:cols], ms[:, 0:cols], halves[:, 0:cols], ALU.pow).then_inc(rstd_ready, 1)

            root(2, N_IN, 2, D)
            pool.wait_ge(w_used, S_OUT)
            pool.dma_start(PSB[:], pool_scale.partition_broadcast(P)).then_inc(pools_landed, 16)
            root(6, N_MIX, 4, COLS)
            pool.dma_start(BARAW[:], w_in2[:, 4 * COLS:4 * COLS + NBA].rearrange("(k p) n -> p k n", p=P)).then_inc(ba_landed, 16)
            root(8, N_MLP, 2, D)
            pool.wait_ge(turned, KT // 2 * (H_MLP + 1))
            pool.dma_start(GB[:], final_g.partition_broadcast(P)).then_inc(final_landed, 16)
            root(10, N_F1, 2, D)
            root(12, N_IN2, 2, D)
            pool.wait_ge(x_final, TT)
            pool.dma_start(out.rearrange("(t p) d -> p t d", p=P), X[:]).then_inc(parked, 16)
            pool.wait_ge(xn_ready, 6)
            pool.memset(CIN[:, :, 0:CONV - 1], 0.0).then_inc(pads_ready, 1)
            pool.wait_ge(parked, 16)
            pool.dma_start(MEM[:], mem.rearrange("(t p) d -> p t d", p=P)).then_inc(mem_landed, 16)
            root(14, N_MEM, 2, D)
            pool.wait_ge(l2_sum, 2)
            own.mark(pool.tensor_scalar(l2[:], l2[:], EPS, None, ALU.add))
            own.wait()
            for n in range(2):
                own.mark(pool.tensor_tensor(l2r[:, n, :], l2[:, n, :], halves[:, 0:U16], ALU.pow))
            own.wait()
            pool.tensor_scalar(l2r[:, 0, :], l2r[:, 0, :], float(HD) ** -0.5, None, ALU.mult).then_inc(l2_ready, 1)
            pool.wait_ge(ba_done, 1)
            pool.memset(ST[:], 0.0).then_inc(state_ready, 1)
            pool.wait_ge(turned, KT // 2 * (H_MEM + 1))
            pool.memset(CIN31[:, :, 0:DW - 1], 0.0).then_inc(pad31_ready, 1)
            pool.wait_ge(wt_done, 1)
            pool.wait_ge(exps_ready, 1)
            for n in range(T // CHUNK - 1):
                pool.wait_ge(state_ready, n + 1)
                pool.tensor_tensor(SD[:], ST[:], egl[:, n, :].unsqueeze(2).broadcast_to([P, HEADS, HD]), ALU.mult).then_inc(sd_ready, 1)
            pool.wait_ge(osum_ready, 1)
            own.mark(pool.tensor_scalar(osum[:], osum[:], 1.0 / HD, EPS, ALU.mult, ALU.add))
            own.wait()
            pool.tensor_tensor(orst[:], osum[:], halves[:, 0:U16], ALU.pow).then_inc(orst_ready, 1)
            pool.wait_ge(c31_done, 1)
            pool.dma_start(X[:], out.rearrange("(t p) d -> p t d", p=P)).then_inc(x_back, 16)
            root(16, N_LN, 2, COLS)
            root(18, N_XQ, 2, D)
            root(20, N_MLP2, 2, D)
            pool.wait_ge(turned, KT // 2 * (H_MLP2 + 1))
            pool.dma_start(GB[:], final_g2.partition_broadcast(P)).then_inc(final_landed, 16)
            root(22, N_F2, 2, D)

        @block.tensor
        def _(pe):
            def vec_turn():
                pe.wait_ge(vec_landed, 16)
                pe.wait_ge(sq_landed, 16)
                for n in range(4):
                    last = pe.transpose(ps[:, 0, n * P:(n + 1) * P], VEC_RAW[:, n, :], IDENT)
                last.then_inc(vec_turned, 1)

            def turn8(src, half, group):
                for k in range(KT // 2 * half, KT // 2 * (half + 1)):
                    for t in range(TT):
                        b = 4 * group + (k % (KT // 2)) // 2
                        last = pe.transpose(ps[:, b, (k % 2) * T + t * P:(k % 2) * T + (t + 1) * P], src(k, t), IDENT)
                    if k % 2:
                        last.then_inc(turned, 1)

            def stationary(h, k=KT):
                pe.wait_ge(ht_hi, KT * h + k)
                pe.wait_ge(ht_lo, KT * h + k)

            def step(s, hi, lo, k, group, first, last, off=0, between=None):
                pe.wait_ge(hi_ready, s + off + 1)
                pe.wait_ge(lo_ready, s + off + 1)
                slot = s % NSPLIT
                for j in range(STEP):
                    if j and between:
                        between()
                    for t in range(TT):
                        xh = hi[:, k + j, t * P:(t + 1) * P]
                        xl = lo[:, k + j, t * P:(t + 1) * P]
                        for c in range(2):
                            o = ps[:, 4 * group + 2 * t + c, :]
                            pe.matmul(o, xh, WHI[:, slot, j, c * BANK:(c + 1) * BANK], start=first and j == 0, stop=False)
                            pe.matmul(o, xh, WLO[:, slot, j, c * BANK:(c + 1) * BANK], start=False, stop=False)
                        for c in range(2):
                            o = ps[:, 4 * group + 2 * t + c, :]
                            mm = pe.matmul(o, xl, WHI[:, slot, j, c * BANK:(c + 1) * BANK], start=False, stop=last and j == STEP - 1)
                mm.then_inc(w_used, 1)

            def bank_free(p, off=0):
                if p >= 2:
                    pe.wait_ge(out0, p + off - 1)
                    pe.wait_ge(out1, p + off - 1)

            def gemm_pass(s0, p, during=None, h=None, turn_second=None):
                before = [n for n in range(p) if GROUPS[n] == GROUPS[p]]
                if before:
                    pe.wait_ge(out0, before[-1] + 1)
                    pe.wait_ge(out1, before[-1] + 1)
                for k in range(PS):
                    if turn_second and k == 2:
                        pe.wait_ge(ht_lo, KT * h + KT // 2)
                        turn8(turn_second, 1, 1 - GROUPS[p])
                    if during:
                        during(k, 0)
                    if h is not None:
                        stationary(h, STEP * (k + 1))
                    step(s0 + k, HHI, HLO, STEP * k, GROUPS[p], k == 0, k == PS - 1,
                         between=(lambda k=k: during(k, 1)) if during else None)

            def first_pass(s0, p, h, src, during=None):
                turn8(src, 0, 1 - GROUPS[p])
                gemm_pass(s0, p, during, h, src)

            def mlp(m, s0, p0, h):
                stationary(h)
                with pe.Fori(0, 2) as half:
                    off, poff, aoff = half * HALF_STEPS, half * HALF_PASSES, half * 16

                    def turn_hidden(p):
                        pe.wait_ge(out0, p0 + p + 1 + poff)
                        pe.wait_ge(out1, p0 + p + 1 + poff)
                        g = 4 * (p % 2)
                        for b in range(4):
                            for k in range(2 * b, 2 * b + 2):
                                for t in range(TT):
                                    last = pe.transpose(ps[:, g + b, (k % 2) * T + t * P:(k % 2) * T + (t + 1) * P],
                                                        R[:, t, k * P:(k + 1) * P], IDENT)
                            last.then_inc(r_turned, 1)

                    for p in range(4):
                        bank_free(p0 + p, poff)
                        if p >= 2:
                            pe.wait_ge(at_hi, 32 * m + 4 * (p - 1) + aoff)
                            pe.wait_ge(at_lo, 32 * m + 4 * (p - 1) + aoff)
                        for k in range(PS):
                            if p >= 1 and k == 2:
                                turn_hidden(p - 1)
                            step(s0 + p * PS + k, HHI, HLO, STEP * k, p % 2, k == 0, k == PS - 1, off)
                    for d in range(2):
                        n = HK // STEP
                        bank_free(p0 + 4 + d, poff)
                        pe.wait_ge(at_hi, 32 * m + 12 + 4 * d + aoff)
                        pe.wait_ge(at_lo, 32 * m + 12 + 4 * d + aoff)
                        for k in range(n):
                            if d == 0 and k == 2:
                                turn_hidden(3)
                            if d == 0 and k == 12:
                                pe.wait_ge(at_hi, 32 * m + 16 + aoff)
                                pe.wait_ge(at_lo, 32 * m + 16 + aoff)
                            step(s0 + 4 * PS + d * n + k, AHI, ALO, STEP * k, d, k == 0, k == n - 1, off)

            vec_turn()
            pe.wait_ge(vec_ready, 1)
            pe.wait_ge(xn_ready, 2)
            first_pass(S_IN, P_IN, H_IN, lambda k, t: xn[:, t, k * P:(k + 1) * P])
            for n in range(1, 4):
                gemm_pass(S_IN + n * PS, P_IN + n)
            pe.wait_ge(out0, P_IN + 4)
            pe.wait_ge(out1, P_IN + 4)
            for n in range(2):
                for h in range(HEADS):
                    for t in range(TT):
                        c = (1 + n) * COLS + h * HD
                        last = pe.transpose(ps[:, 4 * n + h // 2, (h % 2) * T + t * P:(h % 2) * T + (t + 1) * P],
                                            PROJ[:, t, c:c + HD], IDENT)
                last.then_inc(qk_turned, 1)
            pe.wait_ge(poola_landed, 16)
            pe.wait_ge(qt_ready, 1)
            for n in range(2 * len(WINDOWS)):
                for t in range(TT):
                    last = pe.matmul(ps[:, n // 2, (n % 2) * T:(n % 2 + 1) * T], PROJ[:, t, n * P:(n + 1) * P],
                                     POOLA[:, n // 2, t, :], start=t == 0, stop=t == TT - 1)
            last.then_inc(pooled, 1)
            pe.wait_ge(pooled_ready, 1)
            pe.wait_ge(poolw_landed, 16)
            pe.wait_ge(kt_ready, 1)
            for t in range(TT):
                for g in range(len(WINDOWS)):
                    for c in range(2):
                        last = pe.matmul(ps[:, 4 + 2 * t + g // 2, (g % 2) * GROUP:(g % 2 + 1) * GROUP],
                                         DT[:, 2 * g + c, t * P:(t + 1) * P], POOLW[:, g, c, :], start=c == 0, stop=c == 1)
            last.then_inc(pool_out, 1)

            def scores(h):
                if h >= 2:
                    pe.wait_ge(max_ready, h - 1)
                pe.matmul(ps[:, h % 2, 0:P], QT[:, h, 0:P], KTT[:, h, 0:P], start=True, stop=True)
                pe.matmul(ps[:, h % 2, P:P + T], QT[:, h, P:T], KTT[:, h, :], start=True, stop=True).then_inc(scored, 1)

            def attend(h):
                s = h % 2
                pe.wait_ge(probs_ready, h + 1)
                if h >= 2:
                    pe.wait_ge(pt_ready, h - 1)
                pe.transpose(ps[:, 2 + s, 0:P], S1[:, s, 0:P], IDENT)
                pe.transpose(ps[:, 2 + s, P:T], S1[:, s, P:T], IDENT)
                pe.transpose(ps[:, 2 + s, T:NS], S1[:, s, T:NS], IDENT).then_inc(probs_turned, 1)
                pe.wait_ge(pt_ready, h + 1)
                if h >= 2:
                    pe.wait_ge(y_attn, h - 1)
                v = [PROJ[:, t, 3 * COLS + h * HD:3 * COLS + (h + 1) * HD] for t in range(TT)]
                pe.matmul(ps[:, 4 + s, 0:P], PT1[:, s, 0:P], v[0], start=True, stop=True)
                pe.matmul(ps[:, 4 + s, P:T], PT1[:, s, P:T], v[0], start=True, stop=False)
                pe.matmul(ps[:, 4 + s, P:T], PT1[:, s, T:NS], v[1], start=False, stop=True).then_inc(attended, 1)

            pe.wait_ge(y_pool, 1)
            scores(0)
            for h in range(HEADS):
                if h + 1 < HEADS:
                    scores(h + 1)
                attend(h)
            pe.wait_ge(y_ready, 1)
            first_pass(S_OUT, P_OUT, H_OUT, lambda k, t: PROJ[:, t, k * P:(k + 1) * P])
            gemm_pass(S_OUT + PS, P_OUT + 1)
            pe.wait_ge(xn_ready, 4)
            for half in range(2):
                turn8(lambda k, t: xn[:, t, k * P:(k + 1) * P], half, half)
            mlp(0, S_MLP, P_MLP, H_MLP)

            pe.wait_ge(xn_ready, 6)
            other = ps[:, 4:8, :].rearrange("p b n -> p (b n)")

            def turn_rows(src, group, done, n=HEADS):
                for c in range(n):
                    for t in range(TT):
                        last = pe.transpose(ps[:, 4 * group + c // 2, (c % 2) * T + t * P:(c % 2) * T + (t + 1) * P], src(c, t), IDENT)
                last.then_inc(done, 1)

            def turn_back(src, group, done):
                for t in range(TT):
                    for c in range(HEADS):
                        last = pe.transpose(ps[:, 4 * group + 2 * t + c // 4, (c % 4) * P:(c % 4 + 1) * P], src[:, c, t * P:(t + 1) * P], IDENT)
                last.then_inc(done, 1)

            def units(lhs, rhs):
                for u in range(U16):
                    last = pe.matmul(ps[:, 4 + u // 4, (u % 4) * P:(u % 4 + 1) * P], lhs[:, u, :], rhs[:, u, :], start=True, stop=True)
                return last

            def left(p):
                pe.wait_ge(out0, p + 1)
                pe.wait_ge(out1, p + 1)

            def during_q(k, j):
                if (k, j) == (PS - 1, 0):
                    pe.wait_ge(ba_split, 2)
                    for t in range(TT):
                        for f in range(KT):
                            xh, xl = HHI[:, f, t * P:(t + 1) * P], HLO[:, f, t * P:(t + 1) * P]
                            o = ps[:, 4 + 2 * t, 0:NBA]
                            pe.matmul(o, xh, BAHI[:, f, :], start=f == 0, stop=False)
                            pe.matmul(o, xh, BALO[:, f, :], start=False, stop=False)
                            last = pe.matmul(o, xl, BAHI[:, f, :], start=False, stop=f == KT - 1)
                    last.then_inc(ba_done, 1)

            def during_k(k, j):
                if (k, j) == (2, 0):
                    left(P_IN2)
                    turn_rows(lambda c, t: QTOK[:, t, c * P:(c + 1) * P], 0, conv_turned)
                elif (k, j) == (5, 0):
                    pe.wait_ge(cin_ready, 1)
                    pe.wait_ge(gate_ready, 1)
                    G16 = gate[:].rearrange("p t h -> p (t h)")
                    pe.matmul(ps[:, 0, 0:U16], TRI, G16, start=True, stop=True)
                    pe.matmul(ps[:, 0, 16:16 + U16], SAME, G16, start=True, stop=True)
                    for n in range(T // CHUNK):
                        r = CHUNK * (n % 2)
                        last = pe.matmul(ps[:, n % 2, 32 + n // 2 * HEADS:32 + (n // 2 + 1) * HEADS], ONES[r:r + CHUNK, :],
                                         gate[r:r + CHUNK, n // 2, :], start=True, stop=True)
                    last.then_inc(gate_summed, 1)

            def during_v(k, j):
                if (k, j) == (1, 0):
                    left(P_IN2 + 1)
                    pe.wait_ge(silu_ready, 1)
                    turn_back(COUT, 1, conv_back)
                elif (k, j) == (2, 0):
                    pe.wait_ge(sec0, 1)
                    pe.wait_ge(sec1, 1)
                    turn_rows(lambda c, t: KTOK[:, t, c * P:(c + 1) * P], 1, conv_turned)

            def during_z(k, j):
                if (k, j) == (1, 0):
                    left(P_IN2 + 2)
                    pe.wait_ge(silu_ready, 2)
                    turn_back(COUT, 0, conv_back)
                elif (k, j) == (2, 0):
                    pe.wait_ge(sec0, 2)
                    pe.wait_ge(sec1, 2)
                    turn_rows(lambda c, t: VTOK[:, t, c * P:(c + 1) * P], 0, conv_turned)

            def during_ga(k, j):
                if j:
                    return
                if k == 1:
                    left(P_IN2 + 3)
                    pe.wait_ge(silu_ready, 3)
                    turn_back(COUT, 1, conv_back)
                elif k == 2:
                    pe.wait_ge(sec0, 3)
                    pe.wait_ge(sec1, 3)
                    pe.wait_ge(qn_ready, 1)
                    turn_rows(lambda h, t: QTOK[:, t, h * HD:(h + 1) * HD], 1, qk2_turned)
                elif k == 3:
                    pe.wait_ge(qk2_ready, 1)
                    pe.wait_ge(kn_ready, 1)
                    turn_rows(lambda h, t: KTOK[:, t, h * HD:(h + 1) * HD], 1, qk2_turned)
                elif k == 4:
                    pe.wait_ge(qk2_ready, 2)
                    pe.wait_ge(kb_ready, 1)
                    turn_rows(lambda h, t: KB_[:, t, h, :], 1, qk2_turned)
                elif k == 5:
                    pe.wait_ge(qk2_ready, 3)
                    pe.wait_ge(diag_ready, 1)
                    for b in range(4):
                        last = pe.matmul(ps[:, 4 + b, :], ONES, DIAG[:, 4 * b:4 * b + 4, :].rearrange("p u c -> p (u c)"), start=True, stop=True)
                    last.then_inc(rows_ready, 1)
                elif k in (6, 7):
                    if k == 6:
                        pe.wait_ge(decsub_ready, 1)
                    else:
                        pe.wait_ge(gram_ready, 1)
                    with_ = KBT if k == 6 else QT2
                    for u in range(U16):
                        t, h = u // HEADS, u % HEADS
                        last = pe.matmul(ps[:, 4 + u // 4, (u % 4) * P:(u % 4 + 1) * P],
                                         KT2[:, h, t * P:(t + 1) * P], with_[:, h, t * P:(t + 1) * P], start=True, stop=True)
                    last.then_inc(gram_done, 1)

            def during_gb(k, j):
                if (k, j) == (0, 1):
                    pe.wait_ge(gram_ready, 2)
                    pe.wait_ge(level0_ready, 1)
                    for u in range(U16):
                        last = pe.transpose(ps[:, 4 + u // 4, (u % 4) * P:(u % 4 + 1) * P], WL[:, u, :], IDENT)
                    last.then_inc(level0_turned, 1)
                elif k >= 1:
                    lv, part = level_part(k, j)
                    if part == 0:
                        pe.wait_ge(x_up, lv)
                        pe.wait_ge(xt_up, lv)
                        units(LT, XI).then_inc(wl_done, 1)
                    elif part == 1:
                        pe.wait_ge(wl_ready, lv)
                        units(XT, WL).then_inc(xw_done, 1)
                    else:
                        pe.wait_ge(wl_ready, lv)
                        if lv < LEVELS - 1:
                            pe.wait_ge(x_up, lv + 1)
                        units(WL, XT).then_inc(xt_done, 1)

            def during_wk0(k, j):
                if j:
                    return
                if k == 4:
                    pe.wait_ge(ht_lo, KT * (H_MEM + 1))
                    pe.wait_ge(glu_ready, 1)
                    turn_rows(lambda c, t: GA[:, t, c * P:(c + 1) * P], 1, c31_turned)
                elif k == 5:
                    pe.wait_ge(c31_in, 1)
                    pe.wait_ge(v_ready, 1)
                    for u in range(U16):
                        t, h = u // HEADS, u % HEADS
                        last = pe.matmul(ps[:, 4 + u // 4, (u % 4) * P:(u % 4 + 1) * P], XT[:, u, :], VTOK[:, t, h * HD:(h + 1) * HD], start=True, stop=True)
                    last.then_inc(u_done, 1)
                elif k == 6:
                    pe.wait_ge(u_ready, 1)
                    pe.wait_ge(kbg_ready, 1)
                    for h in range(HEADS):
                        for t in range(TT):
                            last = pe.matmul(ps[:, 4 + h // 2, (h % 2) * T + t * P:(h % 2) * T + (t + 1) * P],
                                             KBG[:, t, h, :], XT[:, t * HEADS + h, :], start=True, stop=True)
                    last.then_inc(wt_done, 1)

            def during_wk1(k, j):
                if j:
                    return
                n = k // 2
                t, r = n // 2, CHUNK * (n % 2)
                rows = slice(r, r + CHUNK)
                if k % 2 == 0:
                    if n == 0:
                        pe.wait_ge(wt_ready, 1)
                    else:
                        pe.wait_ge(o_ready, n)
                    pe.wait_ge(state_ready, n + 1)
                    for h in range(HEADS):
                        pe.matmul(ps[rows, 4 + h // 4, (h % 4) * P:(h % 4 + 1) * P], WT[:, h, t * P + r:t * P + r + CHUNK], ST[:, h, :], start=True, stop=True)
                    for h in range(HEADS):
                        last = pe.matmul(ps[rows, 6 + h // 4, (h % 4) * P:(h % 4 + 1) * P], QT2[:, h, t * P + r:t * P + r + CHUNK], ST[:, h, :], start=True, stop=True)
                    last.then_inc(ws_done, 1)
                else:
                    pe.wait_ge(kdec_ready, 1)
                    pe.wait_ge(vn_ready, n + 1)
                    pe.wait_ge(qs_ready, n + 1)
                    for h in range(HEADS):
                        pe.matmul(ps[:, 4 + h // 4, (h % 4) * P:(h % 4 + 1) * P], KTOK[rows, t, h * HD:(h + 1) * HD], U[rows, t, h, :], start=True, stop=True)
                    for h in range(HEADS):
                        last = pe.matmul(ps[rows, 6 + h // 4, (h % 4) * P:(h % 4 + 1) * P], ATT[rows, t * HEADS + h, r:r + CHUNK], U[rows, t, h, :], start=True, stop=True)
                    last.then_inc(vn_used, 1)

            def during_wv1(k, j):
                if (k, j) == (6, 0):
                    left(P_KV + 2)
                    pe.wait_ge(o_final, 1)
                    turn8(lambda k, t: O[:, t, k, :], 0, 1)

            def during_out0(k, j):
                if (k, j) == (1, 0):
                    left(P_KV + 3)
                    pe.wait_ge(c31_done, 1)
                    turn_back(COUT31, 0, c31_back)
                elif (k, j) == (4, 0):
                    pe.wait_ge(c_final, 1)
                    turn8(lambda k, t: C[:, t, (k - HEADS) * P:(k - HEADS + 1) * P], 1, 0)

            def during_out1(k, j):
                if (k, j) == (2, 0):
                    left(P_OUT2)
                    turn_rows(lambda c, t: K_0[:, t, c * P:(c + 1) * P], 1, kx_turned)
                elif (k, j) == (4, 0):
                    pe.wait_ge(kx_ready, 1)
                    turn_rows(lambda c, t: K_1[:, t, c * P:(c + 1) * P], 1, kx_turned)

            first_pass(S_IN2, P_IN2, H_IN2, lambda k, t: xn[:, t, k * P:(k + 1) * P], during_q)
            pe.wait_ge(ba_out, 1)
            gemm_pass(S_IN2 + PS, P_IN2 + 1, during_k)
            pe.wait_ge(gcs_ready, 1)
            pe.wait_ge(kd_sub, 1)
            gemm_pass(S_IN2 + 2 * PS, P_IN2 + 2, during_v)
            pe.wait_ge(cin_ready, 2)
            gemm_pass(S_IN2 + 3 * PS, P_IN2 + 3, during_z)
            pe.wait_ge(cin_ready, 3)
            gemm_pass(S_IN2 + 4 * PS, P_IN2 + 4, during_ga)
            gemm_pass(S_IN2 + 5 * PS, P_IN2 + 5, during_gb)
            pe.wait_ge(xt_up, LEVELS)
            pe.wait_ge(mem_ready, 2)
            first_pass(S_KV, P_KV, H_MEM, lambda k, t: MEM[:, t, k * P:(k + 1) * P], during_wk0)
            gemm_pass(S_KV + PS, P_KV + 1, during_wk1)
            pe.wait_ge(o_ready, T // CHUNK)
            gemm_pass(S_KV + 2 * PS, P_KV + 2)
            gemm_pass(S_KV + 3 * PS, P_KV + 3, during_wv1)
            pe.wait_ge(ht_lo, KT * H_OUT2 + KT // 2)
            gemm_pass(S_OUT2, P_OUT2, during_out0, H_OUT2)
            gemm_pass(S_OUT2 + PS, P_OUT2 + 1, during_out1)

            pe.wait_ge(kx_ready, 2)
            pe.wait_ge(xn_ready, 8)
            first_pass(S_Q, P_Q, H_XQ, lambda k, t: XQN[:, t, k * P:(k + 1) * P])
            gemm_pass(S_Q + PS, P_Q + 1)
            left(P_Q + 1)
            for n in range(2):
                turn_rows(lambda k, t: QX[:, t, n * COLS + k * P:n * COLS + (k + 1) * P], n, kx_turned)
            pe.wait_ge(kx_ready, 4)

            def xscores(h):
                if h >= 2:
                    pe.wait_ge(xprobs, h - 1)
                for q in range(TT):
                    for d in range(XDT):
                        last = pe.matmul(ps[:, h % 2, q * T:(q + 1) * T], QXT[:, XDT * h + d, q * P:(q + 1) * P],
                                         KXT[:, XDT * h + d, :], start=d == 0, stop=d == XDT - 1)
                last.then_inc(xscored, 1)

            def xattend(h):
                s = h % 2
                pe.wait_ge(xprobs, h + 1)
                if h >= 2:
                    pe.wait_ge(xpt, h - 1)
                for k in range(TT):
                    for q in range(TT):
                        last = pe.transpose(ps[:, 2 + s, k * T + q * P:k * T + (q + 1) * P], PX[:, s, q, k * P:(k + 1) * P], IDENT)
                last.then_inc(xturned, 1)
                pe.wait_ge(xpt, h + 1)
                if h >= 2:
                    pe.wait_ge(xout, h - 1)
                for q in range(TT):
                    for k in range(TT):
                        last = pe.matmul(ps[:, 4 + 2 * s + q, :], PXT[:, s, k, q * P:(q + 1) * P],
                                         (V_0, V_1)[h // 2][:, k, (h % 2) * XHD:(h % 2 + 1) * XHD], start=k == 0, stop=k == TT - 1)
                last.then_inc(xatt, 1)

            xscores(0)
            for h in range(XHEADS):
                if h + 1 < XHEADS:
                    xscores(h + 1)
                xattend(h)
            pe.wait_ge(xout, XHEADS)
            first_pass(S_O, P_O, H_XO, lambda k, t: QX[:, t, k * P:(k + 1) * P])
            gemm_pass(S_O + PS, P_O + 1)
            pe.wait_ge(xn_ready, 10)
            for half in range(2):
                turn8(lambda k, t: xn[:, t, k * P:(k + 1) * P], half, half)
            mlp(1, S_MLP2, P_MLP2, H_MLP2)

        @block.scalar
        def _(act):
            own = Own(act, act_own)

            def split(s, off=0):
                act.wait_ge(raw_landed[s % NRAW], 16 * (s // NRAW + 1) + off * (16 // NRAW))
                if s >= NSPLIT:
                    act.wait_ge(w_used, s + off - NSPLIT + 1)
                act.activation(WHI[:, s % NSPLIT], RAW[:, s % NRAW], ACT.Copy).then_inc(hi_ready, 1)

            def squares_of(src, dst, junk=xn):
                for t in range(TT):
                    act.activation(junk[:, t, :], src[:, t, :], ACT.Square, accum_out=dst[:, t:t + 1]).then_inc(sq_done, 1)

            def split_turned(h, g, half, group):
                for k in range(KT // 2 * half, KT // 2 * (half + 1)):
                    act.wait_ge(turned, KT // 2 * h + k // 2 + 1)
                    v = ps[:, 4 * group + (k % 8) // 2, (k % 2) * T:(k % 2 + 1) * T]
                    if g is None:
                        act.activation(HHI[:, k, :], v, ACT.Copy).then_inc(ht_hi, 1)
                    else:
                        act.activation(HHI[:, k, :], v, ACT.Copy, scale=gain(g(k))).then_inc(ht_hi, 1)

            def left(s_end, p, t, dst, func=ACT.Copy):
                act.wait_ge(w_used, s_end)
                g = 4 * GROUPS[p] + 2 * t
                act.activation(dst, ps[:, g:g + 2, :].rearrange("p b n -> p (b n)"), func).then_inc((out0, out1)[t], 1)

            def passes(s0, p0, dsts, h=None, g=None):
                for n, dst in enumerate(dsts):
                    for k in range(PS):
                        split(s0 + n * PS + k)
                        if k == 0 and n > 0 and dsts[n - 1] is not None:
                            left(s0 + n * PS, p0 + n - 1, 0, dsts[n - 1])
                        if k == 1 and n == 0:
                            for half in range(2):
                                split_turned(h, g, half, 1 - GROUPS[p0])
                if dsts[-1] is not None:
                    left(s0 + len(dsts) * PS, p0 + len(dsts) - 1, 0, dsts[-1])

            def mlp(m, s0, p0):
                with act.Fori(0, 2) as half:
                    off, roff = half * HALF_STEPS, half * 16

                    def relu(p):
                        act.wait_ge(w_used, s0 + (p + 1) * PS + off)
                        if p >= 1:
                            act.wait_ge(r_turned, 32 * m + 4 * p + roff)
                        g = 4 * (p % 2)
                        for t in range(TT):
                            act.activation(R[:, t, :], ps[:, g + 2 * t:g + 2 * t + 2, :].rearrange("p b n -> p (b n)"), ACT.Relu).then_inc(relu_done, 1)

                    def hidden_hi(p):
                        g = 4 * (p % 2)
                        for b in range(4):
                            act.wait_ge(r_turned, 32 * m + 4 * p + b + 1 + roff)
                            act.activation(AHI[:, 8 * p + 2 * b:8 * p + 2 * b + 2, :].rearrange("p k t -> p (k t)"), ps[:, g + b, :], ACT.Copy).then_inc(at_hi, 1)

                    for p in range(4):
                        for k in range(PS):
                            split(s0 + p * PS + k, off)
                            if p >= 1 and k == 0:
                                relu(p - 1)
                            if p >= 1 and k == 2:
                                hidden_hi(p - 1)
                    n = HK // STEP
                    for k in range(2 * n):
                        split(s0 + 4 * PS + k, off)
                        if k == 0:
                            relu(3)
                        if k == 2:
                            hidden_hi(3)

            act.wait_ge(x_landed, 16)
            squares_of(X, ss)
            act.wait_ge(vec_ready, 1)
            passes(S_IN, P_IN, [PROJ[:, 0, n * COLS:(n + 1) * COLS] for n in range(4)], H_IN, lambda k: G_IN + k)
            act.wait_ge(qk_turned, 1)
            act.activation(QT[:].rearrange("p h t -> p (h t)"), ps[:, 0:4, :].rearrange("p b n -> p (b n)"), ACT.Copy).then_inc(qt_ready, 1)
            act.wait_ge(pooled, 1)
            act.activation(DT[:].rearrange("p h t -> p (h t)"), ps[:, 0:4, :].rearrange("p b n -> p (b n)"), ACT.Copy).then_inc(pooled_ready, 1)
            for h in range(HEADS):
                s = h % 2
                act.wait_ge(max_ready, h + 1)
                act.activation(S1[:, s, 0:P], S1[:, s, 0:P], ACT.Exp, bias=nmax[:, s, 0:1], accum_out=den[:, s, 0:1])
                act.activation(S1[:, s, P:NS], S1[:, s, P:NS], ACT.Exp, bias=nmax[:, s, 1:2], accum_out=den[:, s, 1:2]).then_inc(probs_ready, 1)
                act.wait_ge(probs_turned, h + 1)
                if h >= 2:
                    act.wait_ge(attended, h - 1)
                act.activation(PT1[:, s, :], ps[:, 2 + s, 0:NS], ACT.Copy).then_inc(pt_ready, 1)
            act.wait_ge(y_attn, HEADS)
            for n in range(2):
                for t in range(TT):
                    act.activation((DT, QT)[n][:, 4 * t:4 * t + 4, :].rearrange("p h t -> p (h t)"), PROJ[:, t, n * COLS:(n + 1) * COLS], ACT.Square,
                                   accum_out=ss[:, 2 * n + t:2 * n + t + 1]).then_inc(sq_done, 1)
            passes(S_OUT, P_OUT, [None, None], H_OUT, lambda k: G_OUT + k)
            act.wait_ge(out1, P_OUT + 2)
            squares_of(X, ss)
            for half in range(2):
                split_turned(H_MLP, lambda k: G_MLP + k, half, half)
            mlp(0, S_MLP, P_MLP)
            act.wait_ge(out1, P_MLP + 2 * HALF_PASSES)
            squares_of(X, ss, ROWS)
            act.wait_ge(x_final, 2)
            squares_of(X, ss)
            act.wait_ge(ba_landed, 16)
            act.activation(BAHI[:], BARAW[:], ACT.Copy).then_inc(ba_split, 1)
            flat_low = ps[:, 0:4, :].rearrange("p b n -> p (b n)")
            flat_high = ps[:, 4:8, :].rearrange("p b n -> p (b n)")

            def conv_load(n, group):
                act.wait_ge(conv_turned, n + 1)
                act.wait_ge(pads_ready, 1)
                if n >= 1:
                    act.wait_ge(conv_done, n)
                act.activation(CIN[:, :, CONV - 1:], ps[:, 4 * group:4 * group + 4, :].rearrange("p b (c t) -> p (b c) t", t=T), ACT.Copy).then_inc(cin_ready, 1)

            def conv_silu(n):
                act.wait_ge(conv_done, n + 1)
                act.activation(COUT[:], COUT[:], ACT.Silu).then_inc(silu_ready, 1)

            def conv_store(n, dst, group):
                act.wait_ge(conv_back, n + 1)
                act.activation(dst[:, 0, :], ps[:, 4 * group:4 * group + 2, :].rearrange("p b n -> p (b n)"), ACT.Copy).then_inc(sec0, 1)

            def square_heads(n, src):
                act.wait_ge(sec0, n + 1)
                act.wait_ge(sec1, n + 1)
                if n >= 1:
                    act.wait_ge(l2_sum, n)
                act.activation(SQT[:].rearrange("p t h d -> p (t h d)"), src.rearrange("p t d -> p (t d)"), ACT.Square).then_inc(l2_sq, 1)

            for k in range(PS):
                split(S_IN2 + k)
                if k == 1:
                    for half in range(2):
                        split_turned(H_IN2, lambda k: G_IN2 + k, half, 1)
            for k in range(PS):
                split(S_IN2 + PS + k)
                if k == 0:
                    left(S_IN2 + PS, P_IN2, 0, QTOK[:, 0, :])
                elif k == 1:
                    act.wait_ge(ba_out, 1)
                    act.activation(beta[:], ba[:, :, 0:HEADS], ACT.Sigmoid).then_inc(beta_ready, 1)
                    act.wait_ge(gates_landed, 32)
                    act.activation(alog[:], alog[:], ACT.Exp).then_inc(ea_ready, 1)
                    act.wait_ge(adt_ready, 1)
                    act.activation(sp_e[:], sp_e[:], ACT.Exp, scale=-1.0).then_inc(spe_ready, 1)
                elif k == 2:
                    conv_load(0, 0)
                elif k == 5:
                    act.wait_ge(gate_summed, 1)
                    act.activation(egl[:].rearrange("p (t b) h -> p b t h", b=2), ps[:, 0:2, 32:48].rearrange("p b (t h) -> p b t h", h=HEADS), ACT.Exp)
                    act.activation(gcs[:].rearrange("p t h -> p (t h)"), ps[:, 0, 0:U16], ACT.Copy).then_inc(gcs_ready, 1)
                    act.wait_ge(gcs_ready, 1)
                    act.activation(eg[:], gcs[:], ACT.Exp)
                elif k == 6:
                    act.wait_ge(kd_sub, 1)
                    act.activation(kd[:], kd[:], ACT.Exp).then_inc(exps_ready, 1)
                elif k == 7:
                    conv_silu(0)
            for k in range(PS):
                split(S_IN2 + 2 * PS + k)
                if k == 0:
                    left(S_IN2 + 2 * PS, P_IN2 + 1, 0, KTOK[:, 0, :])
                elif k == 1:
                    conv_store(0, QTOK, 1)
                elif k == 2:
                    conv_load(1, 1)
                elif k == 3:
                    square_heads(0, QTOK)
                elif k in (4, 5):
                    act.wait_ge(mem_landed, 16)
                    if k == 5:
                        act.wait_ge(sq_done, 13)
                    act.activation(MEM_JUNK[:], MEM[:, k - 4, :], ACT.Square, accum_out=ss[:, k - 4:k - 3]).then_inc(sq_done, 1)
                elif k == 7:
                    conv_silu(1)
            for k in range(PS):
                split(S_IN2 + 3 * PS + k)
                if k == 0:
                    left(S_IN2 + 3 * PS, P_IN2 + 2, 0, VTOK[:, 0, :])
                elif k == 1:
                    conv_store(1, KTOK, 0)
                elif k == 2:
                    conv_load(2, 0)
                elif k == 3:
                    square_heads(1, KTOK)
                elif k == 7:
                    conv_silu(2)
            for k in range(PS):
                split(S_IN2 + 4 * PS + k)
                if k == 0:
                    for t in range(TT):
                        left(S_IN2 + 4 * PS, P_IN2 + 3, t, ZTOK[:, t, :], ACT.Silu)
                elif k == 1:
                    conv_store(2, VTOK, 1)
                elif k in (2, 3, 4):
                    act.wait_ge(qk2_turned, k - 1)
                    dst = (QT2, KT2, KBT)[k - 2]
                    act.activation(dst[:].rearrange("p h t -> p (h t)"), flat_high, ACT.Copy).then_inc(qk2_ready, 1)
                elif k == 6:
                    act.wait_ge(decsub_ready, 1)
                    act.activation(DEC[:], DEC[:], ACT.Exp).then_inc(decay_ready, 1)
            for k in range(PS):
                split(S_IN2 + 5 * PS + k)
                if k == 0:
                    left(S_IN2 + 5 * PS, P_IN2 + 4, 0, GA[:, 0, :])
            for k in range(PS):
                split(S_KV + k)
                if k == 0:
                    for t in range(TT):
                        left(S_KV, P_IN2 + 5, t, GBT[:, t, :], ACT.Sigmoid)
                elif k == 1:
                    for half in range(2):
                        split_turned(H_MEM, lambda k: G_MEM + k, half, 1)
                elif k == 4:
                    act.wait_ge(c31_turned, 1)
                    act.wait_ge(pad31_ready, 1)
                    act.activation(CIN31[:, :, DW - 1:], ps[:, 4:8, :].rearrange("p b (c t) -> p (b c) t", t=T), ACT.Copy).then_inc(c31_in, 1)
                elif k == 5:
                    act.wait_ge(u_done, 1)
                    act.activation(U[:].rearrange("p t h d -> p (t h d)"), flat_high, ACT.Copy).then_inc(u_ready, 1)
                elif k == 6:
                    act.wait_ge(wt_done, 1)
                    act.activation(WT[:].rearrange("p h t -> p (h t)"), flat_high, ACT.Copy).then_inc(wt_ready, 1)
            for k in range(PS):
                split(S_KV + PS + k)
                if k == 0:
                    left(S_KV + PS, P_KV, 0, K_0[:, 0, :])
            for k in range(PS):
                split(S_KV + 2 * PS + k)
                if k == 0:
                    left(S_KV + 2 * PS, P_KV + 1, 0, K_1[:, 0, :])
                elif k == 1:
                    act.wait_ge(o_ready, T // CHUNK)
                    act.activation(OSQ[:], O[:], ACT.Square).then_inc(osq_ready, 1)
            for k in range(PS):
                split(S_KV + 3 * PS + k)
                if k == 0:
                    left(S_KV + 3 * PS, P_KV + 2, 0, V_0[:, 0, :])
                elif k == 6:
                    split_turned(H_OUT2, lambda k: G_DN, 0, 1)
            for k in range(PS):
                split(S_OUT2 + k)
                if k == 0:
                    left(S_OUT2, P_KV + 3, 0, V_1[:, 0, :])
                elif k == 1:
                    act.wait_ge(c31_back, 1)
                    act.activation(C[:, 0, :], ps[:, 0:2, :].rearrange("p b n -> p (b n)"), ACT.Copy).then_inc(c_rows0, 1)
                elif k == 3:
                    act.wait_ge(csum, 1)
                    for t in range(TT):
                        act.activation(CSQ[:, t, :], C[:, t, :], ACT.Square, accum_out=ss[:, t:t + 1]).then_inc(sq_done, 1)
                elif k == 4:
                    for c in range(HEADS):
                        act.wait_ge(turned, KT // 2 * H_OUT2 + (HEADS + c) // 2 + 1)
                        act.activation(CS[:, c, :], ps[:, c // 2, (c % 2) * T:(c % 2 + 1) * T], ACT.Silu, scale=dw_vec(1, c), bias=dw_vec(2, c)).then_inc(cs_ready, 1)
                        act.wait_ge(cs_ready, c + 1)
                        act.activation(HHI[:, HEADS + c, :], CS[:, c, :], ACT.Copy).then_inc(ht_hi, 1)
            for k in range(PS):
                split(S_OUT2 + PS + k)
                if k in (2, 4):
                    n = k // 2 - 1
                    act.wait_ge(kx_turned, n + 1)
                    act.activation(KXT[:, 8 * n:8 * n + 8, :].rearrange("p k t -> p (k t)"), flat_high, ACT.Copy).then_inc(kx_ready, 1)
            act.wait_ge(out1, P_OUT2 + 2)
            squares_of(X, ss, XQN)
            passes(S_Q, P_Q, [QX[:, 0, n * COLS:(n + 1) * COLS] for n in range(2)], H_XQ, lambda k: G_XQ + k)
            act.wait_ge(kx_turned, 3)
            act.activation(QXT[:, 0:8, :].rearrange("p k t -> p (k t)"), flat_low, ACT.Copy).then_inc(kx_ready, 1)
            for h in range(XHEADS):
                s = h % 2
                act.wait_ge(xmax, h + 1)
                if h >= 2:
                    act.wait_ge(xturned, h - 1)
                for q in range(TT):
                    last = act.activation(PX[:, s, q, :], ps[:, s, q * T:(q + 1) * T], ACT.Exp, bias=nmax[:, s, q:q + 1],
                                          scale=float(XHD) ** -0.5, accum_out=den[:, s, q:q + 1])
                last.then_inc(xprobs, 1)
                act.wait_ge(xturned, h + 1)
                if h >= 2:
                    act.wait_ge(xatt, h - 1)
                act.activation(PXT[:, s].rearrange("p k t -> p (k t)"), ps[:, 2 + s, :], ACT.Copy).then_inc(xpt, 1)
            passes(S_O, P_O, [None, None], H_XO)
            act.wait_ge(out1, P_O + 2)
            squares_of(X, ss)
            for half in range(2):
                split_turned(H_MLP2, lambda k: G_MLP2 + k, half, half)
            mlp(1, S_MLP2, P_MLP2)
            act.wait_ge(out1, P_MLP2 + 2 * HALF_PASSES)
            squares_of(X, ss, ROWS)

        @block.vector
        def _(dve):
            own = Own(dve, dve_own)

            def split(s, off=0):
                dve.wait_ge(hi_ready, s + off + 1)
                if s >= NSPLIT:
                    dve.wait_ge(w_used, s + off - NSPLIT + 1)
                dve.tensor_tensor(WLO[:, s % NSPLIT], RAW[:, s % NRAW], WHI[:, s % NSPLIT].bitcast(F32), ALU.subtract).then_inc(lo_ready, 1)

            def normalise(n, dst, src):
                dve.wait_ge(rstd_ready, n + 1)
                for t in range(TT):
                    dve.tensor_scalar(dst[:, t, :], src[:, t, :], rstd[:, t:t + 1], None, ALU.mult).then_inc(xn_ready, 1)

            def split_turned(h, g, half, group):
                for k in range(KT // 2 * half, KT // 2 * (half + 1)):
                    dve.wait_ge(ht_hi, KT * h + k // 2 * 2 + 2)
                    v = ps[:, 4 * group + (k % 8) // 2, (k % 2) * T:(k % 2 + 1) * T]
                    if g is None:
                        dve.tensor_tensor(HLO[:, k, :], v, HHI[:, k, :].bitcast(F32), ALU.subtract).then_inc(ht_lo, 1)
                    else:
                        dve.scalar_tensor_tensor(HLO[:, k, :], v, gain(g(k)), HHI[:, k, :].bitcast(F32), ALU.mult, ALU.subtract).then_inc(ht_lo, 1)

            def left(s_end, p, dst):
                dve.wait_ge(w_used, s_end)
                g = 4 * GROUPS[p] + 2
                dve.tensor_copy(dst, ps[:, g:g + 2, :].rearrange("p b n -> p (b n)")).then_inc(out1, 1)

            def add_residual(s_end, group, c0, off=0):
                dve.wait_ge(w_used, s_end + off)
                for t, o in enumerate((out0, out1)):
                    g = 4 * group + 2 * t
                    v = X[:, t, c0:c0 + COLS]
                    dve.tensor_tensor(v, ps[:, g:g + 2, :].rearrange("p b n -> p (b n)"), v, ALU.add).then_inc(o, 1)

            def passes(s0, p0, dsts, h=None, g=None):
                for n in range(len(dsts)):
                    for k in range(PS):
                        split(s0 + n * PS + k)
                        if k == 0 and n > 0:
                            done(s0, p0, n - 1, dsts)
                        if k == 1 and n == 0:
                            for half in range(2):
                                split_turned(h, g, half, 1 - GROUPS[p0])
                done(s0, p0, len(dsts) - 1, dsts)

            def done(s0, p0, n, dsts):
                if dsts[n] is None:
                    add_residual(s0 + (n + 1) * PS, GROUPS[p0 + n], n * COLS)
                else:
                    left(s0 + (n + 1) * PS, p0 + n, dsts[n])

            def mlp(m, s0, p0):
                with dve.Fori(0, 2) as half:
                    off, roff, hoff = half * HALF_STEPS, half * 16, half * 8

                    def square(p):
                        g = 4 * (p % 2)
                        for t, o in enumerate((out0, out1)):
                            dve.wait_ge(relu_done, 16 * m + 2 * p + t + 1 + hoff)
                            dve.scalar_tensor_tensor(R[:, t, :], ps[:, g + 2 * t:g + 2 * t + 2, :].rearrange("p b n -> p (b n)"), 0.0, R[:, t, :],
                                                     ALU.max, ALU.mult).then_inc(o, 1)

                    def hidden_lo(p):
                        g = 4 * (p % 2)
                        for b in range(4):
                            dve.wait_ge(at_hi, 32 * m + 4 * p + b + 1 + roff)
                            k = 8 * p + 2 * b
                            dve.tensor_tensor(ALO[:, k:k + 2, :].rearrange("p k t -> p (k t)"), ps[:, g + b, :],
                                              AHI[:, k:k + 2, :].bitcast(F32).rearrange("p k t -> p (k t)"), ALU.subtract).then_inc(at_lo, 1)

                    for p in range(4):
                        for k in range(PS):
                            split(s0 + p * PS + k, off)
                            if p >= 1 and k == 0:
                                square(p - 1)
                            if p >= 1 and k == 2:
                                hidden_lo(p - 1)
                    n = HK // STEP
                    for k in range(2 * n):
                        split(s0 + 4 * PS + k, off)
                        if k == 0:
                            square(3)
                        if k == 2:
                            hidden_lo(3)
                        if k == n:
                            add_residual(s0 + 4 * PS + n, 0, 0, off)
                    add_residual(s0 + 4 * PS + 2 * n, 1, COLS, off)

            dve.wait_ge(vec_turned, 1)
            dve.tensor_copy(VEC[:].rearrange("p n c -> p (n c)"), ps[:, 0, :]).then_inc(vec_ready, 1)
            normalise(N_IN, xn, X)
            dve.wait_ge(vec_ready, 1)
            passes(S_IN, P_IN, [PROJ[:, 1, n * COLS:(n + 1) * COLS] for n in range(4)], H_IN, lambda k: G_IN + k)
            dve.wait_ge(qk_turned, 2)
            dve.tensor_copy(KTT[:].rearrange("p h t -> p (h t)"), ps[:, 4:8, :].rearrange("p b n -> p (b n)")).then_inc(kt_ready, 1)
            dve.wait_ge(pool_out, 1)
            dve.wait_ge(pools_landed, 16)
            for t in range(TT):
                last = dve.tensor_tensor(PROJ[:, t, 0:COLS], ps[:, 4 + 2 * t:6 + 2 * t, :].rearrange("p b n -> p (b n)"), PSB[:], ALU.mult)
            last.then_inc(y_pool, 1)
            dve.wait_ge(alibi_landed, 16)

            def biased(h):
                s = h % 2
                slope = 2.0 ** (-8.0 * (h + 1) / HEADS)
                own.wait()
                own.mark(dve.scalar_tensor_tensor(BIAS[:], ALIBI[:, 0, :], -slope, ALIBI[:, 1, :], ALU.mult, ALU.add))
                own.wait()
                dve.wait_ge(scored, h + 1)
                if h >= 2:
                    dve.wait_ge(probs_turned, h - 1)
                own.mark(dve.scalar_tensor_tensor(S1[:, s, :], ps[:, s, 0:NS], float(HD) ** -0.5, BIAS[:], ALU.mult, ALU.add))
                own.wait()
                own.mark(dve.tensor_reduce(nmax[:, s, 0:1], S1[:, s, 0:P], AX_X, ALU.max))
                own.mark(dve.tensor_reduce(nmax[:, s, 1:2], S1[:, s, P:NS], AX_X, ALU.max))
                own.wait()
                dve.tensor_scalar(nmax[:, s, :], nmax[:, s, :], -1.0, None, ALU.mult).then_inc(max_ready, 1)

            def weighted(h):
                s = h % 2
                dve.wait_ge(attended, h + 1)
                own.mark(dve.reciprocal(rden[:, s, :], den[:, s, :]))
                own.wait()
                for t in range(TT):
                    last = dve.tensor_scalar(PROJ[:, t, COLS + h * HD:COLS + (h + 1) * HD], ps[:, 4 + s, t * P:(t + 1) * P], rden[:, s, t:t + 1], None, ALU.mult)
                last.then_inc(y_attn, 1)

            biased(0)
            for h in range(HEADS):
                if h + 1 < HEADS:
                    biased(h + 1)
                weighted(h)
            dve.wait_ge(rstd_ready, N_MIX + 1)
            for n in range(2):
                for t in range(TT):
                    v = PROJ[:, t, n * COLS:(n + 1) * COLS]
                    last = dve.tensor_scalar(v, v, rstd[:, 2 * n + t:2 * n + t + 1], None, ALU.mult)
            last.then_inc(y_ready, 1)
            passes(S_OUT, P_OUT, [None, None], H_OUT, lambda k: G_OUT + k)
            normalise(N_MLP, xn, X)
            for half in range(2):
                split_turned(H_MLP, lambda k: G_MLP + k, half, half)
            mlp(0, S_MLP, P_MLP)

            def final(n, dst):
                dve.wait_ge(rstd_ready, n + 1)
                dve.wait_ge(final_landed, 16 if n == N_F1 else 32)
                for t in range(TT):
                    dve.scalar_tensor_tensor(dst[:, t, :], X[:, t, :], rstd[:, t:t + 1], GB[:], ALU.mult, ALU.mult).then_inc(x_final, 1)

            final(N_F1, X)
            dve.wait_ge(x_final, 2)
            normalise(N_IN2, xn, X)
            dve.wait_ge(ba_split, 1)
            dve.tensor_tensor(BALO[:], BARAW[:], BAHI[:].bitcast(F32), ALU.subtract).then_inc(ba_split, 1)
            low = ps[:, 0:4, :].rearrange("p b n -> p (b n)")
            high = ps[:, 4:8, :].rearrange("p b n -> p (b n)")

            def conv4_tap(n, j):
                if j == 0:
                    dve.wait_ge(cin_ready, n + 1)
                    if n >= 1:
                        dve.wait_ge(conv_back, n)
                for c in range(HEADS):
                    src, weight = CIN[:, c, j:j + T], tap(j, n * HEADS + c)
                    if j == 0:
                        last = dve.tensor_scalar(COUT[:, c, :], src, weight, None, ALU.mult)
                    else:
                        if c == 0:
                            own.wait()
                        last = dve.scalar_tensor_tensor(COUT[:, c, :], src, weight, COUT[:, c, :], ALU.mult, ALU.add)
                    if j < CONV - 1:
                        own.mark(last)
                if j == CONV - 1:
                    last.then_inc(conv_done, 1)

            def conv31_taps(first, end):
                for j in range(first, end):
                    for c in range(HEADS):
                        src = CIN31[:, c, j:j + T]
                        if j == 0:
                            last = dve.tensor_scalar(COUT31[:, c, :], src, dw_tap(j, c), dw_vec(0, c), ALU.mult, ALU.add)
                        else:
                            if c == 0:
                                dve.wait_ge(c31_own, HEADS * j)
                            last = dve.scalar_tensor_tensor(COUT31[:, c, :], src, dw_tap(j, c), COUT31[:, c, :], ALU.mult, ALU.add)
                        last.then_inc(c31_own if j < DW - 1 or c < HEADS - 1 else c31_done, 1)

            def conv_store(n, dst, group):
                dve.wait_ge(conv_back, n + 1)
                dve.tensor_copy(dst[:, 1, :], ps[:, 4 * group + 2:4 * group + 4, :].rearrange("p b n -> p (b n)")).then_inc(sec1, 1)

            def heads(v):
                return v.rearrange("p t (h d) -> p t h d", d=HD)

            def per_head(v):
                return v.unsqueeze(3).broadcast_to([P, TT, HEADS, HD])

            def l2_of(n):
                return per_head(l2r[:, n, :].rearrange("p (t h) -> p t h", t=TT))

            def sum_squares(n):
                dve.wait_ge(l2_sq, n + 1)
                dve.tensor_reduce(l2[:, n, :], SQT[:].rearrange("p t h d -> p (t h) d"), AX_X, ALU.add).then_inc(l2_sum, 1)

            def softplus_gate():
                dve.wait_ge(spe_ready, 1)
                own.mark(dve.tensor_scalar(sp_z[:], sp_e[:], 2.0, None, ALU.add))
                own.wait()
                own.mark(dve.reciprocal(sp_z[:], sp_z[:]))
                own.wait()
                own.mark(dve.tensor_tensor(sp_z[:], sp_z[:], sp_e[:], ALU.mult))
                own.wait()
                own.mark(dve.tensor_tensor(sp_q[:], sp_z[:], sp_z[:], ALU.mult))
                own.wait()
                own.mark(dve.tensor_scalar(sp_p[:], sp_q[:], 1.0 / (2 * LOG_TERMS - 1), None, ALU.mult))
                for n in range(LOG_TERMS - 2, 0, -1):
                    own.wait()
                    own.mark(dve.scalar_tensor_tensor(sp_p[:], sp_p[:], 1.0 / (2 * n + 1), sp_q[:], ALU.add, ALU.mult))
                own.wait()
                own.mark(dve.scalar_tensor_tensor(sp_p[:], sp_p[:], 1.0, sp_z[:], ALU.add, ALU.mult))
                own.mark(dve.tensor_scalar(adt[:], adt[:], 0.0, None, ALU.max))
                own.wait()
                own.mark(dve.scalar_tensor_tensor(sp_p[:], sp_p[:], 2.0, adt[:], ALU.mult, ALU.add))
                own.wait()
                dve.wait_ge(ea_ready, 1)
                dve.scalar_tensor_tensor(gate[:], sp_p[:], -1.0, alog[:].unsqueeze(1).broadcast_to([P, TT, HEADS]), ALU.mult, ALU.mult).then_inc(gate_ready, 1)

            flat_x = XI[:].rearrange("p u c -> p (u c)")
            flat_xt = XT[:].rearrange("p u c -> p (u c)")
            eye = IDENT.unsqueeze(1).broadcast_to([P, U16, P])
            high_units = ps[:, 4:8, :].rearrange("p b (u c) -> p (b u) c", c=P)

            def mask(lv):
                return SQ[:, 5 + lv, :].unsqueeze(1).broadcast_to([P, U16, P])

            for k in range(PS):
                split(S_IN2 + k)
                if k == 1:
                    for half in range(2):
                        split_turned(H_IN2, lambda k: G_IN2 + k, half, 1)
                elif k == 7:
                    dve.wait_ge(ba_done, 1)
                    dve.tensor_copy(ba[:], ps[:, 4:8:2, 0:NBA]).then_inc(ba_out, 1)
            for k in range(PS):
                split(S_IN2 + PS + k)
                if k == 0:
                    left(S_IN2 + PS, P_IN2, QTOK[:, 1, :])
                    dve.wait_ge(gates_landed, 32)
                    dve.wait_ge(ba_out, 1)
                    own.mark(dve.tensor_tensor(adt[:], ba[:, :, HEADS:NBA], dtb[:].unsqueeze(1).broadcast_to([P, TT, HEADS]), ALU.add))
                    own.wait()
                    dve.scalar_tensor_tensor(sp_e[:], adt[:], -1.0, adt[:], ALU.mult, ALU.max).then_inc(adt_ready, 1)
                elif k == 2:
                    softplus_gate()
                elif 3 <= k < 3 + CONV:
                    conv4_tap(0, k - 3)
                    if k == 6:
                        dve.wait_ge(gcs_ready, 1)
                        dve.tensor_tensor(kd[:].rearrange("p t h -> p (t h)"), ps[:, 0, 16:16 + U16], gcs[:].rearrange("p t h -> p (t h)"), ALU.subtract).then_inc(kd_sub, 1)
                elif k == 7:
                    dve.wait_ge(exps_ready, 1)
                    dve.wait_ge(beta_ready, 1)
                    own.mark(dve.tensor_tensor(bke[:], beta[:], eg[:], ALU.mult))
            for k in range(PS):
                split(S_IN2 + 2 * PS + k)
                if k == 0:
                    left(S_IN2 + 2 * PS, P_IN2 + 1, KTOK[:, 1, :])
                elif k == 1:
                    conv_store(0, QTOK, 1)
                elif 3 <= k < 3 + CONV:
                    conv4_tap(1, k - 3)
                elif k == 7:
                    sum_squares(0)
            for k in range(PS):
                split(S_IN2 + 3 * PS + k)
                if k == 0:
                    left(S_IN2 + 3 * PS, P_IN2 + 2, VTOK[:, 1, :])
                elif k == 1:
                    conv_store(1, KTOK, 0)
                elif k == 2:
                    dve.wait_ge(rstd_ready, N_MEM + 1)
                    for t in range(TT):
                        dve.tensor_scalar(MEM[:, t, :], MEM[:, t, :], rstd[:, t:t + 1], None, ALU.mult).then_inc(mem_ready, 1)
                elif 3 <= k < 3 + CONV:
                    conv4_tap(2, k - 3)
                elif k == 7:
                    sum_squares(1)
            for k in range(PS):
                split(S_IN2 + 4 * PS + k)
                if k == 0:
                    dve.wait_ge(l2_ready, 1)
                    dve.tensor_tensor(heads(QTOK), heads(QTOK), l2_of(0), ALU.mult).then_inc(qn_ready, 1)
                elif k == 1:
                    conv_store(2, VTOK, 1)
                    dve.tensor_tensor(heads(KTOK), heads(KTOK), l2_of(1), ALU.mult).then_inc(kn_ready, 1)
                elif k == 2:
                    dve.wait_ge(kn_ready, 1)
                    dve.tensor_tensor(KB_[:], heads(KTOK), per_head(beta[:]), ALU.mult).then_inc(kb_ready, 1)
                elif k == 3:
                    for u in range(U16):
                        last = dve.tensor_scalar(DIAG[:, u, :], IDENT, gcs[:, u // HEADS, u % HEADS:u % HEADS + 1], None, ALU.mult)
                    last.then_inc(diag_ready, 1)
                elif k == 4:
                    dve.wait_ge(sec0, 3)
                    dve.wait_ge(sec1, 3)
                    dve.tensor_tensor(heads(VTOK), heads(VTOK), per_head(beta[:]), ALU.mult).then_inc(v_ready, 1)
                elif k == 5:
                    dve.wait_ge(rows_ready, 1)
                    own.mark(dve.tensor_tensor(DEC[:], high_units, gcs[:].rearrange("p t h -> p (t h)").unsqueeze(2).broadcast_to([P, U16, P]), ALU.subtract))
                    own.wait()
                    dve.tensor_tensor(DEC[:], DEC[:], NEGMASK.unsqueeze(1).broadcast_to([P, U16, P]), ALU.add).then_inc(decsub_ready, 1)
                elif k in (6, 7):
                    dve.wait_ge(gram_done, k - 5)
                    dve.wait_ge(decay_ready, 1)
                    dst = LT if k == 6 else ATT
                    dve.tensor_tensor(dst[:].rearrange("p u c -> p (u c)"), high, DEC[:].rearrange("p u c -> p (u c)"), ALU.mult).then_inc(gram_ready, 1)
            for k in range(PS):
                split(S_IN2 + 5 * PS + k)
                if k == 0:
                    left(S_IN2 + 5 * PS, P_IN2 + 4, GA[:, 1, :])
                    dve.wait_ge(gram_ready, 1)
                    dve.tensor_tensor(WL[:], LT[:], mask(0), ALU.mult).then_inc(level0_ready, 1)
                    dve.wait_ge(level0_ready, 1)
                    dve.tensor_tensor(XT[:], eye, WL[:], ALU.subtract).then_inc(xt_up, 1)
                    dve.wait_ge(level0_turned, 1)
                    dve.tensor_tensor(XI[:], eye, high_units, ALU.subtract).then_inc(x_up, 1)
                    continue
                for j in range(STEP):
                    lv, part = level_part(k, j)
                    if part == 0:
                        dve.wait_ge(wl_done, lv)
                        dve.tensor_tensor(WL[:], high_units, mask(lv), ALU.mult).then_inc(wl_ready, 1)
                    elif part == 1:
                        dve.wait_ge(xw_done, lv)
                        dve.wait_ge(x_up, lv)
                        dve.tensor_tensor(flat_x, flat_x, high, ALU.subtract).then_inc(x_up, 1)
                    else:
                        dve.wait_ge(xt_done, lv)
                        dve.wait_ge(xt_up, lv)
                        dve.tensor_tensor(flat_xt, flat_xt, high, ALU.subtract).then_inc(xt_up, 1)
            for k in range(PS):
                split(S_KV + k)
                if k == 0:
                    dve.wait_ge(out0, P_IN2 + 6)
                    dve.wait_ge(out1, P_IN2 + 6)
                    dve.tensor_tensor(GA, GA, GBT, ALU.mult).then_inc(glu_ready, 1)
                elif k == 1:
                    for half in range(2):
                        split_turned(H_MEM, lambda k: G_MEM + k, half, 1)
                elif k == 2:
                    dve.tensor_tensor(KBG[:], heads(KTOK), per_head(bke[:]), ALU.mult).then_inc(kbg_ready, 1)
                elif k == 3:
                    dve.wait_ge(kbg_ready, 1)
                    dve.tensor_tensor(heads(KTOK), heads(KTOK), per_head(kd[:]), ALU.mult).then_inc(kdec_ready, 1)
                elif k >= 5:
                    if k == 5:
                        dve.wait_ge(c31_in, 1)
                    conv31_taps(k - 5, k - 4)

            def two(b):
                return ps[:, b:b + 2, :].rearrange("p b (h d) -> p (b h) d", d=HD)

            for k in range(PS):
                split(S_KV + PS + k)
                if k == 0:
                    left(S_KV + PS, P_KV, K_0[:, 1, :])
                n = k // 2
                t, r = n // 2, CHUNK * (n % 2)
                rows = slice(r, r + CHUNK)
                if k % 2 == 0:
                    dve.wait_ge(u_ready, 1)
                    dve.wait_ge(ws_done, n + 1)
                    dve.tensor_tensor(U[rows, t], U[rows, t], two(4)[rows], ALU.subtract).then_inc(vn_ready, 1)
                    dve.tensor_tensor(O[rows, t], two(6)[rows], eg[rows, t, :].unsqueeze(2).broadcast_to([CHUNK, HEADS, HD]), ALU.mult).then_inc(qs_ready, 1)
                    conv31_taps(C31_WK0 + 3 * n, C31_WK0 + 3 * n + 1)
                else:
                    dve.wait_ge(vn_used, n + 1)
                    if n + 1 < T // CHUNK:
                        dve.wait_ge(sd_ready, n + 1)
                        dve.tensor_tensor(ST[:], SD[:], two(4), ALU.add).then_inc(state_ready, 1)
                    dve.wait_ge(qs_ready, n + 1)
                    dve.tensor_tensor(O[rows, t], O[rows, t], two(6)[rows], ALU.add).then_inc(o_ready, 1)
                    conv31_taps(C31_WK0 + 3 * n + 1, C31_WK0 + 3 * n + 3)
            for k in range(PS):
                split(S_KV + 2 * PS + k)
                if k == 0:
                    left(S_KV + 2 * PS, P_KV + 1, K_1[:, 1, :])
                elif k == 2:
                    dve.wait_ge(osq_ready, 1)
                    dve.tensor_reduce(osum[:], OSQ[:].rearrange("p t h d -> p (t h) d"), AX_X, ALU.add).then_inc(osum_ready, 1)
                elif k == 4:
                    flat_o = O[:].rearrange("p t h d -> p (t h d)")
                    own.mark(dve.tensor_tensor(flat_o, flat_o, ZTOK.rearrange("p t d -> p (t d)"), ALU.mult))
                elif k == 6:
                    own.wait()
                    dve.wait_ge(orst_ready, 1)
                    dve.tensor_tensor(O[:], O[:], per_head(orst[:].rearrange("p (t h) -> p t h", t=TT)), ALU.mult).then_inc(o_final, 1)
                conv31_taps(C31_WK1 + k, C31_WK1 + k + 1)
            for k in range(PS):
                split(S_KV + 3 * PS + k)
                if k == 0:
                    left(S_KV + 3 * PS, P_KV + 2, V_0[:, 1, :])
                elif k == 6:
                    split_turned(H_OUT2, lambda k: G_DN, 0, 1)
                conv31_taps(C31_WK1 + PS + k, C31_WK1 + PS + k + 1)
            for k in range(PS):
                split(S_OUT2 + k)
                if k == 0:
                    left(S_OUT2, P_KV + 3, V_1[:, 1, :])
                elif k == 1:
                    dve.wait_ge(c31_back, 1)
                    dve.tensor_copy(C[:, 1, :], ps[:, 2:4, :].rearrange("p b n -> p (b n)")).then_inc(c_rows1, 1)
                    dve.wait_ge(c_rows0, 1)
                    dve.wait_ge(c_rows1, 1)
                    own.mark(dve.tensor_reduce(cmean[:], C, AX_X, ALU.add))
                    own.wait()
                    own.mark(dve.tensor_scalar(cmean[:], cmean[:], -1.0 / COLS, None, ALU.mult))
                    own.wait()
                    for t in range(TT):
                        last = dve.tensor_scalar(C[:, t, :], C[:, t, :], cmean[:, t:t + 1], None, ALU.add)
                    last.then_inc(csum, 1)
                elif k == 3:
                    dve.wait_ge(rstd_ready, N_LN + 1)
                    for t in range(TT):
                        last = dve.tensor_scalar(C[:, t, :], C[:, t, :], rstd[:, t:t + 1], None, ALU.mult)
                    last.then_inc(c_final, 1)
                elif k == 4:
                    for c in range(HEADS):
                        dve.wait_ge(ht_hi, KT * H_OUT2 + HEADS + c + 1)
                        dve.tensor_tensor(HLO[:, HEADS + c, :], CS[:, c, :], HHI[:, HEADS + c, :].bitcast(F32), ALU.subtract).then_inc(ht_lo, 1)
            for k in range(PS):
                split(S_OUT2 + PS + k)
                if k == 0:
                    dve.wait_ge(x_back, 16)
                    add_residual(S_OUT2 + PS, GROUPS[P_OUT2], 0)
            add_residual(S_OUT2 + 2 * PS, GROUPS[P_OUT2 + 1], COLS)
            normalise(N_XQ, XQN, X)
            passes(S_Q, P_Q, [QX[:, 1, n * COLS:(n + 1) * COLS] for n in range(2)], H_XQ, lambda k: G_XQ + k)
            dve.wait_ge(kx_turned, 4)
            dve.tensor_copy(QXT[:, 8:16, :].rearrange("p k t -> p (k t)"), high).then_inc(kx_ready, 1)

            def xmaxima(h):
                s = h % 2
                dve.wait_ge(xscored, h + 1)
                if h >= 2:
                    dve.wait_ge(xprobs, h - 1)
                own.mark(dve.tensor_reduce(nmax[:, s, :], ps[:, s, :].rearrange("p (q k) -> p q k", q=TT), AX_X, ALU.max))
                own.wait()
                dve.tensor_scalar(nmax[:, s, :], nmax[:, s, :], -float(XHD) ** -0.5, None, ALU.mult).then_inc(xmax, 1)

            xmaxima(0)
            for h in range(XHEADS):
                s = h % 2
                if h + 1 < XHEADS:
                    xmaxima(h + 1)
                dve.wait_ge(xatt, h + 1)
                own.mark(dve.reciprocal(rden[:, s, :], den[:, s, :]))
                own.wait()
                for q in range(TT):
                    last = dve.tensor_scalar(QX[:, q, h * XHD:(h + 1) * XHD], ps[:, 4 + 2 * s + q, :], rden[:, s, q:q + 1], None, ALU.mult)
                last.then_inc(xout, 1)
            passes(S_O, P_O, [None, None], H_XO)
            normalise(N_MLP2, xn, X)
            for half in range(2):
                split_turned(H_MLP2, lambda k: G_MLP2 + k, half, half)
            mlp(1, S_MLP2, P_MLP2)
            final(N_F2, ROWS)


def kernel(**inputs):
    import numpy as _np
    import concourse.bacc as _bacc
    from concourse import mybir as _mybir
    from concourse.bass_utils import run_bass_kernel_spmd as _run

    a = {k: _np.asarray(v) for k, v in inputs.items()}

    def rows(*names):
        got = _np.concatenate([a[n].reshape(-1, 128) for n in names], 0)
        return _np.concatenate([got, _np.zeros((128 - len(got), 128), got.dtype)], 0)

    taps = a["cf_dw_w_2"].reshape(-1, 128)
    pad = _np.zeros((4, 128), taps.dtype)
    vectors = _np.stack([
        rows("norm_mix_g", "pool_out_norm_g", "attn_out_norm_g", "norm_mlp_g", "norm_mix_g_2", "norm_xa_g_2", "norm_mem_g_2",
             "norm_mlp_g_2", "dn_norm_g_2"),
        rows("dn_conv_w_2", "cf_dw_b_2", "cf_ln_g_2", "cf_ln_b_2"),
        _np.concatenate([taps[:124], pad], 0), _np.concatenate([taps[124:], pad], 0)])
    squares, alibi, pool_avg = shape_constants()
    feeds = {
        "x": a["x"][0], "mem": a["mem_2"][0], "vectors": vectors, "squares": squares, "alibi": alibi, "pool_avg": pool_avg,
        "w_in": a["w_in"][0], "pool_w": a["pool_w"][0], "pool_scale": a["pool_scale"][0], "w_out": a["w_out"][0],
        "w_up": a["w_up"][0], "w_down": a["w_down"][0], "final_g": a["norm_final_g"], "w_in2": a["w_in_2"][0],
        "a_log": a["dn_a_log_2"][0], "dt_bias": a["dn_dt_bias_2"][0], "w_out2": a["w_out_2"][0],
        "wq": a["xa_wq_2"][0], "wk": a["xa_wk_2"][0], "wv": a["xa_wv_2"][0], "wo": a["xa_wo_2"][0],
        "w1": a["mlp_w1_2"][0], "w2": a["mlp_w2_2"][0], "final_g2": a["norm_final_g_2"],
    }
    nc = _bacc.Bacc("TRN2", target_bir_lowering=False, num_devices=1)
    arrays, args = {}, {}
    for name, v in feeds.items():
        v = _np.ascontiguousarray(v)
        arrays[f"in_{name}"] = v
        args[name] = nc.dram_tensor(f"in_{name}", v.shape, _mybir.dt.from_np(v.dtype), kind="ExternalInput").ap()
    args["out"] = nc.dram_tensor("out_y", (T, D), F32, kind="ExternalOutput").ap()
    build(nc, **args)
    r = _run(nc, [arrays], core_ids=[0])
    return r.results[0]["out_y"].reshape(1, T, D)
```

```python
from contextlib import ExitStack

import numpy as np

import concourse.bass as bass
from concourse import mybir

F32 = mybir.dt.float32
F32R = mybir.dt.float32r
ACT = mybir.ActivationFunctionType
ALU = mybir.AluOpType
AX_X = mybir.AxisListType.X

P = 128
T = 256
TT = T // P
D = 2048
KT = D // P
FF = 4 * D
HALF = FF // 2
HK = HALF // P
EPS = 1e-6

COLS = 1024
BANK = 512
STEP = 2
NRAW = 4
NSPLIT = 2

HEADS = 8
HD = 128
CHUNK = 64
WINDOWS = (2, 4, 8, 16)
GROUP = 256
PATTERNS = ((128, 1), (512, 4), (2048, 16))
CONV = 4
DW = 31
XHEADS = 4
XHD = D // XHEADS
XDT = XHD // P
QK_TILES = 3 * HEADS
LOG_TERMS = 8
NEG = -1e30


def shape_constants():
    i = np.arange(P)
    same = (i[:, None] // CHUNK) == (i[None, :] // CHUNK)
    ident = np.eye(P)
    tri = same & (i[:, None] <= i[None, :])
    negmask = np.where(tri, 0.0, NEG)
    mats = [ident, tri, same, negmask, np.ones((P, P))]
    b = 1
    while b < CHUNK:
        lower = (i[:, None] // (2 * b) == i[None, :] // (2 * b)) & (i[:, None] // b < i[None, :] // b)
        mats.append(lower if b == 1 else lower.T)
        b *= 2
    squares = np.stack([np.asarray(m, np.float32) for m in mats], 1)

    t = np.arange(T)
    dist = t[:, None] - t[None, :]
    times = sum(((dist >= 0) & (dist <= w) & (dist % r == 0)).astype(np.float64) for w, r in PATTERNS)
    logs = np.where(times > 0, np.log(np.maximum(times, 1.0)), NEG)
    far = np.maximum(dist, 0)
    cut = lambda m: np.concatenate([m[:P, :P], m[P:, :]], 1)
    alibi = np.stack([cut(far), cut(logs)], 1).astype(np.float32)

    pool = np.zeros((len(WINDOWS), T, T))
    for g, w in enumerate(WINDOWS):
        pool[g] = np.where((dist >= 0) & (dist < w), 1.0 / np.minimum(t + 1, w)[:, None], 0.0) - np.eye(T)
    pool_t = pool.transpose(2, 0, 1).reshape(TT, P, len(WINDOWS), T).transpose(1, 2, 0, 3)
    return squares, alibi, np.ascontiguousarray(pool_t, np.float32)


class Own:

    def __init__(self, eng, sem):
        self.eng, self.sem, self.n = eng, sem, 0

    def mark(self, ins):
        self.n += 1
        ins.then_inc(self.sem, 1)

    def wait(self):
        self.eng.wait_ge(self.sem, self.n)


def build(nc, x, mem, vectors, squares, alibi, pool_avg, w_in, pool_w, pool_scale, w_out, w_up, w_down,
          final_g, w_in2, a_log, dt_bias, w_out2, wq, wk, wv, wo, w1, w2, final_g2, out):
    ctx = ExitStack()
    with ctx:
        def sem(name):
            return ctx.enter_context(nc.semaphore(name))

        KB = 1024
        base = (nc.sbuf_base + 63) // 64 * 64
        ctx.enter_context(nc.sbuf_tensor("slab", [P, (207 * KB + 512) // 4], F32))

        def at(name, shape, where, dtype=F32):
            return nc.alloc_sbuf_tensor_at(name, shape, dtype, offset=base + int(where * KB))

        X = at("residual", [P, TT, D], 0)
        HHI = at("stationary_hi", [P, KT, T], 16, F32R)
        HLO = at("stationary_lo", [P, KT, T], 32, F32R)
        RAW = at("weights_raw", [P, NRAW, STEP, COLS], 48)
        WHI = at("weights_hi", [P, NSPLIT, STEP, COLS], 80, F32R)
        WLO = at("weights_lo", [P, NSPLIT, STEP, COLS], 96, F32R)
        SQ = at("squares", [P, 11, P], 112)
        VEC = at("vectors", [P, 4, P], 117.5)
        VEC_RAW = at("vectors_raw", [P, 4, P], 121.5 + 84)
        free_small = [119.5]

        def small(name, shape, dtype=F32):
            t = at(name, shape, free_small[0], dtype)
            free_small[0] += (int(np.prod(shape[1:])) * 4 + 31) // 32 * 32 / KB
            assert free_small[0] <= 121.5
            return t

        A0 = 121.5
        IDENT, TRI, SAME, NEGMASK, ONES = (SQ[:, n, :] for n in range(5))
        LEVELS = 6

        NORMS = 10
        ss = small("ss", [P, TT * NORMS])
        ms = small("ms", [P, TT * NORMS])
        rstd = small("rstd", [P, TT * NORMS])
        halves = small("halves", [P, TT * HEADS])
        minus_ones = small("minus_ones", [P, TT])

        JUNK = at("squares_unused", [P, TT, D], A0 + 64)
        AHI = at("hidden_hi", [P, HK, T], A0 + 0, F32R)
        ALO = at("hidden_lo", [P, HK, T], A0 + 32, F32R)
        R = at("hidden", [P, TT, COLS], A0 + 64)
        GB = at("final_gain", [P, D], A0 + 72)
        ROWS = at("final_rows", [P, TT, D], A0 + 0)

        PROJ = at("proj", [P, 4, TT, COLS], A0 + 0)
        U_ROWS, Q_ROWS, K_ROWS, V_ROWS = (PROJ[:, n] for n in range(4))
        QT = at("q_t", [P, HEADS, T], A0 + 32)
        KTT = at("k_t", [P, HEADS, T], A0 + 40)
        POOLW = at("pool_w", [P, len(WINDOWS), 2, GROUP], A0 + 48)
        POOLA = at("pool_avg", [P, len(WINDOWS), TT, T], A0 + 56)
        DT = at("pooled_t", [P, HEADS, T], A0 + 64)
        NS = P + T
        S1 = at("scores", [P, 2, NS], A0 + 72)
        PT1 = at("probs_t", [P, 2, NS], A0 + 76)
        ALIBI = at("alibi", [P, 2, NS], A0 + 80)
        BIAS = at("bias", [P, NS], A0 + 83)
        PSB = at("pool_scale", [P, COLS], A0 + 16)
        nmax = small("nmax", [P, 2, 2])
        den = small("den", [P, HEADS, 2])
        rden = small("rden", [P, 2, 2])

        def slot(n):
            return A0 + 8 * n

        def rows_at(name, n):
            return at(name, [P, TT, COLS], slot(n))[:]

        def units_at(name, n):
            return at(name, [P, U16, P], slot(n))

        U16 = TT * HEADS
        QTOK, KTOK, VTOK, ZTOK = rows_at("q_tok", 0), rows_at("k_tok", 1), rows_at("v_tok", 2), rows_at("z_tok", 9)
        GA, GBT = rows_at("glu_a", 8), rows_at("glu_gate", 5)
        CIN = at("conv_in", [P, HEADS, CONV - 1 + T], slot(3))
        COUT = at("conv_out", [P, HEADS, T], slot(4) + 1)
        SQT = at("squared", [P, TT, HEADS, HD], slot(6))
        MEM_JUNK = at("memory_squares", [P, D], slot(7))
        KB_ = at("k_beta", [P, TT, HEADS, HD], slot(7))
        QT2 = at("q2_t", [P, HEADS, T], slot(6))
        KT2 = at("k2_t", [P, HEADS, T], slot(3))
        KBT = at("k_beta_t", [P, HEADS, T], slot(4))
        DIAG = units_at("gate_diag", 5)
        DEC = units_at("decay", 0)
        LT = units_at("lower_t", 5)
        ATT = units_at("attn_t", 4)
        XI = units_at("inverse", 0)
        XT = units_at("inverse_t", 3)
        WL = units_at("level_product", 7)
        KBG = at("k_beta_decayed", [P, TT, HEADS, HD], slot(0))
        U = at("u", [P, TT, HEADS, HD], slot(5))
        WT = at("w_t", [P, HEADS, T], slot(7))
        ST = at("state", [P, HEADS, HD], slot(10))
        SD = at("state_decayed", [P, HEADS, HD], slot(3))
        O = at("delta_out", [P, TT, HEADS, HD], slot(0))
        OSQ = at("delta_out_squared", [P, TT, HEADS, HD], slot(5))
        MEM = at("memory", [P, TT, D], 0)
        CIN31 = at("conv31_in", [P, HEADS, DW - 1 + T], 0)
        COUT31 = at("conv31_out", [P, HEADS, T], slot(8))
        LN_VAR = at("conv_variance", [P, TT], slot(6))
        LN_RSTD = at("conv_rstd", [P, TT], slot(6) + 0.125)
        LN_DIAG = at("conv_rstd_diag", [P, TT, P], slot(6) + 1)
        CS = at("conv_silu", [P, HEADS, T], slot(7))
        CSQ = at("conv_squares", [P, HEADS, T], slot(5))
        NBA = 16
        BARAW = at("w_ba", [P, KT, NBA], slot(10) + 2)
        BAHI = at("w_ba_hi", [P, KT, NBA], slot(10) + 3, F32R)
        BALO = at("w_ba_lo", [P, KT, NBA], slot(10) + 4, F32R)
        BAT = at("beta_alpha_columns", [P, T], slot(10) + 5)
        ba = small("beta_alpha", [P, TT, NBA])
        beta = small("beta", [P, TT, HEADS])
        adt = small("a_plus_dt", [P, TT, HEADS])
        sp_e = small("softplus_e", [P, TT, HEADS])
        sp_z = small("softplus_z", [P, TT, HEADS])
        sp_q = small("softplus_q", [P, TT, HEADS])
        sp_p = small("softplus_p", [P, TT, HEADS])
        gate = small("gate", [P, TT, HEADS])
        gcs = small("gate_cumsum", [P, TT, HEADS])
        eg = small("exp_gate", [P, TT, HEADS])
        kd = small("exp_to_end", [P, TT, HEADS])
        bke = small("beta_exp_gate", [P, TT, HEADS])
        egl = small("exp_chunk", [P, T // CHUNK, HEADS])
        alog = small("a_log", [P, HEADS])
        dtb = small("dt_bias", [P, HEADS])
        l2 = small("l2", [P, 2, U16])
        l2r = small("l2r", [P, 2, U16])
        osum = small("osum", [P, U16])
        orst = small("orst", [P, U16])

        KV = at("kv", [P, 4, TT, COLS], slot(1))
        V_0, K_0, K_1, V_1 = (KV[:, n] for n in range(4))
        KXT = at("kx_t", [P, KT, T], slot(8))
        QX = at("qx", [P, TT, D], slot(5))
        QXT = at("qx_t", [P, KT, T], slot(2))
        PX = at("probs", [P, 2, TT, T], slot(7))
        PXT = at("xprobs_t", [P, 2, TT, T], slot(7) + 4)

        ps = ctx.enter_context(nc.psum_tensor("ps", [P, 8, BANK], F32))

        x_landed = [sem(f"x_landed{n}") for n in range(2)]
        vec_landed = sem("vec_landed")
        ident_landed = sem("ident_landed")
        sq_landed = sem("sq_landed")
        alibi_landed = sem("alibi_landed")
        poolw_landed = sem("poolw_landed")
        poola_landed = sem("poola_landed")
        pools_landed = sem("pools_landed")
        ba_landed = sem("ba_landed")
        gates_landed = sem("gates_landed")
        final_landed = sem("final_landed")
        mem_landed = sem("mem_landed")
        raw_landed = [sem(f"raw_landed{n}") for n in range(NRAW)]
        out_landed = sem("out_landed")
        hi_ready = sem("hi_ready")
        lo_ready = sem("lo_ready")
        w_used = sem("w_used")
        out0 = sem("out0")
        out1 = sem("out1")
        vec_turned = sem("vec_turned")
        vec_ready = sem("vec_ready")
        halves_ready = sem("halves_ready")
        sq_done = sem("sq_done")
        rstd_ready = sem("rstd_ready")
        turned = sem("turned")
        ht_hi = sem("ht_hi")
        ht_lo = sem("ht_lo")
        relu_done = sem("relu_done")
        r_turned = sem("r_turned")
        at_hi = sem("at_hi")
        at_lo = sem("at_lo")
        x_final = sem("x_final")
        act_own = sem("act_own")
        dve_own = sem("dve_own")
        c31_own = sem("c31_own")
        pool_own = sem("pool_own")
        qk_turned = sem("qk_turned")
        qt_ready = sem("qt_ready")
        kt_ready = sem("kt_ready")
        pooled = sem("pooled")
        pooled_ready = sem("pooled_ready")
        pool_out = sem("pool_out")
        y_pool = sem("y_pool")
        scored = sem("scored")
        max_ready = sem("max_ready")
        probs_ready = sem("probs_ready")
        probs_turned = sem("probs_turned")
        pt_ready = sem("pt_ready")
        attended = sem("attended")
        y_attn = sem("y_attn")
        y_ready = sem("y_ready")
        parked = sem("parked")
        x_back = sem("x_back")
        mem_ready = sem("mem_ready")
        ba_split = sem("ba_split")
        ba_done = sem("ba_done")
        ba_columns = sem("ba_columns")
        ba_turned = sem("ba_turned")
        ba_out = sem("ba_out")
        pads_ready = sem("pads_ready")
        conv_turned = sem("conv_turned")
        cin_ready = sem("cin_ready")
        conv_done = sem("conv_done")
        silu_ready = sem("silu_ready")
        conv_back = sem("conv_back")
        sec0 = sem("sec0")
        sec1 = sem("sec1")
        beta_ready = sem("beta_ready")
        adt_ready = sem("adt_ready")
        ea_ready = sem("ea_ready")
        spe_ready = sem("spe_ready")
        gate_ready = sem("gate_ready")
        gate_summed = sem("gate_summed")
        gcs_ready = sem("gcs_ready")
        kd_sub = sem("kd_sub")
        exps_ready = sem("exps_ready")
        l2_sq = sem("l2_sq")
        l2_sum = sem("l2_sum")
        l2_ready = sem("l2_ready")
        qn_ready = sem("qn_ready")
        kn_ready = sem("kn_ready")
        kb_ready = sem("kb_ready")
        v_ready = sem("v_ready")
        kbg_ready = sem("kbg_ready")
        kdec_ready = sem("kdec_ready")
        diag_ready = sem("diag_ready")
        qk2_turned = sem("qk2_turned")
        qk2_ready = sem("qk2_ready")
        rows_ready = sem("rows_ready")
        decsub_ready = sem("decsub_ready")
        decay_ready = sem("decay_ready")
        gram_done = sem("gram_done")
        gram_ready = sem("gram_ready")
        level0_ready = sem("level0_ready")
        level0_turned = sem("level0_turned")
        wl_done = sem("wl_done")
        wl_ready = sem("wl_ready")
        xw_done = sem("xw_done")
        x_up = sem("x_up")
        xt_done = sem("xt_done")
        xt_up = sem("xt_up")
        glu_ready = sem("glu_ready")
        pad31_ready = sem("pad31_ready")
        c31_turned = sem("c31_turned")
        c31_in = sem("c31_in")
        c31_done = sem("c31_done")
        c_summed = sem("c_summed")
        c_centred = sem("c_centred")
        c_squared = sem("c_squared")
        c_sq_summed = sem("c_sq_summed")
        c_var = sem("c_var")
        c_rstd = sem("c_rstd")
        c_diag = sem("c_diag")
        c_spread = sem("c_spread")
        u_done = sem("u_done")
        u_ready = sem("u_ready")
        wt_done = sem("wt_done")
        wt_ready = sem("wt_ready")
        state_ready = sem("state_ready")
        sd_ready = sem("sd_ready")
        ws_done = sem("ws_done")
        vn_ready = sem("vn_ready")
        qs_ready = sem("qs_ready")
        vn_used = sem("vn_used")
        o_ready = sem("o_ready")
        osq_ready = sem("osq_ready")
        oz_ready = sem("oz_ready")
        bke_ready = sem("bke_ready")
        orst_ready = sem("orst_ready")
        o_final = sem("o_final")
        c_final = sem("c_final")
        cs_ready = sem("cs_ready")
        kx_turned = sem("kx_turned")
        kx_ready = sem("kx_ready")
        xscored = sem("xscored")
        xmax = sem("xmax")
        xprobs = sem("xprobs")
        xturned = sem("xturned")
        xpt = sem("xpt")
        xatt = sem("xatt")
        xout = sem("xout")

        PS = D // (STEP * P)
        S_IN, P_IN = 0, 0
        S_OUT, P_OUT = S_IN + 4 * PS, P_IN + 4
        S_MLP, P_MLP = S_OUT + 2 * PS, P_OUT + 2
        HALF_STEPS = 4 * PS + 2 * (HK // STEP)
        HALF_PASSES = 6
        S_IN2, P_IN2 = S_MLP + 2 * HALF_STEPS, P_MLP + 2 * HALF_PASSES
        S_KV, P_KV = S_IN2 + 6 * PS, P_IN2 + 6
        S_OUT2, P_OUT2 = S_KV + 4 * PS, P_KV + 4
        S_Q, P_Q = S_OUT2 + 2 * PS, P_OUT2 + 2
        S_O, P_O = S_Q + 2 * PS, P_Q + 2
        S_MLP2, P_MLP2 = S_O + 2 * PS, P_O + 2
        GROUPS = [0, 1] * ((P_IN2 + 4) // 2) + [0, 0] + [0, 0, 1, 0] + [1, 0] * 3 + [0, 1] * HALF_PASSES
        S_END = S_MLP2 + 2 * HALF_STEPS
        C31_TAPS = [0, 0, 0, 1, 1, 2, 2, 1] + [1] * PS + [1] * PS + [1, 1, 1, 1, 1, 1, 0, 1] + [1]
        assert sum(C31_TAPS) == DW

        def level_part(k, j):
            n = 2 * (k - 1) + j
            return (1 + n // 3, n % 3) if n < 3 * (LEVELS - 2) else (LEVELS - 1, (0, 2)[n - 3 * (LEVELS - 2)])

        GLU0 = 4 * COLS + NBA
        IN_COLS = [1, 2, 3, 0]
        IN2_COLS = [0, COLS, 2 * COLS, 3 * COLS, GLU0, GLU0 + COLS]
        (H_IN, H_OUT, H_MLP, H_IN2, H_MEM, H_OUT2, H_XQ, H_XO, H_MLP2) = range(9)
        (N_IN, N_ATT, N_POOL, N_MLP, N_F1, N_IN2, N_MEM, N_XQ, N_MLP2, N_F2) = range(NORMS)
        G_IN, G_OUT, G_MLP, G_IN2, G_XQ, G_MEM, G_MLP2, G_F1 = 0, 16, 32, 48, 64, 80, 96, 112
        G_DN = P + CONV * QK_TILES + 3 * HEADS

        def gain(k):
            return VEC[:, k // P, k % P:k % P + 1]

        def rstd_of(n, t):
            return rstd[:, TT * n + t:TT * n + t + 1]

        def tap(j, c):
            return VEC[:, 1, j * QK_TILES + c:j * QK_TILES + c + 1]

        def dw_vec(n, c):
            k = CONV * QK_TILES + n * HEADS + c
            return VEC[:, 1, k:k + 1]

        def dw_tap(j, c):
            k = j * HEADS + c
            return VEC[:, 2 + k // 124, k % 124:k % 124 + 1]

        def blocks(w):
            return w.rearrange("(s j p) n -> s p j n", j=STEP, p=P)

        block = ctx.enter_context(nc.Block())

        @block.sync
        def _(sp):
            sp.dma_start(VEC_RAW[:], vectors.rearrange("n r c -> r n c")).then_inc(vec_landed, 16)
            sp.dma_start(SQ[:, 0, :], squares[:, 0, :]).then_inc(ident_landed, 16)

            def load(s, src, off=0):
                if s >= NRAW:
                    sp.wait_ge(hi_ready, s + off - NRAW + 1)
                    sp.wait_ge(lo_ready, s + off - NRAW + 1)
                sp.dma_start(RAW[:, s % NRAW], src).then_inc(raw_landed[s % NRAW], 16)

            def load_pass(s0, w, c0, first=0):
                for k in range(PS):
                    load(s0 + k, blocks(w)[(first + k) % PS, :, :, c0:c0 + COLS])

            def load_x(n):
                cols = slice(n * COLS, (n + 1) * COLS)
                sp.dma_start(X[:, :, cols], x.rearrange("(t p) d -> p t d", p=P)[:, :, cols]).then_inc(x_landed[n], 16)

            def load_mlp(s0, up, down):
                with sp.Fori(0, 2) as half:
                    off = half * HALF_STEPS
                    for p in range(4):
                        for k in range(PS):
                            load(s0 + p * PS + k, blocks(up)[k, :, :, bass.ds(half * HALF + p * COLS, COLS)], off)
                    rows = down.rearrange("(h s j p) n -> h s p j n", h=2, j=STEP, p=P)
                    for d in range(2):
                        for k in range(HK // STEP):
                            load(s0 + 4 * PS + d * (HK // STEP) + k,
                                 rows[bass.ds(half, 1), k, :, :, d * COLS:(d + 1) * COLS].rearrange("h p j n -> (h p) j n"), off)

            load_x(0)
            for n in range(4):
                for k in range(PS):
                    load(S_IN + n * PS + k, blocks(w_in)[k, :, :, IN_COLS[n] * COLS:(IN_COLS[n] + 1) * COLS])
                    if (n, k) == (0, 1):
                        load_x(1)
                    elif (n, k) == (0, NRAW - 1):
                        sp.dma_start(SQ[:, 1:, :], squares[:, 1:, :]).then_inc(sq_landed, 16)
            for n in range(2):
                load_pass(S_OUT + n * PS, w_out, n * COLS, PS // 2)
            load_mlp(S_MLP, w_up, w_down)
            for n in range(6):
                load_pass(S_IN2 + n * PS, w_in2, IN2_COLS[n])
            for n in range(4):
                load_pass(S_KV + n * PS, wk if n < 2 else wv, (n % 2) * COLS)
            for n in range(2):
                load_pass(S_OUT2 + n * PS, w_out2, n * COLS)
            for n in range(2):
                load_pass(S_Q + n * PS, wq, n * COLS)
            for n in range(2):
                load_pass(S_O + n * PS, wo, n * COLS)
            load_mlp(S_MLP2, w1, w2)
            for k in range(NSPLIT):
                load(S_END + k, blocks(w1)[k, :, :, 0:COLS])
            for t in range(TT):
                sp.wait_ge(x_final, t + 1 + TT)
                sp.dma_start(out[t * P:(t + 1) * P, :], ROWS[:, t, :]).then_inc(out_landed, 16)
            sp.wait_ge(out_landed, 16 * TT)

        @block.gpsimd
        def _(pool):
            own = Own(pool, pool_own)
            pool.memset(halves[:], -0.5).then_inc(halves_ready, 1)
            pool.wait_ge(hi_ready, NRAW)
            pool.dma_start(ALIBI[:], alibi).then_inc(alibi_landed, 16)
            pool.dma_start(POOLW[:], pool_w.rearrange("g (c p) f -> p g c f", p=P)).then_inc(poolw_landed, 16)
            pool.dma_start(POOLA[:], pool_avg).then_inc(poola_landed, 16)
            pool.dma_start(alog[:], a_log.partition_broadcast(P)).then_inc(gates_landed, 16)
            pool.dma_start(dtb[:], dt_bias.partition_broadcast(P)).then_inc(gates_landed, 16)

            pool.memset(minus_ones[:], -1.0).then_inc(halves_ready, 1)

            def root(n, width, power=None, times=None):
                cols = slice(TT * n, TT * n + TT)
                power = halves[:, 0:TT] if power is None else power
                pool.wait_ge(sq_done, TT * (n + 1))
                own.mark(pool.tensor_scalar(ms[:, cols], ss[:, cols], 1.0 / width, EPS, ALU.mult, ALU.add))
                own.wait()
                pool.wait_ge(halves_ready, 2)
                last = pool.tensor_tensor(rstd[:, cols], ms[:, cols], power, ALU.pow)
                if times is not None:
                    own.mark(last)
                    own.wait()
                    last = pool.tensor_tensor(rstd[:, cols], rstd[:, cols], rstd[:, TT * times:TT * times + TT], ALU.mult)
                last.then_inc(rstd_ready, 1)

            root(N_IN, D)
            pool.wait_ge(qk_turned, 2)
            pool.dma_start(PSB[:], pool_scale.partition_broadcast(P)).then_inc(pools_landed, 16)
            root(N_ATT, COLS)
            root(N_POOL, COLS)
            pool.dma_start(BARAW[:], w_in2[:, 4 * COLS:4 * COLS + NBA].rearrange("(k p) n -> p k n", p=P)).then_inc(ba_landed, 16)
            root(N_MLP, D, minus_ones[:])
            pool.dma_start(GB[:], final_g.partition_broadcast(P)).then_inc(final_landed, 16)
            root(N_F1, D)
            root(N_IN2, D, times=N_F1)
            pool.wait_ge(x_final, TT)
            pool.dma_start(out.rearrange("(t p) d -> p t d", p=P), X[:]).then_inc(parked, 16)
            pool.memset(CIN[:, :, 0:CONV - 1], 0.0).then_inc(pads_ready, 1)
            pool.wait_ge(parked, 16)
            pool.dma_start(MEM[:], mem.rearrange("(t p) d -> p t d", p=P)).then_inc(mem_landed, 16)
            root(N_MEM, D)
            pool.wait_ge(l2_sum, 2)
            own.mark(pool.tensor_scalar(l2[:], l2[:], EPS, None, ALU.add))
            own.wait()
            for n in range(2):
                own.mark(pool.tensor_tensor(l2r[:, n, :], l2[:, n, :], halves[:, 0:U16], ALU.pow))
            own.wait()
            pool.tensor_scalar(l2r[:, 0, :], l2r[:, 0, :], float(HD) ** -0.5, None, ALU.mult).then_inc(l2_ready, 1)
            pool.wait_ge(ba_done, 1)
            pool.memset(ST[:], 0.0).then_inc(state_ready, 1)
            pool.wait_ge(turned, KT // 2 * (H_MEM + 1))
            pool.memset(CIN31[:, :, 0:DW - 1], 0.0).then_inc(pad31_ready, 1)
            pool.wait_ge(wt_done, 1)
            pool.wait_ge(exps_ready, 1)
            for n in range(T // CHUNK - 1):
                pool.wait_ge(state_ready, n + 1)
                pool.tensor_tensor(SD[:], ST[:], egl[:, n, :].unsqueeze(2).broadcast_to([P, HEADS, HD]), ALU.mult).then_inc(sd_ready, 1)
            pool.wait_ge(osq_ready, 1)
            own.mark(pool.tensor_scalar(osum[:], osum[:], 1.0 / HD, EPS, ALU.mult, ALU.add))
            own.wait()
            pool.tensor_tensor(orst[:], osum[:], halves[:, 0:U16], ALU.pow).then_inc(orst_ready, 1)
            pool.wait_ge(c31_done, 1)
            pool.dma_start(X[:], out.rearrange("(t p) d -> p t d", p=P)).then_inc(x_back, 16)
            pool.wait_ge(c_var, 1)
            pool.tensor_tensor(LN_RSTD[:], LN_VAR[:], halves[:, 0:TT], ALU.pow).then_inc(c_rstd, 1)
            root(N_XQ, D)
            root(N_MLP2, D, minus_ones[:])
            pool.dma_start(GB[:], final_g2.partition_broadcast(P)).then_inc(final_landed, 16)
            for t in range(TT):
                col = slice(TT * N_F2 + t, TT * N_F2 + t + 1)
                pool.wait_ge(sq_done, TT * N_F2 + t + 1)
                own.mark(pool.tensor_scalar(ms[:, col], ss[:, col], 1.0 / D, EPS, ALU.mult, ALU.add))
                own.wait()
                pool.tensor_tensor(rstd[:, col], ms[:, col], halves[:, 0:1], ALU.pow).then_inc(rstd_ready, 1)

        @block.tensor
        def _(pe):
            def vec_turn():
                pe.wait_ge(vec_landed, 16)
                pe.wait_ge(ident_landed, 16)
                for n in range(4):
                    last = pe.transpose(ps[:, 0, n * P:(n + 1) * P], VEC_RAW[:, n, :], IDENT)
                last.then_inc(vec_turned, 1)

            def turn8(src, half, group):
                for k in range(KT // 2 * half, KT // 2 * (half + 1)):
                    for t in range(TT):
                        b = 4 * group + (k % (KT // 2)) // 2
                        last = pe.transpose(ps[:, b, (k % 2) * T + t * P:(k % 2) * T + (t + 1) * P], src(k, t), IDENT)
                    if k % 2:
                        last.then_inc(turned, 1)

            def stationary(h, k=KT):
                pe.wait_ge(ht_hi, KT * h + k)
                pe.wait_ge(ht_lo, KT * h + k)

            def step(s, hi, lo, k, group, first, last, off=0, between=None):
                pe.wait_ge(hi_ready, s + off + 1)
                pe.wait_ge(lo_ready, s + off + 1)
                slot = s % NSPLIT
                for j in range(STEP):
                    if j and between:
                        between()
                    for t in range(TT):
                        xh = hi[:, k + j, t * P:(t + 1) * P]
                        xl = lo[:, k + j, t * P:(t + 1) * P]
                        for c in range(2):
                            o = ps[:, 4 * group + 2 * t + c, :]
                            pe.matmul(o, xh, WHI[:, slot, j, c * BANK:(c + 1) * BANK], start=first and j == 0, stop=False)
                            pe.matmul(o, xh, WLO[:, slot, j, c * BANK:(c + 1) * BANK], start=False, stop=False)
                        for c in range(2):
                            o = ps[:, 4 * group + 2 * t + c, :]
                            mm = pe.matmul(o, xl, WHI[:, slot, j, c * BANK:(c + 1) * BANK], start=False, stop=last and j == STEP - 1)
                mm.then_inc(w_used, 1)

            def bank_free(p, off=0):
                if p >= 2:
                    pe.wait_ge(out0, p + off - 1)
                    pe.wait_ge(out1, p + off - 1)

            def gemm_pass(s0, p, during=None, h=None, turn_second=None):
                before = [n for n in range(p) if GROUPS[n] == GROUPS[p]]
                if before:
                    pe.wait_ge(out0, before[-1] + 1)
                    pe.wait_ge(out1, before[-1] + 1)
                for k in range(PS):
                    if turn_second and k == 2:
                        pe.wait_ge(ht_lo, KT * h + KT // 2)
                        turn8(turn_second, 1, 1 - GROUPS[p])
                    if during:
                        during(k, 0)
                    if h is not None:
                        stationary(h, STEP * (k + 1))
                    step(s0 + k, HHI, HLO, STEP * k, GROUPS[p], k == 0, k == PS - 1,
                         between=(lambda k=k: during(k, 1)) if during else None)

            def first_pass(s0, p, h, src, during=None):
                turn8(src, 0, 1 - GROUPS[p])
                gemm_pass(s0, p, during, h, src)

            def mlp(m, s0, p0, h):
                pe.wait_ge(ht_lo, KT * h + KT // 2)
                with pe.Fori(0, 2) as half:
                    off, poff, aoff = half * HALF_STEPS, half * HALF_PASSES, half * 16

                    def turn_hidden(p):
                        pe.wait_ge(out0, p0 + p + 1 + poff)
                        pe.wait_ge(out1, p0 + p + 1 + poff)
                        g = 4 * (p % 2)
                        for b in range(4):
                            for k in range(2 * b, 2 * b + 2):
                                for t in range(TT):
                                    last = pe.transpose(ps[:, g + b, (k % 2) * T + t * P:(k % 2) * T + (t + 1) * P],
                                                        R[:, t, k * P:(k + 1) * P], IDENT)
                            last.then_inc(r_turned, 1)

                    for p in range(4):
                        bank_free(p0 + p, poff)
                        if p >= 2:
                            pe.wait_ge(at_hi, 32 * m + 4 * (p - 1) + aoff)
                            pe.wait_ge(at_lo, 32 * m + 4 * (p - 1) + aoff)
                        for k in range(PS):
                            if p >= 1 and k == 2:
                                turn_hidden(p - 1)
                            if p == 0:
                                stationary(h, STEP * (k + 1))
                            step(s0 + p * PS + k, HHI, HLO, STEP * k, p % 2, k == 0, k == PS - 1, off)
                    for d in range(2):
                        n = HK // STEP
                        bank_free(p0 + 4 + d, poff)
                        pe.wait_ge(at_hi, 32 * m + 12 + 4 * d + aoff)
                        pe.wait_ge(at_lo, 32 * m + 12 + 4 * d + aoff)
                        for k in range(n):
                            if d == 0 and k == 2:
                                turn_hidden(3)
                            if d == 0 and k == 12:
                                pe.wait_ge(at_hi, 32 * m + 16 + aoff)
                                pe.wait_ge(at_lo, 32 * m + 16 + aoff)
                            step(s0 + 4 * PS + d * n + k, AHI, ALO, STEP * k, d, k == 0, k == n - 1, off)

            vec_turn()

            def during_wq_in(k, j):
                if (k, j) == (2, 0):
                    pe.wait_ge(x_landed[1], 16)
                    pe.wait_ge(ht_lo, KT * H_IN + KT // 2)
                    turn8(residual, 1, 1)

            def residual(k, t):
                return X[:, t, k * P:(k + 1) * P]

            def left(p):
                pe.wait_ge(out0, p + 1)
                pe.wait_ge(out1, p + 1)

            pe.wait_ge(x_landed[0], 16)
            turn8(residual, 0, 1)
            pe.wait_ge(vec_ready, 1)
            gemm_pass(S_IN, P_IN, during_wq_in, H_IN)

            def turn_rows(src, group, done):
                for c in range(HEADS):
                    for t in range(TT):
                        last = pe.transpose(ps[:, 4 * group + c // 2, (c % 2) * T + t * P:(c % 2) * T + (t + 1) * P], src(c, t), IDENT)
                last.then_inc(done, 1)

            def during_wk_in(k, j):
                if (k, j) == (2, 0):
                    left(P_IN)
                    turn_rows(lambda h, t: Q_ROWS[:, t, h * HD:(h + 1) * HD], 0, qk_turned)

            def during_wv_in(k, j):
                if (k, j) == (2, 0):
                    left(P_IN + 1)
                    turn_rows(lambda h, t: K_ROWS[:, t, h * HD:(h + 1) * HD], 1, qk_turned)

            def scores(h):
                if h >= 2:
                    pe.wait_ge(max_ready, h - 1)
                pe.matmul(ps[:, h % 2, 0:P], QT[:, h, 0:P], KTT[:, h, 0:P], start=True, stop=True)
                pe.matmul(ps[:, h % 2, P:P + T], QT[:, h, P:T], KTT[:, h, :], start=True, stop=True).then_inc(scored, 1)

            def turn_probs(h):
                s = h % 2
                pe.wait_ge(probs_ready, h + 1)
                if h >= 2:
                    pe.wait_ge(y_attn, h - 1)
                pe.transpose(ps[:, 2 + s, 0:P], S1[:, s, 0:P], IDENT)
                pe.transpose(ps[:, 2 + s, P:T], S1[:, s, P:T], IDENT)
                pe.transpose(ps[:, 2 + s, T:NS], S1[:, s, T:NS], IDENT).then_inc(probs_turned, 1)

            def attend(h):
                s = h % 2
                pe.wait_ge(pt_ready, h + 1)
                v = [V_ROWS[:, t, h * HD:(h + 1) * HD] for t in range(TT)]
                pe.matmul(ps[:, 2 + s, 0:P], PT1[:, s, 0:P], v[0], start=True, stop=True)
                pe.matmul(ps[:, 2 + s, P:T], PT1[:, s, P:T], v[0], start=True, stop=False)
                pe.matmul(ps[:, 2 + s, P:T], PT1[:, s, T:NS], v[1], start=False, stop=True).then_inc(attended, 1)

            def during_u(k, j):
                pair = range(2 * (k - 2), 2 * (k - 2) + 2)
                if j == 0 and 2 <= k < 2 + HEADS // 2:
                    for h in pair:
                        turn_probs(h)
                if j == 0 and 1 <= k < 1 + HEADS // 2:
                    if k == 1:
                        left(P_IN + 2)
                    for h in pair:
                        scores(h + 2)
                if j == 1 and 2 <= k < 2 + HEADS // 2:
                    for h in pair:
                        attend(h)
                if (k, j) == (PS - 1, 0):
                    pe.wait_ge(y_attn, HEADS)
                    pe.wait_ge(y_ready, 1)
                    turn8(lambda k, t: Q_ROWS[:, t, k * P:(k + 1) * P], 0, 0)

            gemm_pass(S_IN + PS, P_IN + 1, during_wk_in)
            pe.wait_ge(qt_ready, 1)
            gemm_pass(S_IN + 2 * PS, P_IN + 2, during_wv_in)
            pe.wait_ge(kt_ready, 1)
            gemm_pass(S_IN + 3 * PS, P_IN + 3, during_u)

            def during_out_a(k, j):
                if (k, j) == (1, 0):
                    left(P_IN + 3)
                    pe.wait_ge(poola_landed, 16)
                    for n in range(2 * len(WINDOWS)):
                        for t in range(TT):
                            last = pe.matmul(ps[:, 4 + n // 2, (n % 2) * T:(n % 2 + 1) * T], U_ROWS[:, t, n * P:(n + 1) * P],
                                             POOLA[:, n // 2, t, :], start=t == 0, stop=t == TT - 1)
                    last.then_inc(pooled, 1)
                elif (k, j) == (2, 0):
                    pe.wait_ge(pooled_ready, 1)
                    pe.wait_ge(poolw_landed, 16)
                    for t in range(TT):
                        for g in range(len(WINDOWS)):
                            for c in range(2):
                                last = pe.matmul(ps[:, 4 + 2 * t + g // 2, (g % 2) * GROUP:(g % 2 + 1) * GROUP],
                                                 DT[:, 2 * g + c, t * P:(t + 1) * P], POOLW[:, g, c, :], start=c == 0, stop=c == 1)
                    last.then_inc(pool_out, 1)
                elif (k, j) == (4, 0):
                    pe.wait_ge(y_ready, 2)
                    turn8(lambda k, t: U_ROWS[:, t, (k - HEADS) * P:(k - HEADS + 1) * P], 1, 1)

            def during_out_b(k, j):
                if (k, j) == (6, 0):
                    left(P_OUT)
                    turn8(residual, 0, 0)

            pe.wait_ge(ht_lo, KT * H_OUT + KT // 2)
            gemm_pass(S_OUT, P_OUT, during_out_a, H_OUT)
            gemm_pass(S_OUT + PS, P_OUT + 1, during_out_b)
            left(P_OUT + 1)
            turn8(residual, 1, 1)
            mlp(0, S_MLP, P_MLP, H_MLP)

            def turn_back(src, group, done):
                for t in range(TT):
                    for c in range(HEADS):
                        last = pe.transpose(ps[:, 4 * group + 2 * t + c // 4, (c % 4) * P:(c % 4 + 1) * P], src[:, c, t * P:(t + 1) * P], IDENT)
                last.then_inc(done, 1)

            def units(lhs, rhs):
                for u in range(U16):
                    last = pe.matmul(ps[:, 4 + u // 4, (u % 4) * P:(u % 4 + 1) * P], lhs[:, u, :], rhs[:, u, :], start=True, stop=True)
                return last

            def during_q(k, j):
                if (k, j) == (PS - 2, 0):
                    stationary(H_IN2)
                    pe.wait_ge(ba_split, 2)
                    for f in range(KT):
                        o = ps[0:NBA, 4, 0:T]
                        pe.matmul(o, BAHI[:, f, :], HHI[:, f, :], start=f == 0, stop=False)
                        pe.matmul(o, BALO[:, f, :], HHI[:, f, :], start=False, stop=False)
                        last = pe.matmul(o, BAHI[:, f, :], HLO[:, f, :], start=False, stop=f == KT - 1)
                    last.then_inc(ba_done, 1)
                elif (k, j) == (PS - 1, 0):
                    pe.wait_ge(ba_columns, 1)
                    for t in range(TT):
                        last = pe.transpose(ps[:, 5, t * NBA:(t + 1) * NBA], BAT[0:NBA, t * P:(t + 1) * P], IDENT[0:NBA, 0:NBA])
                    last.then_inc(ba_turned, 1)

            def during_k(k, j):
                if (k, j) == (2, 0):
                    left(P_IN2)
                    turn_rows(lambda c, t: QTOK[:, t, c * P:(c + 1) * P], 0, conv_turned)
                elif (k, j) == (5, 0):
                    pe.wait_ge(cin_ready, 1)
                    pe.wait_ge(gate_ready, 1)
                    pe.wait_ge(sq_landed, 16)
                    G16 = gate[:].rearrange("p t h -> p (t h)")
                    pe.matmul(ps[:, 0, 0:U16], TRI, G16, start=True, stop=True)
                    pe.matmul(ps[:, 0, 16:16 + U16], SAME, G16, start=True, stop=True)
                    for n in range(T // CHUNK):
                        r = CHUNK * (n % 2)
                        last = pe.matmul(ps[:, n % 2, 32 + n // 2 * HEADS:32 + (n // 2 + 1) * HEADS], ONES[r:r + CHUNK, :],
                                         gate[r:r + CHUNK, n // 2, :], start=True, stop=True)
                    last.then_inc(gate_summed, 1)

            def during_v(k, j):
                if (k, j) == (1, 0):
                    left(P_IN2 + 1)
                    pe.wait_ge(silu_ready, 1)
                    turn_back(COUT, 1, conv_back)
                elif (k, j) == (2, 0):
                    pe.wait_ge(sec0, 1)
                    pe.wait_ge(sec1, 1)
                    turn_rows(lambda c, t: KTOK[:, t, c * P:(c + 1) * P], 1, conv_turned)

            def during_z(k, j):
                if (k, j) == (1, 0):
                    left(P_IN2 + 2)
                    pe.wait_ge(silu_ready, 2)
                    turn_back(COUT, 0, conv_back)
                elif (k, j) == (2, 0):
                    pe.wait_ge(sec0, 2)
                    pe.wait_ge(sec1, 2)
                    turn_rows(lambda c, t: VTOK[:, t, c * P:(c + 1) * P], 0, conv_turned)

            def during_ga(k, j):
                if j:
                    return
                if k == 1:
                    left(P_IN2 + 3)
                    pe.wait_ge(silu_ready, 3)
                    turn_back(COUT, 1, conv_back)
                elif k == 2:
                    pe.wait_ge(sec0, 3)
                    pe.wait_ge(sec1, 3)
                    pe.wait_ge(qn_ready, 1)
                    turn_rows(lambda h, t: QTOK[:, t, h * HD:(h + 1) * HD], 1, qk2_turned)
                elif k == 3:
                    pe.wait_ge(qk2_ready, 1)
                    pe.wait_ge(kn_ready, 1)
                    turn_rows(lambda h, t: KTOK[:, t, h * HD:(h + 1) * HD], 1, qk2_turned)
                elif k == 4:
                    pe.wait_ge(qk2_ready, 2)
                    pe.wait_ge(kb_ready, 1)
                    turn_rows(lambda h, t: KB_[:, t, h, :], 1, qk2_turned)
                elif k == 5:
                    pe.wait_ge(qk2_ready, 3)
                    pe.wait_ge(diag_ready, 1)
                    for b in range(4):
                        last = pe.matmul(ps[:, 4 + b, :], ONES, DIAG[:, 4 * b:4 * b + 4, :].rearrange("p u c -> p (u c)"), start=True, stop=True)
                    last.then_inc(rows_ready, 1)
                elif k in (6, 7):
                    if k == 6:
                        pe.wait_ge(decsub_ready, 1)
                    else:
                        pe.wait_ge(gram_ready, 1)
                    with_ = KBT if k == 6 else QT2
                    for u in range(U16):
                        t, h = u // HEADS, u % HEADS
                        last = pe.matmul(ps[:, 4 + u // 4, (u % 4) * P:(u % 4 + 1) * P],
                                         KT2[:, h, t * P:(t + 1) * P], with_[:, h, t * P:(t + 1) * P], start=True, stop=True)
                    last.then_inc(gram_done, 1)

            def during_gb(k, j):
                if (k, j) == (0, 1):
                    pe.wait_ge(gram_ready, 2)
                    pe.wait_ge(level0_ready, 1)
                    for u in range(U16):
                        last = pe.transpose(ps[:, 4 + u // 4, (u % 4) * P:(u % 4 + 1) * P], WL[:, u, :], IDENT)
                    last.then_inc(level0_turned, 1)
                elif k >= 1:
                    lv, part = level_part(k, j)
                    if part == 0:
                        pe.wait_ge(x_up, lv)
                        pe.wait_ge(xt_up, lv)
                        units(LT, XI).then_inc(wl_done, 1)
                    elif part == 1:
                        pe.wait_ge(wl_ready, lv)
                        units(XT, WL).then_inc(xw_done, 1)
                    else:
                        pe.wait_ge(wl_ready, lv)
                        if lv < LEVELS - 1:
                            pe.wait_ge(x_up, lv + 1)
                        units(WL, XT).then_inc(xt_done, 1)

            def during_wk0(k, j):
                if j:
                    return
                if k == 3:
                    pe.wait_ge(ht_lo, KT * (H_MEM + 1))
                    pe.wait_ge(glu_ready, 1)
                    turn_rows(lambda c, t: GA[:, t, c * P:(c + 1) * P], 1, c31_turned)
                elif k == 4:
                    pe.wait_ge(c31_in, 1)
                    pe.wait_ge(v_ready, 1)
                    for u in range(U16):
                        t, h = u // HEADS, u % HEADS
                        last = pe.matmul(ps[:, 4 + u // 4, (u % 4) * P:(u % 4 + 1) * P], XT[:, u, :], VTOK[:, t, h * HD:(h + 1) * HD], start=True, stop=True)
                    last.then_inc(u_done, 1)
                elif k == 5:
                    pe.wait_ge(u_ready, 1)
                    pe.wait_ge(kbg_ready, 1)
                    for h in range(HEADS):
                        for t in range(TT):
                            last = pe.matmul(ps[:, 4 + h // 2, (h % 2) * T + t * P:(h % 2) * T + (t + 1) * P],
                                             KBG[:, t, h, :], XT[:, t * HEADS + h, :], start=True, stop=True)
                    last.then_inc(wt_done, 1)

            def during_wk1(k, j):
                if j:
                    return
                n = k // 2
                t, r = n // 2, CHUNK * (n % 2)
                rows = slice(r, r + CHUNK)
                if k % 2 == 0:
                    if n == 0:
                        pe.wait_ge(wt_ready, 1)
                    else:
                        pe.wait_ge(o_ready, n)
                    pe.wait_ge(state_ready, n + 1)
                    for h in range(HEADS):
                        pe.matmul(ps[rows, 4 + h // 4, (h % 4) * P:(h % 4 + 1) * P], WT[:, h, t * P + r:t * P + r + CHUNK], ST[:, h, :], start=True, stop=True)
                    for h in range(HEADS):
                        last = pe.matmul(ps[rows, 6 + h // 4, (h % 4) * P:(h % 4 + 1) * P], QT2[:, h, t * P + r:t * P + r + CHUNK], ST[:, h, :], start=True, stop=True)
                    last.then_inc(ws_done, 1)
                else:
                    pe.wait_ge(kdec_ready, 1)
                    pe.wait_ge(vn_ready, n + 1)
                    pe.wait_ge(qs_ready, n + 1)
                    for h in range(HEADS):
                        pe.matmul(ps[:, 4 + h // 4, (h % 4) * P:(h % 4 + 1) * P], KTOK[rows, t, h * HD:(h + 1) * HD], U[rows, t, h, :], start=True, stop=True)
                    for h in range(HEADS):
                        last = pe.matmul(ps[rows, 6 + h // 4, (h % 4) * P:(h % 4 + 1) * P], ATT[rows, t * HEADS + h, r:r + CHUNK], U[rows, t, h, :], start=True, stop=True)
                    last.then_inc(vn_used, 1)

            def during_wv1(k, j):
                if (k, j) == (6, 0):
                    left(P_KV + 2)
                    pe.wait_ge(o_final, 1)
                    turn8(lambda k, t: O[:, t, k, :], 0, 1)

            def during_out0(k, j):
                if (k, j) == (2, 0):
                    left(P_KV + 3)
                    pe.wait_ge(c31_done, 1)
                    for c in range(HEADS):
                        last = pe.matmul(ps[:, 0, 0:T], ONES, COUT31[:, c, :], start=c == 0, stop=c == HEADS - 1)
                    last.then_inc(c_summed, 1)
                elif (k, j) == (3, 0):
                    pe.wait_ge(c_squared, 1)
                    for t in range(TT):
                        for c in range(HEADS):
                            last = pe.matmul(ps[:, 1 + t, 0:2], CSQ[:, c, t * P:(t + 1) * P], ONES[:, 0:2], start=c == 0, stop=c == HEADS - 1)
                    last.then_inc(c_sq_summed, 1)
                elif (k, j) == (3, 1):
                    pe.wait_ge(c_diag, 1)
                    pe.matmul(ps[:, 3, 0:T], ONES, LN_DIAG[:].rearrange("p t c -> p (t c)"), start=True, stop=True).then_inc(c_spread, 1)

            def during_out1(k, j):
                if (k, j) == (2, 0):
                    left(P_OUT2)
                    turn_rows(lambda c, t: K_0[:, t, c * P:(c + 1) * P], 1, kx_turned)
                elif (k, j) == (4, 0):
                    pe.wait_ge(kx_ready, 1)
                    turn_rows(lambda c, t: K_1[:, t, c * P:(c + 1) * P], 1, kx_turned)
                elif (k, j) == (6, 0):
                    pe.wait_ge(kx_ready, 2)
                    turn8(residual, 0, 1)

            def during_wq0(k, j):
                if (k, j) == (2, 0):
                    left(P_OUT2 + 1)
                    turn8(residual, 1, 0)

            left(P_IN2 - 2)
            turn8(residual, 0, 0)
            left(P_IN2 - 1)
            turn8(residual, 1, 1)
            pe.wait_ge(ht_lo, KT * H_IN2 + KT // 2)
            gemm_pass(S_IN2, P_IN2, during_q, H_IN2)
            pe.wait_ge(ba_out, 1)
            gemm_pass(S_IN2 + PS, P_IN2 + 1, during_k)
            pe.wait_ge(gcs_ready, 1)
            pe.wait_ge(kd_sub, 1)
            gemm_pass(S_IN2 + 2 * PS, P_IN2 + 2, during_v)
            pe.wait_ge(cin_ready, 2)
            gemm_pass(S_IN2 + 3 * PS, P_IN2 + 3, during_z)
            pe.wait_ge(cin_ready, 3)
            gemm_pass(S_IN2 + 4 * PS, P_IN2 + 4, during_ga)
            gemm_pass(S_IN2 + 5 * PS, P_IN2 + 5, during_gb)
            pe.wait_ge(xt_up, LEVELS)
            pe.wait_ge(mem_ready, 2)
            first_pass(S_KV, P_KV, H_MEM, lambda k, t: MEM[:, t, k * P:(k + 1) * P], during_wk0)
            gemm_pass(S_KV + PS, P_KV + 1, during_wk1)
            pe.wait_ge(o_ready, T // CHUNK)
            gemm_pass(S_KV + 2 * PS, P_KV + 2)
            gemm_pass(S_KV + 3 * PS, P_KV + 3, during_wv1)
            pe.wait_ge(ht_lo, KT * H_OUT2 + KT // 2)
            gemm_pass(S_OUT2, P_OUT2, during_out0, H_OUT2)
            gemm_pass(S_OUT2 + PS, P_OUT2 + 1, during_out1)

            pe.wait_ge(ht_lo, KT * H_XQ + KT // 2)
            gemm_pass(S_Q, P_Q, during_wq0, H_XQ)

            def xscores(h, b0):
                for q in range(TT):
                    for d in range(XDT):
                        last = pe.matmul(ps[:, b0 + h % 2, q * T:(q + 1) * T], QXT[:, XDT * h + d, q * P:(q + 1) * P],
                                         KXT[:, XDT * h + d, :], start=d == 0, stop=d == XDT - 1)
                last.then_inc(xscored, 1)

            def xturn(h, b0):
                pe.wait_ge(xprobs, h + 1)
                for k in range(TT):
                    for q in range(TT):
                        last = pe.transpose(ps[:, b0 + 2 + h % 2, k * T + q * P:k * T + (q + 1) * P], PX[:, h % 2, q, k * P:(k + 1) * P], IDENT)
                last.then_inc(xturned, 1)

            def xattend(h, b0):
                pe.wait_ge(xpt, h + 1)
                for q in range(TT):
                    for k in range(TT):
                        last = pe.matmul(ps[:, b0 + 2 * (h % 2) + q, :], PXT[:, h % 2, k, q * P:(q + 1) * P],
                                         (V_0, V_1)[h // 2][:, k, (h % 2) * XHD:(h % 2 + 1) * XHD], start=k == 0, stop=k == TT - 1)
                last.then_inc(xatt, 1)

            def during_wq1(k, j):
                if j:
                    return
                if k == 2:
                    left(P_Q)
                    turn_rows(lambda c, t: QX[:, t, c * P:(c + 1) * P], 1, kx_turned)
                elif k == 3:
                    pe.wait_ge(kx_ready, 3)
                    xscores(0, 4)
                    xscores(1, 4)
                elif k == 5:
                    xturn(0, 4)
                    xturn(1, 4)
                elif k == 6:
                    xattend(0, 4)
                elif k == 7:
                    xattend(1, 4)

            def during_wo0(k, j):
                if j:
                    return
                if k == 1:
                    pe.wait_ge(kx_ready, 4)
                    xscores(2, 0)
                    xscores(3, 0)
                elif k == 2:
                    xturn(2, 0)
                    xturn(3, 0)
                elif k == 3:
                    xattend(2, 0)
                    xattend(3, 0)
                elif k == 4:
                    pe.wait_ge(xout, XHEADS)
                    turn8(lambda k, t: QX[:, t, k * P:(k + 1) * P], 1, 0)

            def during_wo1(k, j):
                if (k, j) == (6, 0):
                    left(P_O)
                    turn8(residual, 0, 1)

            gemm_pass(S_Q + PS, P_Q + 1, during_wq1)
            pe.wait_ge(xout, 2)
            turn8(lambda k, t: QX[:, t, k * P:(k + 1) * P], 0, 1)
            left(P_Q + 1)
            turn_rows(lambda c, t: QX[:, t, COLS + c * P:COLS + (c + 1) * P], 0, kx_turned)
            pe.wait_ge(ht_lo, KT * H_XO + KT // 2)
            gemm_pass(S_O, P_O, during_wo0, H_XO)
            gemm_pass(S_O + PS, P_O + 1, during_wo1)
            left(P_O + 1)
            pe.wait_ge(ht_lo, KT * H_MLP2 + KT // 2)
            turn8(residual, 1, 1)
            mlp(1, S_MLP2, P_MLP2, H_MLP2)

        @block.scalar
        def _(act):
            own = Own(act, act_own)

            def split(s, off=0):
                act.wait_ge(raw_landed[s % NRAW], 16 * (s // NRAW + 1) + off * (16 // NRAW))
                if s >= NSPLIT:
                    act.wait_ge(w_used, s + off - NSPLIT + 1)
                act.activation(WHI[:, s % NSPLIT], RAW[:, s % NRAW], ACT.Copy).then_inc(hi_ready, 1)

            def squares_of(src, n, junk=JUNK):
                for t in range(TT):
                    act.activation(junk[:, t, :], src[:, t, :], ACT.Square, accum_out=ss[:, TT * n + t:TT * n + t + 1]).then_inc(sq_done, 1)

            def split_turned(h, g, half, group):
                for k in range(KT // 2 * half, KT // 2 * (half + 1)):
                    missing = HEADS // 2 if h > H_OUT2 else 0
                    act.wait_ge(turned, KT // 2 * h + k // 2 + 1 - missing)
                    v = ps[:, 4 * group + (k % 8) // 2, (k % 2) * T:(k % 2 + 1) * T]
                    if g is None:
                        act.activation(HHI[:, k, :], v, ACT.Copy).then_inc(ht_hi, 1)
                    else:
                        act.activation(HHI[:, k, :], v, ACT.Copy, scale=gain(g(k))).then_inc(ht_hi, 1)

            def left(s_end, p, t, dst, func=ACT.Copy, norm=None):
                act.wait_ge(w_used, s_end)
                g = 4 * GROUPS[p] + 2 * t
                scale = 1.0
                if norm is not None:
                    act.wait_ge(rstd_ready, norm + 1)
                    scale = rstd_of(norm, t)
                act.activation(dst, ps[:, g:g + 2, :].rearrange("p b n -> p (b n)"), func, scale=scale).then_inc((out0, out1)[t], 1)

            def ahead(s0):
                for k in range(NSPLIT):
                    split(s0 + k)

            def mlp(m, s0, p0, norm):
                act.wait_ge(rstd_ready, norm + 1)
                with act.Fori(0, 2) as half:
                    off, roff = half * HALF_STEPS, half * 16

                    def relu(p):
                        act.wait_ge(w_used, s0 + (p + 1) * PS + off)
                        if p >= 1:
                            act.wait_ge(r_turned, 32 * m + 4 * p + roff)
                        g = 4 * (p % 2)
                        for t in range(TT):
                            act.activation(R[:, t, :], ps[:, g + 2 * t:g + 2 * t + 2, :].rearrange("p b n -> p (b n)"), ACT.Relu,
                                           scale=rstd_of(norm, t)).then_inc(relu_done, 1)

                    def hidden_hi(p):
                        g = 4 * (p % 2)
                        for b in range(4):
                            act.wait_ge(r_turned, 32 * m + 4 * p + b + 1 + roff)
                            act.activation(AHI[:, 8 * p + 2 * b:8 * p + 2 * b + 2, :].rearrange("p k t -> p (k t)"), ps[:, g + b, :], ACT.Copy).then_inc(at_hi, 1)

                    for k in range(NSPLIT, HALF_STEPS + NSPLIT):
                        split(s0 + k, off)
                        p = k // PS - 1
                        if 0 <= p < 4 and k % PS == 1:
                            relu(p)
                        elif 0 <= p < 4 and k % PS == 3:
                            hidden_hi(p)

            def probs(h):
                s = h % 2
                act.wait_ge(max_ready, h + 1)
                act.activation(S1[:, s, 0:P], S1[:, s, 0:P], ACT.Exp, bias=nmax[:, s, 0:1], accum_out=den[:, h, 0:1])
                act.activation(S1[:, s, P:NS], S1[:, s, P:NS], ACT.Exp, bias=nmax[:, s, 1:2], accum_out=den[:, h, 1:2]).then_inc(probs_ready, 1)

            def turned_probs(h):
                s = h % 2
                act.wait_ge(probs_turned, h + 1)
                if h >= 2:
                    act.wait_ge(attended, h - 1)
                act.activation(PT1[:, s, :], ps[:, 2 + s, 0:NS], ACT.Copy).then_inc(pt_ready, 1)

            act.wait_ge(vec_ready, 1)
            for n in range(4):
                for k in range(PS):
                    if (n, k) == (0, 0):
                        split_turned(H_IN, lambda k: G_IN + k, 0, 1)
                    split(S_IN + n * PS + k)
                    if (n, k) == (0, 2):
                        split_turned(H_IN, lambda k: G_IN + k, 1, 1)
                    elif (n, k) == (0, 3):
                        for n_x in range(2):
                            act.wait_ge(x_landed[n_x], 16)
                        squares_of(X, N_IN)
                    elif n > 0 and k == 1:
                        left(S_IN + n * PS, P_IN + n - 1, 0, PROJ[:, IN_COLS[n - 1], 0, :], norm=N_IN)
                    elif n in (1, 2) and k == 3:
                        act.wait_ge(qk_turned, n)
                        dst, g = ((QT, 0), (KTT, 4))[n - 1]
                        act.activation(dst[:].rearrange("p h t -> p (h t)"), ps[:, g:g + 4, :].rearrange("p b n -> p (b n)"), ACT.Copy).then_inc((qt_ready, kt_ready)[n - 1], 1)
                    if n == 3 and 2 <= k < 2 + HEADS // 2:
                        for h in range(2 * k - 4, 2 * k - 2):
                            turned_probs(h)
                    if n == 3 and 1 <= k < 1 + HEADS // 2:
                        for h in range(2 * k - 2, 2 * k):
                            probs(h)
                    if (n, k) == (3, 6):
                        act.wait_ge(y_attn, HEADS)
                        for t in range(TT):
                            act.activation(QT[:, 4 * t:4 * t + 4, :].rearrange("p h t -> p (h t)"), Q_ROWS[:, t, :], ACT.Square,
                                           accum_out=ss[:, TT * N_ATT + t:TT * N_ATT + t + 1]).then_inc(sq_done, 1)
                    elif (n, k) == (3, 7):
                        split_turned(H_OUT, lambda k: G_OUT + k, 0, 0)
            ahead(S_OUT)
            left(S_IN + 4 * PS, P_IN + 3, 0, U_ROWS[:, 0, :], norm=N_IN)
            for n in range(2):
                for k in range(PS):
                    if n > 0 or k >= NSPLIT:
                        split(S_OUT + n * PS + k)
                    if (n, k) == (0, 2):
                        act.wait_ge(pooled, 1)
                        act.activation(DT[:].rearrange("p h t -> p (h t)"), ps[:, 4:8, :].rearrange("p b n -> p (b n)"), ACT.Copy).then_inc(pooled_ready, 1)
                    elif (n, k) == (0, 3):
                        act.wait_ge(y_pool, 1)
                        for t in range(TT):
                            act.activation(DT[:, 4 * t:4 * t + 4, :].rearrange("p h t -> p (h t)"), U_ROWS[:, t, :], ACT.Square,
                                           accum_out=ss[:, TT * N_POOL + t:TT * N_POOL + t + 1]).then_inc(sq_done, 1)
                    elif (n, k) == (0, 4):
                        split_turned(H_OUT, lambda k: G_OUT + k, 1, 1)
                    elif (n, k) == (1, 7):
                        split_turned(H_MLP, lambda k: G_MLP + k, 0, 0)
            ahead(S_MLP)
            act.wait_ge(out1, P_OUT + 2)
            squares_of(X, N_MLP)
            split_turned(H_MLP, lambda k: G_MLP + k, 1, 1)
            mlp(0, S_MLP, P_MLP, N_MLP)
            act.wait_ge(ba_landed, 16)
            act.activation(BAHI[:], BARAW[:], ACT.Copy).then_inc(ba_split, 1)
            flat_low = ps[:, 0:4, :].rearrange("p b n -> p (b n)")
            flat_high = ps[:, 4:8, :].rearrange("p b n -> p (b n)")

            def conv_load(n, group):
                act.wait_ge(conv_turned, n + 1)
                act.wait_ge(pads_ready, 1)
                if n >= 1:
                    act.wait_ge(conv_done, n)
                act.activation(CIN[:, :, CONV - 1:], ps[:, 4 * group:4 * group + 4, :].rearrange("p b (c t) -> p (b c) t", t=T), ACT.Copy).then_inc(cin_ready, 1)

            def conv_silu(n):
                act.wait_ge(conv_done, n + 1)
                act.activation(COUT[:], COUT[:], ACT.Silu).then_inc(silu_ready, 1)

            def conv_store(n, dst, group):
                act.wait_ge(conv_back, n + 1)
                act.activation(dst[:, 0, :], ps[:, 4 * group:4 * group + 2, :].rearrange("p b n -> p (b n)"), ACT.Copy).then_inc(sec0, 1)

            def square_heads(n, src):
                act.wait_ge(sec0, n + 1)
                act.wait_ge(sec1, n + 1)
                if n >= 1:
                    act.wait_ge(l2_sum, n)
                act.activation(SQT[:].rearrange("p t h d -> p (t h d)"), src.rearrange("p t d -> p (t d)"), ACT.Square).then_inc(l2_sq, 1)

            for half in range(2):
                split_turned(H_IN2, lambda k: G_IN2 + k, half, half)
            for k in range(NSPLIT, PS):
                split(S_IN2 + k)
                if k == 2:
                    act.wait_ge(out1, P_IN2)
                    squares_of(X, N_F1, ROWS)
                elif k == 4:
                    act.wait_ge(x_final, TT)
                    squares_of(X, N_IN2)
            for k in range(PS):
                split(S_IN2 + PS + k)
                if k == 0:
                    left(S_IN2 + PS, P_IN2, 0, QTOK[:, 0, :], norm=N_IN2)
                elif k == 1:
                    act.wait_ge(ba_out, 1)
                    act.activation(beta[:], ba[:, :, 0:HEADS], ACT.Sigmoid).then_inc(beta_ready, 1)
                    act.wait_ge(gates_landed, 32)
                    act.activation(alog[:], alog[:], ACT.Exp).then_inc(ea_ready, 1)
                    act.wait_ge(adt_ready, 1)
                    act.activation(sp_e[:], sp_e[:], ACT.Exp, scale=-1.0).then_inc(spe_ready, 1)
                elif k == 3:
                    conv_load(0, 0)
                elif k == 5:
                    act.wait_ge(gate_summed, 1)
                    act.activation(egl[:].rearrange("p (t b) h -> p b t h", b=2), ps[:, 0:2, 32:48].rearrange("p b (t h) -> p b t h", h=HEADS), ACT.Exp)
                    act.activation(gcs[:].rearrange("p t h -> p (t h)"), ps[:, 0, 0:U16], ACT.Copy).then_inc(gcs_ready, 1)
                    act.wait_ge(gcs_ready, 1)
                    act.activation(eg[:], gcs[:], ACT.Exp)
                elif k == 6:
                    act.wait_ge(kd_sub, 1)
                    act.activation(kd[:], kd[:], ACT.Exp).then_inc(exps_ready, 1)
                elif k == 7:
                    conv_silu(0)
            for k in range(PS):
                split(S_IN2 + 2 * PS + k)
                if k == 0:
                    left(S_IN2 + 2 * PS, P_IN2 + 1, 0, KTOK[:, 0, :], norm=N_IN2)
                elif k == 1:
                    conv_store(0, QTOK, 1)
                elif k == 3:
                    conv_load(1, 1)
                    square_heads(0, QTOK)
                elif k in (4, 5):
                    act.wait_ge(mem_landed, 16)
                    if k == 5:
                        act.wait_ge(sq_done, TT * N_MEM + 1)
                    act.activation(MEM_JUNK[:], MEM[:, k - 4, :], ACT.Square, accum_out=ss[:, TT * N_MEM + k - 4:TT * N_MEM + k - 3]).then_inc(sq_done, 1)
                elif k == 7:
                    conv_silu(1)
            for k in range(PS):
                split(S_IN2 + 3 * PS + k)
                if k == 0:
                    left(S_IN2 + 3 * PS, P_IN2 + 2, 0, VTOK[:, 0, :], norm=N_IN2)
                elif k == 1:
                    conv_store(1, KTOK, 0)
                elif k == 3:
                    conv_load(2, 0)
                    square_heads(1, KTOK)
                elif k == 7:
                    conv_silu(2)
            for k in range(PS):
                split(S_IN2 + 4 * PS + k)
                if k == 0:
                    for t in range(TT):
                        left(S_IN2 + 4 * PS, P_IN2 + 3, t, ZTOK[:, t, :], ACT.Silu, N_IN2)
                elif k == 1:
                    conv_store(2, VTOK, 1)
                elif k in (2, 3, 4):
                    act.wait_ge(qk2_turned, k - 1)
                    dst = (QT2, KT2, KBT)[k - 2]
                    act.activation(dst[:].rearrange("p h t -> p (h t)"), flat_high, ACT.Copy).then_inc(qk2_ready, 1)
                elif k == 6:
                    act.wait_ge(decsub_ready, 1)
                    act.activation(DEC[:], DEC[:], ACT.Exp).then_inc(decay_ready, 1)
            for k in range(PS):
                split(S_IN2 + 5 * PS + k)
                if k == 0:
                    left(S_IN2 + 5 * PS, P_IN2 + 4, 0, GA[:, 0, :], norm=N_IN2)
            for k in range(PS):
                split(S_KV + k)
                if k == 0:
                    for t in range(TT):
                        left(S_KV, P_IN2 + 5, t, GBT[:, t, :], ACT.Sigmoid, N_IN2)
                    split_turned(H_MEM, lambda k: G_MEM + k, 0, 1)
                elif k == 2:
                    split_turned(H_MEM, lambda k: G_MEM + k, 1, 1)
                elif k == 3:
                    act.wait_ge(c31_turned, 1)
                    act.wait_ge(pad31_ready, 1)
                    act.activation(CIN31[:, :, DW - 1:], ps[:, 4:8, :].rearrange("p b (c t) -> p (b c) t", t=T), ACT.Copy).then_inc(c31_in, 1)
                    act.wait_ge(bke_ready, 1)
                    for t in range(TT):
                        for h in range(HEADS):
                            last = act.activation(KBG[:, t, h, :], KTOK[:, t, h * HD:(h + 1) * HD], ACT.Copy, scale=bke[:, t, h:h + 1])
                    last.then_inc(kbg_ready, 1)
                elif k == 4:
                    act.wait_ge(u_done, 1)
                    act.activation(U[:].rearrange("p t h d -> p (t h d)"), flat_high, ACT.Copy).then_inc(u_ready, 1)
                elif k == 5:
                    act.wait_ge(wt_done, 1)
                    act.activation(WT[:].rearrange("p h t -> p (h t)"), flat_high, ACT.Copy).then_inc(wt_ready, 1)
                elif k == 6:
                    act.wait_ge(kbg_ready, 1)
                    act.wait_ge(exps_ready, 1)
                    for t in range(TT):
                        for h in range(HEADS):
                            v = KTOK[:, t, h * HD:(h + 1) * HD]
                            last = act.activation(v, v, ACT.Copy, scale=kd[:, t, h:h + 1])
                    last.then_inc(kdec_ready, 1)
            for k in range(PS):
                split(S_KV + PS + k)
                if k == 0:
                    left(S_KV + PS, P_KV, 0, K_0[:, 0, :])
                if k % 2 == 0:
                    n = k // 2
                    t, rows = n // 2, slice(CHUNK * (n % 2), CHUNK * (n % 2) + CHUNK)
                    act.wait_ge(ws_done, n + 1)
                    for h in range(HEADS):
                        last = act.activation(O[rows, t, h, :], ps[rows, 6 + h // 4, (h % 4) * P:(h % 4 + 1) * P], ACT.Copy, scale=eg[rows, t, h:h + 1])
                    last.then_inc(qs_ready, 1)
            for k in range(PS):
                split(S_KV + 2 * PS + k)
                if k == 1:
                    for t in range(TT):
                        left(S_KV + 2 * PS, P_KV + 1, t, K_1[:, t, :])
                    act.wait_ge(o_ready, T // CHUNK)
                    for t in range(TT):
                        for h in range(HEADS):
                            u = t * HEADS + h
                            last = act.activation(OSQ[:, t, h, :], O[:, t, h, :], ACT.Square, accum_out=osum[:, u:u + 1])
                    last.then_inc(osq_ready, 1)
                elif k == 5:
                    act.wait_ge(oz_ready, 1)
                    act.wait_ge(orst_ready, 1)
                    for t in range(TT):
                        for h in range(HEADS):
                            u = t * HEADS + h
                            last = act.activation(O[:, t, h, :], O[:, t, h, :], ACT.Copy, scale=orst[:, u:u + 1])
                    last.then_inc(o_final, 1)
            for k in range(PS):
                split(S_KV + 3 * PS + k)
                if k == 1:
                    for t in range(TT):
                        left(S_KV + 3 * PS, P_KV + 2, t, V_0[:, t, :])
                elif k == 6:
                    split_turned(H_OUT2, lambda k: G_DN, 0, 1)
            for k in range(PS):
                split(S_OUT2 + k)
                if k == 0:
                    left(S_OUT2, P_KV + 3, 0, V_1[:, 0, :])
                elif k == 3:
                    act.wait_ge(c_centred, 1)
                    act.activation(CSQ[:], COUT31[:], ACT.Square).then_inc(c_squared, 1)
                elif k == 4:
                    act.wait_ge(c_final, 1)
                    for c in range(HEADS):
                        act.activation(CS[:, c, :], COUT31[:, c, :], ACT.Silu, scale=dw_vec(1, c), bias=dw_vec(2, c)).then_inc(cs_ready, 1)
                        act.wait_ge(cs_ready, c + 1)
                        act.activation(HHI[:, HEADS + c, :], CS[:, c, :], ACT.Copy).then_inc(ht_hi, 1)
            for k in range(PS):
                split(S_OUT2 + PS + k)
                if k in (3, 5):
                    n = (k - 3) // 2
                    act.wait_ge(kx_turned, n + 1)
                    act.activation(KXT[:, 8 * n:8 * n + 8, :].rearrange("p k t -> p (k t)"), flat_high, ACT.Copy).then_inc(kx_ready, 1)
                elif k == 7:
                    split_turned(H_XQ, lambda k: G_XQ + k, 0, 1)
            def xprobs_of(h, b0):
                s = h % 2
                act.wait_ge(xmax, h + 1)
                if h >= 2:
                    act.wait_ge(xturned, h - 1)
                for q in range(TT):
                    last = act.activation(PX[:, s, q, :], ps[:, b0 + s, q * T:(q + 1) * T], ACT.Exp, bias=nmax[:, s, q:q + 1],
                                          scale=float(XHD) ** -0.5, accum_out=den[:, h, q:q + 1])
                last.then_inc(xprobs, 1)

            def xturned_probs(h, b0):
                s = h % 2
                act.wait_ge(xturned, h + 1)
                if h >= 2:
                    act.wait_ge(xatt, h - 1)
                act.activation(PXT[:, s].rearrange("p k t -> p (k t)"), ps[:, b0 + 2 + s, :], ACT.Copy).then_inc(xpt, 1)

            for n in range(2):
                for k in range(PS):
                    split(S_Q + n * PS + k)
                    if (n, k) == (0, 1):
                        act.wait_ge(out1, P_OUT2 + 2)
                        squares_of(X, N_XQ, QX)
                    elif (n, k) == (0, 2):
                        split_turned(H_XQ, lambda k: G_XQ + k, 1, 0)
                    elif (n, k) == (1, 1):
                        left(S_Q + PS, P_Q, 0, QX[:, 0, 0:COLS], norm=N_XQ)
                    elif (n, k) == (1, 2):
                        act.wait_ge(kx_turned, 3)
                        act.activation(QXT[:, 0:8, :].rearrange("p k t -> p (k t)"), flat_high, ACT.Copy).then_inc(kx_ready, 1)
                    elif (n, k) == (1, 4):
                        xprobs_of(0, 4)
                        xprobs_of(1, 4)
                    elif (n, k) == (1, 5):
                        xturned_probs(0, 4)
                        xturned_probs(1, 4)
            split(S_O)
            left(S_Q + 2 * PS, P_Q + 1, 0, QX[:, 0, COLS:2 * COLS], norm=N_XQ)
            split_turned(H_XO, None, 0, 1)
            split(S_O + 1)
            act.wait_ge(kx_turned, 4)
            act.activation(QXT[:, 8:16, :].rearrange("p k t -> p (k t)"), flat_low, ACT.Copy).then_inc(kx_ready, 1)
            for n in range(2):
                for k in range(PS):
                    if n > 0 or k >= NSPLIT:
                        split(S_O + n * PS + k)
                    if (n, k) == (0, 1):
                        xprobs_of(2, 0)
                        xprobs_of(3, 0)
                    elif (n, k) == (0, 2):
                        xturned_probs(2, 0)
                        xturned_probs(3, 0)
                    elif (n, k) == (0, 4):
                        split_turned(H_XO, None, 1, 0)
                    elif (n, k) == (1, 7):
                        split_turned(H_MLP2, lambda k: G_MLP2 + k, 0, 1)
            ahead(S_MLP2)
            act.wait_ge(out1, P_O + 2)
            squares_of(X, N_MLP2)
            split_turned(H_MLP2, lambda k: G_MLP2 + k, 1, 1)
            mlp(1, S_MLP2, P_MLP2, N_MLP2)
            for t, o in enumerate((out0, out1)):
                act.wait_ge(o, P_MLP2 + 2 * HALF_PASSES)
                act.activation(ROWS[:, t, :], X[:, t, :], ACT.Square, accum_out=ss[:, TT * N_F2 + t:TT * N_F2 + t + 1]).then_inc(sq_done, 1)

        @block.vector
        def _(dve):
            own = Own(dve, dve_own)

            def split(s, off=0):
                dve.wait_ge(hi_ready, s + off + 1)
                if s >= NSPLIT:
                    dve.wait_ge(w_used, s + off - NSPLIT + 1)
                dve.tensor_tensor(WLO[:, s % NSPLIT], RAW[:, s % NRAW], WHI[:, s % NSPLIT].bitcast(F32), ALU.subtract).then_inc(lo_ready, 1)

            def split_turned(h, g, half, group):
                for k in range(KT // 2 * half, KT // 2 * (half + 1)):
                    dve.wait_ge(ht_hi, KT * h + k // 2 * 2 + 2)
                    v = ps[:, 4 * group + (k % 8) // 2, (k % 2) * T:(k % 2 + 1) * T]
                    if g is None:
                        dve.tensor_tensor(HLO[:, k, :], v, HHI[:, k, :].bitcast(F32), ALU.subtract).then_inc(ht_lo, 1)
                    else:
                        dve.scalar_tensor_tensor(HLO[:, k, :], v, gain(g(k)), HHI[:, k, :].bitcast(F32), ALU.mult, ALU.subtract).then_inc(ht_lo, 1)

            def left(s_end, p, dst, norm=None):
                dve.wait_ge(w_used, s_end)
                src = ps[:, 4 * GROUPS[p] + 2:4 * GROUPS[p] + 4, :].rearrange("p b n -> p (b n)")
                if norm is None:
                    dve.tensor_copy(dst, src).then_inc(out1, 1)
                else:
                    dve.wait_ge(rstd_ready, norm + 1)
                    dve.tensor_scalar(dst, src, rstd_of(norm, 1), None, ALU.mult).then_inc(out1, 1)

            def add_residual(s_end, group, c0, off=0):
                dve.wait_ge(w_used, s_end + off)
                for t, o in enumerate((out0, out1)):
                    g = 4 * group + 2 * t
                    v = X[:, t, c0:c0 + COLS]
                    dve.tensor_tensor(v, ps[:, g:g + 2, :].rearrange("p b n -> p (b n)"), v, ALU.add).then_inc(o, 1)

            def ahead(s0):
                for k in range(NSPLIT):
                    split(s0 + k)

            def ahead_and_residual(s_next, p):
                split(s_next)
                add_residual(s_next, GROUPS[p], COLS)
                split(s_next + 1)

            def mlp(m, s0, p0):
                with dve.Fori(0, 2) as half:
                    off, roff, hoff = half * HALF_STEPS, half * 16, half * 8

                    def square(p):
                        g = 4 * (p % 2)
                        for t, o in enumerate((out0, out1)):
                            dve.wait_ge(relu_done, 16 * m + 2 * p + t + 1 + hoff)
                            dve.scalar_tensor_tensor(R[:, t, :], ps[:, g + 2 * t:g + 2 * t + 2, :].rearrange("p b n -> p (b n)"), 0.0, R[:, t, :],
                                                     ALU.max, ALU.mult).then_inc(o, 1)

                    def hidden_lo(p):
                        g = 4 * (p % 2)
                        for b in range(4):
                            dve.wait_ge(at_hi, 32 * m + 4 * p + b + 1 + roff)
                            k = 8 * p + 2 * b
                            dve.tensor_tensor(ALO[:, k:k + 2, :].rearrange("p k t -> p (k t)"), ps[:, g + b, :],
                                              AHI[:, k:k + 2, :].bitcast(F32).rearrange("p k t -> p (k t)"), ALU.subtract).then_inc(at_lo, 1)

                    for k in range(NSPLIT, HALF_STEPS + NSPLIT):
                        if k == HALF_STEPS + 1:
                            add_residual(s0 + HALF_STEPS, 1, COLS, off)
                        split(s0 + k, off)
                        p = k // PS - 1
                        if 0 <= p < 4 and k % PS == 1:
                            square(p)
                        elif 0 <= p < 4 and k % PS == 3:
                            hidden_lo(p)
                        if k == HALF_STEPS // 2 + HK // STEP + 1:
                            add_residual(s0 + HALF_STEPS // 2 + HK // STEP, 0, 0, off)

            dve.wait_ge(vec_turned, 1)
            own.mark(dve.tensor_copy(VEC[:].rearrange("p n c -> p (n c)"), ps[:, 0, :]))
            own.wait()
            dve.tensor_tensor(VEC[:, 0, G_IN2:G_IN2 + KT], VEC[:, 0, G_IN2:G_IN2 + KT], VEC[:, 0, G_F1:G_F1 + KT], ALU.mult).then_inc(vec_ready, 1)
            dve.wait_ge(vec_ready, 1)
            def biased(h):
                s = h % 2
                slope = 2.0 ** (-8.0 * (h + 1) / HEADS)
                own.wait()
                own.mark(dve.scalar_tensor_tensor(BIAS[:], ALIBI[:, 0, :], -slope, ALIBI[:, 1, :], ALU.mult, ALU.add))
                own.wait()
                dve.wait_ge(scored, h + 1)
                if h >= 2:
                    dve.wait_ge(probs_turned, h - 1)
                own.mark(dve.scalar_tensor_tensor(S1[:, s, :], ps[:, s, 0:NS], float(HD) ** -0.5, BIAS[:], ALU.mult, ALU.add))
                own.wait()
                own.mark(dve.tensor_reduce(nmax[:, s, 0:1], S1[:, s, 0:P], AX_X, ALU.max))
                own.mark(dve.tensor_reduce(nmax[:, s, 1:2], S1[:, s, P:NS], AX_X, ALU.max))
                own.wait()
                dve.tensor_scalar(nmax[:, s, :], nmax[:, s, :], -1.0, None, ALU.mult).then_inc(max_ready, 1)

            def weighted(h):
                s = h % 2
                dve.wait_ge(attended, h + 1)
                own.mark(dve.reciprocal(rden[:, s, :], den[:, h, :]))
                own.wait()
                for t in range(TT):
                    last = dve.tensor_scalar(Q_ROWS[:, t, h * HD:(h + 1) * HD], ps[:, 2 + s, t * P:(t + 1) * P], rden[:, s, t:t + 1], None, ALU.mult)
                last.then_inc(y_attn, 1)

            def normalised(n, rows):
                dve.wait_ge(rstd_ready, n + 1)
                for t in range(TT):
                    last = dve.tensor_scalar(rows[:, t, :], rows[:, t, :], rstd_of(n, t), None, ALU.mult)
                last.then_inc(y_ready, 1)

            for n in range(4):
                for k in range(PS):
                    if (n, k) == (0, 0):
                        split_turned(H_IN, lambda k: G_IN + k, 0, 1)
                    split(S_IN + n * PS + k)
                    if (n, k) == (0, 2):
                        split_turned(H_IN, lambda k: G_IN + k, 1, 1)
                    elif n > 0 and k == 1:
                        left(S_IN + n * PS, P_IN + n - 1, PROJ[:, IN_COLS[n - 1], 1, :], N_IN)
                    if n == 3 and 1 <= k < 1 + HEADS // 2:
                        dve.wait_ge(alibi_landed, 16)
                        for h in range(2 * k - 2, 2 * k):
                            biased(h)
                    if n == 3 and 2 <= k < 2 + HEADS // 2:
                        for h in range(2 * k - 4, 2 * k - 2):
                            weighted(h)
                    if (n, k) == (3, 6):
                        normalised(N_ATT, Q_ROWS)
                    elif (n, k) == (3, 7):
                        split_turned(H_OUT, lambda k: G_OUT + k, 0, 0)
            ahead(S_OUT)
            left(S_IN + 4 * PS, P_IN + 3, U_ROWS[:, 1, :], N_IN)
            for n in range(2):
                for k in range(PS):
                    if n > 0 or k >= NSPLIT:
                        split(S_OUT + n * PS + k)
                    if (n, k) == (0, 3):
                        dve.wait_ge(pool_out, 1)
                        dve.wait_ge(pools_landed, 16)
                        for t in range(TT):
                            last = dve.tensor_tensor(U_ROWS[:, t, :], ps[:, 4 + 2 * t:6 + 2 * t, :].rearrange("p b n -> p (b n)"), PSB[:], ALU.mult)
                        last.then_inc(y_pool, 1)
                        normalised(N_POOL, U_ROWS)
                    elif (n, k) == (0, 4):
                        split_turned(H_OUT, lambda k: G_OUT + k, 1, 1)
                    elif (n, k) == (1, 1):
                        add_residual(S_OUT + PS, GROUPS[P_OUT], 0)
                    elif (n, k) == (1, 7):
                        split_turned(H_MLP, lambda k: G_MLP + k, 0, 0)
            ahead_and_residual(S_MLP, P_OUT + 1)
            split_turned(H_MLP, lambda k: G_MLP + k, 1, 1)
            mlp(0, S_MLP, P_MLP)

            def final(n, dst):
                dve.wait_ge(final_landed, 16 if n == N_F1 else 32)
                for t in range(TT):
                    dve.wait_ge(rstd_ready, n + 1 if n == N_F1 else n + 1 + t)
                    dve.scalar_tensor_tensor(dst[:, t, :], X[:, t, :], rstd_of(n, t), GB[:], ALU.mult, ALU.mult).then_inc(x_final, 1)

            dve.wait_ge(ba_split, 1)
            dve.tensor_tensor(BALO[:], BARAW[:], BAHI[:].bitcast(F32), ALU.subtract).then_inc(ba_split, 1)
            low = ps[:, 0:4, :].rearrange("p b n -> p (b n)")
            high = ps[:, 4:8, :].rearrange("p b n -> p (b n)")

            def conv4_tap(n, j):
                if j == 0:
                    dve.wait_ge(cin_ready, n + 1)
                    if n >= 1:
                        dve.wait_ge(conv_back, n)
                for c in range(HEADS):
                    src, weight = CIN[:, c, j:j + T], tap(j, n * HEADS + c)
                    if j == 0:
                        last = dve.tensor_scalar(COUT[:, c, :], src, weight, None, ALU.mult)
                    else:
                        if c == 0:
                            own.wait()
                        last = dve.scalar_tensor_tensor(COUT[:, c, :], src, weight, COUT[:, c, :], ALU.mult, ALU.add)
                    if j < CONV - 1:
                        own.mark(last)
                if j == CONV - 1:
                    last.then_inc(conv_done, 1)

            def conv31_taps(first, end):
                for j in range(first, end):
                    for c in range(HEADS):
                        src = CIN31[:, c, j:j + T]
                        if j == 0:
                            last = dve.tensor_scalar(COUT31[:, c, :], src, dw_tap(j, c), dw_vec(0, c), ALU.mult, ALU.add)
                        else:
                            if c == 0:
                                dve.wait_ge(c31_own, HEADS * j)
                            last = dve.scalar_tensor_tensor(COUT31[:, c, :], src, dw_tap(j, c), COUT31[:, c, :], ALU.mult, ALU.add)
                        last.then_inc(c31_own if j < DW - 1 or c < HEADS - 1 else c31_done, 1)

            def conv31_step(n):
                conv31_taps(sum(C31_TAPS[:n]), sum(C31_TAPS[:n + 1]))

            def conv_store(n, dst, group):
                dve.wait_ge(conv_back, n + 1)
                dve.tensor_copy(dst[:, 1, :], ps[:, 4 * group + 2:4 * group + 4, :].rearrange("p b n -> p (b n)")).then_inc(sec1, 1)

            def heads(v):
                return v.rearrange("p t (h d) -> p t h d", d=HD)

            def per_head(v):
                return v.unsqueeze(3).broadcast_to([P, TT, HEADS, HD])

            def l2_of(n):
                return per_head(l2r[:, n, :].rearrange("p (t h) -> p t h", t=TT))

            def sum_squares(n):
                dve.wait_ge(l2_sq, n + 1)
                dve.tensor_reduce(l2[:, n, :], SQT[:].rearrange("p t h d -> p (t h) d"), AX_X, ALU.add).then_inc(l2_sum, 1)

            def softplus_gate():
                dve.wait_ge(spe_ready, 1)
                own.mark(dve.tensor_scalar(sp_z[:], sp_e[:], 2.0, None, ALU.add))
                own.wait()
                own.mark(dve.reciprocal(sp_z[:], sp_z[:]))
                own.wait()
                own.mark(dve.tensor_tensor(sp_z[:], sp_z[:], sp_e[:], ALU.mult))
                own.wait()
                own.mark(dve.tensor_tensor(sp_q[:], sp_z[:], sp_z[:], ALU.mult))
                own.wait()
                own.mark(dve.tensor_scalar(sp_p[:], sp_q[:], 1.0 / (2 * LOG_TERMS - 1), None, ALU.mult))
                for n in range(LOG_TERMS - 2, 0, -1):
                    own.wait()
                    own.mark(dve.scalar_tensor_tensor(sp_p[:], sp_p[:], 1.0 / (2 * n + 1), sp_q[:], ALU.add, ALU.mult))
                own.wait()
                own.mark(dve.scalar_tensor_tensor(sp_p[:], sp_p[:], 1.0, sp_z[:], ALU.add, ALU.mult))
                own.mark(dve.tensor_scalar(adt[:], adt[:], 0.0, None, ALU.max))
                own.wait()
                own.mark(dve.scalar_tensor_tensor(sp_p[:], sp_p[:], 2.0, adt[:], ALU.mult, ALU.add))
                own.wait()
                dve.wait_ge(ea_ready, 1)
                dve.scalar_tensor_tensor(gate[:], sp_p[:], -1.0, alog[:].unsqueeze(1).broadcast_to([P, TT, HEADS]), ALU.mult, ALU.mult).then_inc(gate_ready, 1)

            flat_x = XI[:].rearrange("p u c -> p (u c)")
            flat_xt = XT[:].rearrange("p u c -> p (u c)")
            eye = IDENT.unsqueeze(1).broadcast_to([P, U16, P])
            high_units = ps[:, 4:8, :].rearrange("p b (u c) -> p (b u) c", c=P)

            def mask(lv):
                return SQ[:, 5 + lv, :].unsqueeze(1).broadcast_to([P, U16, P])

            for half in range(2):
                split_turned(H_IN2, lambda k: G_IN2 + k, half, half)
            for k in range(NSPLIT, PS):
                split(S_IN2 + k)
                if k == 3:
                    dve.wait_ge(turned, KT // 2 * (H_IN2 + 1))
                    final(N_F1, X)
                elif k == 6:
                    dve.wait_ge(ba_done, 1)
                    dve.tensor_copy(BAT[0:NBA, :], ps[0:NBA, 4, 0:T]).then_inc(ba_columns, 1)
                elif k == 7:
                    dve.wait_ge(ba_turned, 1)
                    dve.wait_ge(rstd_ready, N_IN2 + 1)
                    for t in range(TT):
                        last = dve.tensor_scalar(ba[:, t, :], ps[:, 5, t * NBA:(t + 1) * NBA], rstd_of(N_IN2, t), None, ALU.mult)
                    last.then_inc(ba_out, 1)
            for k in range(PS):
                split(S_IN2 + PS + k)
                if k == 0:
                    left(S_IN2 + PS, P_IN2, QTOK[:, 1, :], N_IN2)
                    dve.wait_ge(gates_landed, 32)
                    dve.wait_ge(ba_out, 1)
                    own.mark(dve.tensor_tensor(adt[:], ba[:, :, HEADS:NBA], dtb[:].unsqueeze(1).broadcast_to([P, TT, HEADS]), ALU.add))
                    own.wait()
                    dve.scalar_tensor_tensor(sp_e[:], adt[:], -1.0, adt[:], ALU.mult, ALU.max).then_inc(adt_ready, 1)
                elif k == 2:
                    softplus_gate()
                elif 3 <= k < 3 + CONV:
                    if k == 6:
                        dve.wait_ge(gcs_ready, 1)
                        dve.tensor_tensor(kd[:].rearrange("p t h -> p (t h)"), ps[:, 0, 16:16 + U16], gcs[:].rearrange("p t h -> p (t h)"), ALU.subtract).then_inc(kd_sub, 1)
                    conv4_tap(0, k - 3)
                elif k == 7:
                    dve.wait_ge(exps_ready, 1)
                    dve.wait_ge(beta_ready, 1)
                    dve.tensor_tensor(bke[:], beta[:], eg[:], ALU.mult).then_inc(bke_ready, 1)
            for k in range(PS):
                split(S_IN2 + 2 * PS + k)
                if k == 0:
                    left(S_IN2 + 2 * PS, P_IN2 + 1, KTOK[:, 1, :], N_IN2)
                elif k == 1:
                    conv_store(0, QTOK, 1)
                elif 3 <= k < 3 + CONV:
                    conv4_tap(1, k - 3)
                elif k == 7:
                    sum_squares(0)
            for k in range(PS):
                split(S_IN2 + 3 * PS + k)
                if k == 0:
                    left(S_IN2 + 3 * PS, P_IN2 + 2, VTOK[:, 1, :], N_IN2)
                elif k == 1:
                    conv_store(1, KTOK, 0)
                elif k == 2:
                    dve.wait_ge(rstd_ready, N_MEM + 1)
                    for t in range(TT):
                        dve.tensor_scalar(MEM[:, t, :], MEM[:, t, :], rstd_of(N_MEM, t), None, ALU.mult).then_inc(mem_ready, 1)
                elif 3 <= k < 3 + CONV:
                    conv4_tap(2, k - 3)
                elif k == 7:
                    sum_squares(1)
            for k in range(PS):
                split(S_IN2 + 4 * PS + k)
                if k == 0:
                    dve.wait_ge(l2_ready, 1)
                    dve.tensor_tensor(heads(QTOK), heads(QTOK), l2_of(0), ALU.mult).then_inc(qn_ready, 1)
                elif k == 1:
                    conv_store(2, VTOK, 1)
                    dve.tensor_tensor(heads(KTOK), heads(KTOK), l2_of(1), ALU.mult).then_inc(kn_ready, 1)
                elif k == 2:
                    dve.wait_ge(kn_ready, 1)
                    dve.tensor_tensor(KB_[:], heads(KTOK), per_head(beta[:]), ALU.mult).then_inc(kb_ready, 1)
                elif k == 3:
                    for u in range(U16):
                        last = dve.tensor_scalar(DIAG[:, u, :], IDENT, gcs[:, u // HEADS, u % HEADS:u % HEADS + 1], None, ALU.mult)
                    last.then_inc(diag_ready, 1)
                elif k == 4:
                    dve.wait_ge(sec0, 3)
                    dve.wait_ge(sec1, 3)
                    dve.tensor_tensor(heads(VTOK), heads(VTOK), per_head(beta[:]), ALU.mult).then_inc(v_ready, 1)
                elif k == 5:
                    dve.wait_ge(rows_ready, 1)
                    dve.wait_ge(sq_landed, 16)
                    own.mark(dve.tensor_tensor(DEC[:], high_units, gcs[:].rearrange("p t h -> p (t h)").unsqueeze(2).broadcast_to([P, U16, P]), ALU.subtract))
                    own.wait()
                    dve.tensor_tensor(DEC[:], DEC[:], NEGMASK.unsqueeze(1).broadcast_to([P, U16, P]), ALU.add).then_inc(decsub_ready, 1)
                elif k in (6, 7):
                    dve.wait_ge(gram_done, k - 5)
                    dve.wait_ge(decay_ready, 1)
                    dst = LT if k == 6 else ATT
                    dve.tensor_tensor(dst[:].rearrange("p u c -> p (u c)"), high, DEC[:].rearrange("p u c -> p (u c)"), ALU.mult).then_inc(gram_ready, 1)
            for k in range(PS):
                split(S_IN2 + 5 * PS + k)
                if k == 0:
                    left(S_IN2 + 5 * PS, P_IN2 + 4, GA[:, 1, :], N_IN2)
                    dve.wait_ge(gram_ready, 1)
                    dve.tensor_tensor(WL[:], LT[:], mask(0), ALU.mult).then_inc(level0_ready, 1)
                    dve.wait_ge(level0_ready, 1)
                    dve.tensor_tensor(XT[:], eye, WL[:], ALU.subtract).then_inc(xt_up, 1)
                    dve.wait_ge(level0_turned, 1)
                    dve.tensor_tensor(XI[:], eye, high_units, ALU.subtract).then_inc(x_up, 1)
                    continue
                for j in range(STEP):
                    lv, part = level_part(k, j)
                    if part == 0:
                        dve.wait_ge(wl_done, lv)
                        dve.tensor_tensor(WL[:], high_units, mask(lv), ALU.mult).then_inc(wl_ready, 1)
                    elif part == 1:
                        dve.wait_ge(xw_done, lv)
                        dve.wait_ge(x_up, lv)
                        dve.tensor_tensor(flat_x, flat_x, high, ALU.subtract).then_inc(x_up, 1)
                    else:
                        dve.wait_ge(xt_done, lv)
                        dve.wait_ge(xt_up, lv)
                        dve.tensor_tensor(flat_xt, flat_xt, high, ALU.subtract).then_inc(xt_up, 1)
            for k in range(PS):
                split(S_KV + k)
                if k == 0:
                    split_turned(H_MEM, lambda k: G_MEM + k, 0, 1)
                    dve.wait_ge(out0, P_IN2 + 6)
                    dve.wait_ge(out1, P_IN2 + 6)
                    dve.tensor_tensor(GA, GA, GBT, ALU.mult).then_inc(glu_ready, 1)
                elif k == 2:
                    split_turned(H_MEM, lambda k: G_MEM + k, 1, 1)
                elif k == 3:
                    dve.wait_ge(c31_in, 1)
                conv31_step(k)

            def two(b):
                return ps[:, b:b + 2, :].rearrange("p b (h d) -> p (b h) d", d=HD)

            for k in range(PS):
                split(S_KV + PS + k)
                if k == 0:
                    left(S_KV + PS, P_KV, K_0[:, 1, :])
                n = k // 2
                t, r = n // 2, CHUNK * (n % 2)
                rows = slice(r, r + CHUNK)
                if k % 2 == 0:
                    dve.wait_ge(u_ready, 1)
                    dve.wait_ge(ws_done, n + 1)
                    dve.tensor_tensor(U[rows, t], U[rows, t], two(4)[rows], ALU.subtract).then_inc(vn_ready, 1)
                else:
                    dve.wait_ge(vn_used, n + 1)
                    if n + 1 < T // CHUNK:
                        dve.wait_ge(sd_ready, n + 1)
                        dve.tensor_tensor(ST[:], SD[:], two(4), ALU.add).then_inc(state_ready, 1)
                    dve.wait_ge(qs_ready, n + 1)
                    dve.tensor_tensor(O[rows, t], O[rows, t], two(6)[rows], ALU.add).then_inc(o_ready, 1)
                conv31_step(PS + k)
            for k in range(PS):
                split(S_KV + 2 * PS + k)
                if k == 3:
                    dve.wait_ge(osq_ready, 1)
                    flat_o = O[:].rearrange("p t h d -> p (t h d)")
                    dve.tensor_tensor(flat_o, flat_o, ZTOK.rearrange("p t d -> p (t d)"), ALU.mult).then_inc(oz_ready, 1)
                conv31_step(2 * PS + k)
            for k in range(PS):
                split(S_KV + 3 * PS + k)
                if k == 6:
                    split_turned(H_OUT2, lambda k: G_DN, 0, 1)
                conv31_step(3 * PS + k)
            for k in range(PS):
                split(S_OUT2 + k)
                if k == 0:
                    left(S_OUT2, P_KV + 3, V_1[:, 1, :])
                    conv31_step(4 * PS)
                elif k == 2:
                    dve.wait_ge(c_summed, 1)
                    dve.scalar_tensor_tensor(COUT31[:], ps[:, 0, 0:T].unsqueeze(1).broadcast_to([P, HEADS, T]), -1.0 / COLS, COUT31[:],
                                             ALU.mult, ALU.add).then_inc(c_centred, 1)
                elif k == 3:
                    dve.wait_ge(c_sq_summed, 1)
                    dve.tensor_scalar(LN_VAR[:], ps[:, 1:3, 0], 1.0 / COLS, EPS, ALU.mult, ALU.add).then_inc(c_var, 1)
                    dve.wait_ge(c_rstd, 1)
                    for t in range(TT):
                        last = dve.tensor_scalar(LN_DIAG[:, t, :], IDENT, LN_RSTD[:, t:t + 1], None, ALU.mult)
                    last.then_inc(c_diag, 1)
                    dve.wait_ge(c_spread, 1)
                    dve.tensor_tensor(COUT31[:], COUT31[:], ps[:, 3, 0:T].unsqueeze(1).broadcast_to([P, HEADS, T]), ALU.mult).then_inc(c_final, 1)
                elif k == 4:
                    for c in range(HEADS):
                        dve.wait_ge(ht_hi, KT * H_OUT2 + HEADS + c + 1)
                        dve.tensor_tensor(HLO[:, HEADS + c, :], CS[:, c, :], HHI[:, HEADS + c, :].bitcast(F32), ALU.subtract).then_inc(ht_lo, 1)
            for k in range(PS):
                split(S_OUT2 + PS + k)
                if k == 1:
                    dve.wait_ge(x_back, 16)
                    add_residual(S_OUT2 + PS, GROUPS[P_OUT2], 0)
                elif k == 7:
                    split_turned(H_XQ, lambda k: G_XQ + k, 0, 1)
            ahead_and_residual(S_Q, P_OUT2 + 1)

            def xmaxima(h, b0):
                s = h % 2
                dve.wait_ge(xscored, h + 1)
                if h >= 2:
                    dve.wait_ge(xprobs, h - 1)
                own.mark(dve.tensor_reduce(nmax[:, s, :], ps[:, b0 + s, :].rearrange("p (q k) -> p q k", q=TT), AX_X, ALU.max))
                own.wait()
                dve.tensor_scalar(nmax[:, s, :], nmax[:, s, :], -float(XHD) ** -0.5, None, ALU.mult).then_inc(xmax, 1)

            def xweighted(h, b0):
                s = h % 2
                dve.wait_ge(xatt, h + 1)
                own.mark(dve.reciprocal(rden[:, s, :], den[:, h, :]))
                own.wait()
                for q in range(TT):
                    last = dve.tensor_scalar(QX[:, q, h * XHD:(h + 1) * XHD], ps[:, b0 + 2 * s + q, :], rden[:, s, q:q + 1], None, ALU.mult)
                last.then_inc(xout, 1)

            for n in range(2):
                for k in range(PS):
                    if n > 0 or k >= NSPLIT:
                        split(S_Q + n * PS + k)
                    if (n, k) == (0, 2):
                        split_turned(H_XQ, lambda k: G_XQ + k, 1, 0)
                    elif (n, k) == (1, 1):
                        left(S_Q + PS, P_Q, QX[:, 1, 0:COLS], N_XQ)
                    elif (n, k) == (1, 4):
                        xmaxima(0, 4)
                        xmaxima(1, 4)
                    elif n == 1 and k >= 6:
                        xweighted(k - 6, 4)
            split(S_O)
            left(S_Q + 2 * PS, P_Q + 1, QX[:, 1, COLS:2 * COLS], N_XQ)
            split_turned(H_XO, None, 0, 1)
            split(S_O + 1)
            for n in range(2):
                for k in range(PS):
                    if n > 0 or k >= NSPLIT:
                        split(S_O + n * PS + k)
                    if (n, k) == (0, 1):
                        xmaxima(2, 0)
                        xmaxima(3, 0)
                    elif (n, k) == (0, 3):
                        xweighted(2, 0)
                        xweighted(3, 0)
                    elif (n, k) == (0, 4):
                        split_turned(H_XO, None, 1, 0)
                    elif (n, k) == (1, 1):
                        add_residual(S_O + PS, GROUPS[P_O], 0)
                    elif (n, k) == (1, 7):
                        split_turned(H_MLP2, lambda k: G_MLP2 + k, 0, 1)
            ahead_and_residual(S_MLP2, P_O + 1)
            split_turned(H_MLP2, lambda k: G_MLP2 + k, 1, 1)
            mlp(1, S_MLP2, P_MLP2)
            final(N_F2, ROWS)


def kernel(**inputs):
    import numpy as _np
    import concourse.bacc as _bacc
    from concourse import mybir as _mybir
    from concourse.bass_utils import run_bass_kernel_spmd as _run

    a = {k: _np.asarray(v) for k, v in inputs.items()}

    def rows(*names):
        got = _np.concatenate([a[n].reshape(-1, 128) for n in names], 0)
        return _np.concatenate([got, _np.zeros((128 - len(got), 128), got.dtype)], 0)

    taps = a["cf_dw_w_2"].reshape(-1, 128)
    pad = _np.zeros((4, 128), taps.dtype)
    vectors = _np.stack([
        rows("norm_mix_g", "attn_out_norm_g", "pool_out_norm_g", "norm_mlp_g", "norm_mix_g_2", "norm_xa_g_2", "norm_mem_g_2",
             "norm_mlp_g_2", "norm_final_g"),
        rows("dn_conv_w_2", "cf_dw_b_2", "cf_ln_g_2", "cf_ln_b_2", "dn_norm_g_2"),
        _np.concatenate([taps[:124], pad], 0), _np.concatenate([taps[124:], pad], 0)])
    squares, alibi, pool_avg = shape_constants()
    feeds = {
        "x": a["x"][0], "mem": a["mem_2"][0], "vectors": vectors, "squares": squares, "alibi": alibi, "pool_avg": pool_avg,
        "w_in": a["w_in"][0], "pool_w": a["pool_w"][0], "pool_scale": a["pool_scale"][0], "w_out": a["w_out"][0],
        "w_up": a["w_up"][0], "w_down": a["w_down"][0], "final_g": a["norm_final_g"], "w_in2": a["w_in_2"][0],
        "a_log": a["dn_a_log_2"][0], "dt_bias": a["dn_dt_bias_2"][0], "w_out2": a["w_out_2"][0],
        "wq": a["xa_wq_2"][0], "wk": a["xa_wk_2"][0], "wv": a["xa_wv_2"][0], "wo": a["xa_wo_2"][0],
        "w1": a["mlp_w1_2"][0], "w2": a["mlp_w2_2"][0], "final_g2": a["norm_final_g_2"],
    }
    nc = _bacc.Bacc("TRN2", target_bir_lowering=False, num_devices=1)
    arrays, args = {}, {}
    for name, v in feeds.items():
        v = _np.ascontiguousarray(v)
        arrays[f"in_{name}"] = v
        args[name] = nc.dram_tensor(f"in_{name}", v.shape, _mybir.dt.from_np(v.dtype), kind="ExternalInput").ap()
    args["out"] = nc.dram_tensor("out_y", (T, D), F32, kind="ExternalOutput").ap()
    build(nc, **args)
    r = _run(nc, [arrays], core_ids=[0])
    return r.results[0]["out_y"].reshape(1, T, D)
```
